# Optimizing a Trainium2 kernel written in Bass

```python
import jax, jax.numpy as jnp
from jax import lax
import numpy as np
import math

D_MODEL = 1024
BATCH = 1
SEQ = 256
DEPTH = 2

CHUNK = 64
SB_BLOCK = 128
EPS = 1e-6
GLA_HEADS = 4
GLA_HEAD_K = 64
GLA_HEAD_V = 128
GLA_DK = GLA_HEADS * GLA_HEAD_K
GLA_DV = GLA_HEADS * GLA_HEAD_V
GLA_GATE_RANK = 16
GLA_GATE_NORMALIZER = 16.0
SB_HEADS = 8
SB_HEAD_DIM = 64
SB_D = SB_HEADS * SB_HEAD_DIM
MIX_WIDTH = GLA_DV + SB_D
IN_WIDTH = 2 * GLA_DK + 2 * GLA_DV + GLA_GATE_RANK + 3 * SB_D
CONV_WIDTH = 31
D_FF = -(-8 * D_MODEL // (3 * 256)) * 256
N_EVEN = (DEPTH + 1) // 2
N_ODD = DEPTH // 2


def _rms_f32(xf, g):
    return xf * lax.rsqrt(jnp.mean(xf * xf, axis=-1, keepdims=True) + EPS) * g.astype(jnp.float32)

def rms_norm(x, g):
    return _rms_f32(x.astype(jnp.float32), g).astype(x.dtype)

def gla_mixer(q, k, v, r, gate_lr, w_gate2, b_gate, g_out):
    f32 = jnp.float32
    B, T, _ = q.shape
    nc = T // CHUNK
    log_a = jax.nn.log_sigmoid((gate_lr @ w_gate2 + b_gate).astype(f32)) / GLA_GATE_NORMALIZER

    def split(t, hd):
        return t.astype(f32).reshape(B, nc, CHUNK, -1, hd).transpose(0, 3, 1, 2, 4)

    qc = split(q, GLA_HEAD_K) * (GLA_HEAD_K ** -0.5)
    kc = split(k, GLA_HEAD_K)
    vc = split(v, GLA_HEAD_V)
    bc = jnp.cumsum(split(log_a, GLA_HEAD_K), axis=3)
    b_end = bc[:, :, :, -1:, :]
    k_end = kc * jnp.exp(b_end - bc)
    scores = jnp.einsum('bhnik,bhnjk->bhnij', qc, k_end)
    intra = jnp.einsum('bhnij,bhnjv->bhniv', scores, vc)
    chunk_update = jnp.einsum('bhnjk,bhnjv->bhnkv', k_end, vc)
    chunk_decay = jnp.exp(b_end[:, :, :, 0, :])

    def step(s, inp):
        a, u = inp
        return a[..., None] * s + u, s

    s0 = jnp.zeros((B, GLA_HEADS, GLA_HEAD_K, GLA_HEAD_V), f32)
    _, s_prev = lax.scan(step, s0, (jnp.moveaxis(chunk_decay, 2, 0), jnp.moveaxis(chunk_update, 2, 0)))
    s_prev = jnp.moveaxis(s_prev, 0, 2)
    inter = jnp.einsum('bhnik,bhnkv->bhniv', qc * jnp.exp(b_end), s_prev)
    o = _rms_f32(intra + inter, g_out)
    o = o.transpose(0, 2, 3, 1, 4).reshape(B, T, GLA_DV)
    return o * jax.nn.silu(r.astype(f32))

def stick_breaking_mixer(q, k, v, g_q, g_k):
    f32 = jnp.float32
    B, T, _ = q.shape

    def heads(t):
        return t.astype(f32).reshape(B, T, SB_HEADS, SB_HEAD_DIM).transpose(0, 2, 1, 3)

    qh = _rms_f32(heads(q), g_q) * (SB_HEAD_DIM ** -0.5)
    kh = _rms_f32(heads(k), g_k)
    vh = heads(v)
    outs = []
    for blk in range(T // SB_BLOCK):
        q0 = blk * SB_BLOCK
        kv_len = q0 + SB_BLOCK
        past = np.arange(kv_len)[None, :] < np.arange(q0, kv_len)[:, None]
        z = jnp.einsum('bhtd,bhsd->bhts', qh[:, :, q0:kv_len], kh[:, :, :kv_len])
        log_keep = jnp.where(past, jax.nn.log_sigmoid(-z), 0.0)
        between = lax.cumsum(log_keep, axis=3, reverse=True) - log_keep
        w = jnp.where(past, jnp.exp(jax.nn.log_sigmoid(z) + between), 0.0)
        outs.append(jnp.einsum('bhts,bhsd->bhtd', w, vh[:, :, :kv_len]))
    o = jnp.concatenate(outs, axis=2)
    return o.transpose(0, 2, 1, 3).reshape(B, T, SB_D)

def hybrid_mixer(h, w_in, w_gate2, b_gate, g_gla, g_q, g_k, w_out):
    proj = h @ w_in
    cuts = np.cumsum([GLA_DK, GLA_DK, GLA_DV, GLA_DV, GLA_GATE_RANK, SB_D, SB_D])
    gq, gk, gv, gr, glr, sq, sk, sv = jnp.split(proj, cuts, axis=-1)
    o_gla = gla_mixer(gq, gk, gv, gr, glr, w_gate2, b_gate, g_gla)
    o_sb = stick_breaking_mixer(sq, sk, sv, g_q, g_k)
    o = jnp.concatenate([o_gla, o_sb], axis=-1).astype(h.dtype)
    return o @ w_out

def conformer_conv(h, w_pw1, b_pw1, w_dw, b_dw, ln_g, ln_b, w_pw2, b_pw2):
    a = h @ w_pw1 + b_pw1
    u = a[..., :D_MODEL] * jax.nn.sigmoid(a[..., D_MODEL:])
    u = lax.conv_general_dilated(u, w_dw[:, None, :].astype(u.dtype), window_strides=(1,),
                                 padding=[(CONV_WIDTH - 1, 0)],
                                 dimension_numbers=('NWC', 'WIO', 'NWC'),
                                 feature_group_count=D_MODEL) + b_dw
    uf = u.astype(jnp.float32)
    mu = jnp.mean(uf, axis=-1, keepdims=True)
    var = jnp.mean(jnp.square(uf - mu), axis=-1, keepdims=True)
    u = ((uf - mu) * lax.rsqrt(var + EPS) * ln_g + ln_b).astype(h.dtype)
    return jax.nn.silu(u) @ w_pw2 + b_pw2

def swiglu(h, wg, wu, wd):
    return (jax.nn.silu(h @ wg) * (h @ wu)) @ wd

def first_inputs(seed: int = 0) -> dict:
    key = jax.random.key(seed)
    ks = iter(jax.random.split(key, 32))

    def nrm(shape, scale):
        return jax.random.normal(next(ks), shape, jnp.float32) * scale

    def gain(shape):
        return 1.0 + nrm(shape, 0.05)

    return {
        "x": nrm((BATCH, SEQ, D_MODEL), 1.0),
        "mix_norm": gain((DEPTH, D_MODEL)),
        "ffn_norm": gain((DEPTH, D_MODEL)),
        "hy_w_in": nrm((N_EVEN, D_MODEL, IN_WIDTH), D_MODEL ** -0.5),
        "hy_w_gate2": nrm((N_EVEN, GLA_GATE_RANK, GLA_DK), GLA_GATE_RANK ** -0.5),
        "hy_b_gate": nrm((N_EVEN, GLA_DK), 0.1),
        "hy_gla_norm": gain((N_EVEN, GLA_HEAD_V)),
        "hy_sb_q_norm": gain((N_EVEN, SB_HEAD_DIM)),
        "hy_sb_k_norm": gain((N_EVEN, SB_HEAD_DIM)),
        "hy_w_out": nrm((N_EVEN, MIX_WIDTH, D_MODEL), MIX_WIDTH ** -0.5),
        "cv_w_pw1": nrm((N_ODD, D_MODEL, 2 * D_MODEL), D_MODEL ** -0.5),
        "cv_b_pw1": nrm((N_ODD, 2 * D_MODEL), 0.02),
        "cv_w_dw": nrm((N_ODD, CONV_WIDTH, D_MODEL), CONV_WIDTH ** -0.5),
        "cv_b_dw": nrm((N_ODD, D_MODEL), 0.02),
        "cv_ln_g": gain((N_ODD, D_MODEL)),
        "cv_ln_b": nrm((N_ODD, D_MODEL), 0.02),
        "cv_w_pw2": nrm((N_ODD, D_MODEL, D_MODEL), D_MODEL ** -0.5),
        "cv_b_pw2": nrm((N_ODD, D_MODEL), 0.02),
        "ffn_w_gate": nrm((DEPTH, D_MODEL, D_FF), D_MODEL ** -0.5),
        "ffn_w_up": nrm((DEPTH, D_MODEL, D_FF), D_MODEL ** -0.5),
        "ffn_w_down": nrm((DEPTH, D_FF, D_MODEL), D_FF ** -0.5),
    }

def first_block(x, mix_norm, ffn_norm, hy_w_in, hy_w_gate2, hy_b_gate, hy_gla_norm,
              hy_sb_q_norm, hy_sb_k_norm, hy_w_out, cv_w_pw1, cv_b_pw1, cv_w_dw, cv_b_dw,
              cv_ln_g, cv_ln_b, cv_w_pw2, cv_b_pw2, ffn_w_gate, ffn_w_up, ffn_w_down):
    h = x
    for layer in range(DEPTH):
        hn = rms_norm(h, mix_norm[layer])
        if layer % 2 == 0:
            i = layer // 2
            mix = hybrid_mixer(hn, hy_w_in[i], hy_w_gate2[i], hy_b_gate[i], hy_gla_norm[i],
                               hy_sb_q_norm[i], hy_sb_k_norm[i], hy_w_out[i])
        else:
            i = layer // 2
            mix = conformer_conv(hn, cv_w_pw1[i], cv_b_pw1[i], cv_w_dw[i], cv_b_dw[i],
                                 cv_ln_g[i], cv_ln_b[i], cv_w_pw2[i], cv_b_pw2[i])
        h = h + mix.astype(h.dtype)
        h = h + swiglu(rms_norm(h, ffn_norm[layer]), ffn_w_gate[layer], ffn_w_up[layer],
                       ffn_w_down[layer]).astype(h.dtype)
    return h


DEPTH_2 = 1

GRID_W = 64
CTX_LEN = 256

MLA_HEADS = 4
MLA_Q_LORA = 256
MLA_KV_LORA = 128
MLA_NOPE = 128
MLA_ROPE = 64
MLA_V = 128
MLA_WIDTH = MLA_HEADS * MLA_V
ROPE_BASE = 10000.0
ATTN_BLOCK = 128

HG_HEADS = 4
HG_K = 128
HG_V = 64
HG_WIDTH = HG_HEADS * HG_V
HG_CHUNK = 64

FN_GROUPS = 4
FN_GROUP_DIM = 64
FN_WIDTH = FN_GROUPS * FN_GROUP_DIM

MIX_WIDTH_2 = MLA_WIDTH + HG_WIDTH + FN_WIDTH
FFN_HIDDEN = -(-8 * D_MODEL // (3 * 256)) * 256

O_CQ = 0
O_CKV = O_CQ + MLA_Q_LORA
O_KR = O_CKV + MLA_KV_LORA
O_HQ = O_KR + MLA_ROPE
O_HFF = O_HQ + HG_HEADS * HG_K
O_HFB = O_HFF + HG_HEADS * HG_K
O_HI = O_HFB + HG_HEADS * HG_K
O_HG = O_HI + HG_WIDTH
O_FN = O_HG + HG_WIDTH
IN_WIDTH_2 = O_FN + FN_WIDTH


def rms_norm_2(x, g):
    xf = x.astype(jnp.float32)
    y = xf * lax.rsqrt(jnp.mean(xf * xf, axis=-1, keepdims=True) + EPS)
    return (y * g.astype(jnp.float32)).astype(x.dtype)

def modulate(x, g, shift, scale):
    return rms_norm_2(x, g) * (1 + scale) + shift

def axial_rope(n_tokens, dtype):
    rows = n_tokens // GRID_W
    row_pos = jnp.repeat(jnp.arange(rows, dtype=jnp.float32), GRID_W)
    col_pos = jnp.tile(jnp.arange(GRID_W, dtype=jnp.float32), rows)
    axis_dim = MLA_ROPE // 2
    inv_freq = ROPE_BASE ** (-jnp.arange(0, axis_dim, 2, dtype=jnp.float32) / axis_dim)
    ang_r = row_pos[:, None] * inv_freq
    ang_c = col_pos[:, None] * inv_freq
    ang = jnp.concatenate([ang_r, ang_r, ang_c, ang_c], axis=-1)
    return (jnp.cos(ang).astype(dtype)[None, :, None, :], jnp.sin(ang).astype(dtype)[None, :, None, :])

def apply_rope(x, cos, sin):
    r1, r2, c1, c2 = jnp.split(x, 4, axis=-1)
    rot = jnp.concatenate([-r2, r1, -c2, c1], axis=-1)
    return x * cos + rot * sin

def mla_queries(p, q_norm_g, w_uq, rope):
    b, t, _ = p.shape
    cq = rms_norm_2(p[..., O_CQ:O_CKV], q_norm_g)
    q = (cq @ w_uq).reshape(b, t, MLA_HEADS, MLA_NOPE + MLA_ROPE)
    q_nope, q_pe = q[..., :MLA_NOPE], q[..., MLA_NOPE:]
    if rope is not None:
        q_pe = apply_rope(q_pe, rope[0], rope[1])
    return jnp.concatenate([q_nope, q_pe], axis=-1)

def mla_keys_values(p, kv_norm_g, w_ukv, rope):
    b, t, _ = p.shape
    ckv = rms_norm_2(p[..., O_CKV:O_KR], kv_norm_g)
    kv = (ckv @ w_ukv).reshape(b, t, MLA_HEADS, MLA_NOPE + MLA_V)
    k_nope, v = kv[..., :MLA_NOPE], kv[..., MLA_NOPE:]
    k_pe = p[..., O_KR:O_HQ][:, :, None, :]
    if rope is not None:
        k_pe = apply_rope(k_pe, rope[0], rope[1])
    k = jnp.concatenate([k_nope, jnp.broadcast_to(k_pe, (b, t, MLA_HEADS, MLA_ROPE))], axis=-1)
    return k, v

def block_attention(q, k, v):
    b, t, h, dk = q.shape
    nb = t // ATTN_BLOCK
    qb = q.reshape(b, nb, ATTN_BLOCK, h, dk).swapaxes(0, 1)
    scale = 1.0 / math.sqrt(dk)

    def one_block(qi):
        s = jnp.einsum('bqhd,bkhd->bhqk', qi, k).astype(jnp.float32) * scale
        pr = jax.nn.softmax(s, axis=-1).astype(v.dtype)
        return jnp.einsum('bhqk,bkhd->bqhd', pr, v)

    o = lax.map(one_block, qb)
    return o.swapaxes(0, 1).reshape(b, t, h * v.shape[-1])

def chunk_gated_scan(q, k, v, log_f, s0, with_output):
    b, t, h, kd = q.shape
    n = t // HG_CHUNK

    def to_chunks(a):
        return a.reshape(b, n, HG_CHUNK, h, a.shape[-1]).swapaxes(0, 1)

    causal = jnp.tril(jnp.ones((HG_CHUNK, HG_CHUNK), dtype=bool))[None, :, :, None, None]

    def step(state, inp):
        qc, kc, vc, gc = inp
        bcum = jnp.cumsum(gc, axis=1)
        total = bcum[:, -1]
        new_state = jnp.exp(total)[..., None] * state + jnp.einsum(
            'bshk,bshv->bhkv', kc * jnp.exp(total[:, None] - bcum), vc)
        if not with_output:
            return new_state, None
        decay = jnp.exp(jnp.where(causal, bcum[:, :, None] - bcum[:, None], -jnp.inf))
        scores = jnp.einsum('bthk,btshk,bshk->bhts', qc, decay, kc)
        o = jnp.einsum('bhts,bshv->bthv', scores, vc) + jnp.einsum(
            'bthk,bhkv->bthv', qc * jnp.exp(bcum), state)
        return new_state, o

    s_fin, o = lax.scan(step, s0, (to_chunks(q), to_chunks(k), to_chunks(v), to_chunks(log_f)))
    if with_output:
        o = o.swapaxes(0, 1).reshape(b, t, h, v.shape[-1])
    return o, s_fin

def hgrn2_inputs(p, lb_fb):
    b, t, _ = p.shape
    q = jax.nn.silu(p[..., O_HQ:O_HFF].astype(jnp.float32)).reshape(b, t, HG_HEADS, HG_K)
    i = p[..., O_HI:O_HG].astype(jnp.float32).reshape(b, t, HG_HEADS, HG_V)

    def gate(z, lb):
        f = lb + (1.0 - lb) * jax.nn.sigmoid(z.astype(jnp.float32))
        return (1.0 - f).reshape(b, t, HG_HEADS, HG_K), jnp.log(f).reshape(b, t, HG_HEADS, HG_K)

    fwd = gate(p[..., O_HFF:O_HFB], lb_fb[0])
    bwd = gate(p[..., O_HFB:O_HI], lb_fb[1])
    return q, i, fwd, bwd

def hgrn2_readout(o, z_gate, gain):
    b, t = o.shape[0], o.shape[1]
    on = o * lax.rsqrt(jnp.mean(o * o, axis=-1, keepdims=True) + EPS)
    on = on * gain.astype(jnp.float32).reshape(HG_HEADS, HG_V)
    return (on.reshape(b, t, HG_WIDTH) * jax.nn.silu(z_gate.astype(jnp.float32))).astype(z_gate.dtype)

def fourier_mix(z, w):
    b, t, _ = z.shape
    zg = z.astype(jnp.float32).reshape(b, t, FN_GROUPS, FN_GROUP_DIM)
    mixed = jnp.fft.fft2(zg, axes=(1, 3), norm='ortho').real
    return mixed.reshape(b, t, FN_WIDTH).astype(z.dtype) @ w

def swiglu_ffn(h, w_gu, w_dn):
    gate, up = jnp.split(h @ w_gu, 2, axis=-1)
    return (jax.nn.silu(gate) * up) @ w_dn

def second_inputs(seed: int = 0) -> dict:
    key = jax.random.key(seed)
    ks = jax.random.split(key, 20)
    f32 = jnp.float32

    def nrm(k, shape, scale):
        return jax.random.normal(k, shape, f32) * scale

    def gain(k, shape):
        return 1.0 + 0.02 * jax.random.normal(k, shape, f32)

    return {
        'x': nrm(ks[0], (BATCH, SEQ, D_MODEL), 1.0),
        'c': nrm(ks[1], (BATCH, D_MODEL), 1.0),
        'ctx': nrm(ks[2], (BATCH, CTX_LEN, D_MODEL), 1.0),
        'c_ctx': nrm(ks[3], (D_MODEL,), 1.0),
        'w_mod': nrm(ks[4], (DEPTH_2, D_MODEL, 6 * D_MODEL), D_MODEL ** -0.5),
        'b_mod': nrm(ks[5], (DEPTH_2, 6 * D_MODEL), 0.02),
        'norm1_g': gain(ks[6], (DEPTH_2, D_MODEL)),
        'norm2_g': gain(ks[7], (DEPTH_2, D_MODEL)),
        'w_in': nrm(ks[8], (DEPTH_2, D_MODEL, IN_WIDTH_2), D_MODEL ** -0.5),
        'q_norm_g': gain(ks[9], (DEPTH_2, MLA_Q_LORA)),
        'w_uq': nrm(ks[10], (DEPTH_2, MLA_Q_LORA, MLA_HEADS * (MLA_NOPE + MLA_ROPE)), MLA_Q_LORA ** -0.5),
        'kv_norm_g': gain(ks[11], (DEPTH_2, MLA_KV_LORA)),
        'w_ukv': nrm(ks[12], (DEPTH_2, MLA_KV_LORA, MLA_HEADS * (MLA_NOPE + MLA_V)), MLA_KV_LORA ** -0.5),
        'lb_param': nrm(ks[13], (DEPTH_2, 2, HG_HEADS * HG_K), 1.0),
        'hg_norm_g': gain(ks[14], (DEPTH_2, HG_WIDTH)),
        'w_fourier': nrm(ks[15], (DEPTH_2, FN_WIDTH, FN_WIDTH), FN_WIDTH ** -0.5),
        'w_out': nrm(ks[16], (DEPTH_2, MIX_WIDTH_2, D_MODEL), MIX_WIDTH_2 ** -0.5),
        'w_gate_up': nrm(ks[17], (DEPTH_2, D_MODEL, 2 * FFN_HIDDEN), D_MODEL ** -0.5),
        'w_down': nrm(ks[18], (DEPTH_2, FFN_HIDDEN, D_MODEL), FFN_HIDDEN ** -0.5),
        'final_norm_g': gain(ks[19], (D_MODEL,)),
    }

def second_block(x, c, ctx, c_ctx, w_mod, b_mod, norm1_g, norm2_g, w_in, q_norm_g, w_uq, kv_norm_g, w_ukv,
              lb_param, hg_norm_g, w_fourier, w_out, w_gate_up, w_down, final_norm_g):
    b, t, _ = x.shape
    rope = axial_rope(t, x.dtype)
    probs = jax.nn.softmax(lb_param.astype(jnp.float32), axis=0)
    lower_bounds = jnp.cumsum(probs, axis=0) - probs[0]
    s_zero = jnp.zeros((b, HG_HEADS, HG_K, HG_V), jnp.float32)
    c_act = jax.nn.silu(c)
    cc_act = jax.nn.silu(c_ctx)

    def flip(a):
        return jnp.flip(a, axis=1)

    for l in range(DEPTH_2):
        last = l == DEPTH_2 - 1
        sh1, sc1, g1, sh2, sc2, g2 = jnp.split((c_act @ w_mod[l] + b_mod[l])[:, None, :], 6, axis=-1)
        csh1, csc1, cg1, csh2, csc2, cg2 = jnp.split((cc_act @ w_mod[l] + b_mod[l])[None, None, :], 6, axis=-1)

        p = modulate(x, norm1_g[l], sh1, sc1) @ w_in[l]
        pc = modulate(ctx, norm1_g[l], csh1, csc1) @ w_in[l]

        k_lat, v_lat = mla_keys_values(p, kv_norm_g[l], w_ukv[l], rope)
        k_ctx, v_ctx = mla_keys_values(pc, kv_norm_g[l], w_ukv[l], None)
        q_lat = mla_queries(p, q_norm_g[l], w_uq[l], rope)
        attn = block_attention(q_lat, jnp.concatenate([k_lat, k_ctx], axis=1),
                               jnp.concatenate([v_lat, v_ctx], axis=1))

        lb_fb = lower_bounds[l]
        qc, ic, (kcf, lcf), (kcb, lcb) = hgrn2_inputs(pc, lb_fb)
        o_cf, s_cf = chunk_gated_scan(qc, kcf, ic, lcf, s_zero, not last)
        o_cb, s_cb = chunk_gated_scan(flip(qc), flip(kcb), flip(ic), flip(lcb), s_zero, not last)
        ql, il, (klf, llf), (klb, llb) = hgrn2_inputs(p, lb_fb)
        o_lf, _ = chunk_gated_scan(ql, klf, il, llf, s_cf, True)
        o_lb, _ = chunk_gated_scan(flip(ql), flip(klb), flip(il), flip(llb), s_cb, True)
        hg = hgrn2_readout(o_lf + flip(o_lb), p[..., O_HG:O_FN], hg_norm_g[l])

        fn = fourier_mix(p[..., O_FN:IN_WIDTH_2], w_fourier[l])

        y = jnp.concatenate([attn, hg, fn], axis=-1) @ w_out[l]
        x_new = x + g1 * y
        x_new = x_new + g2 * swiglu_ffn(modulate(x_new, norm2_g[l], sh2, sc2), w_gate_up[l], w_down[l])

        if not last:
            attn_c = block_attention(mla_queries(pc, q_norm_g[l], w_uq[l], None), k_ctx, v_ctx)
            hg_c = hgrn2_readout(o_cf + flip(o_cb), pc[..., O_HG:O_FN], hg_norm_g[l])
            fn_c = fourier_mix(pc[..., O_FN:IN_WIDTH_2], w_fourier[l])
            yc = jnp.concatenate([attn_c, hg_c, fn_c], axis=-1) @ w_out[l]
            ctx = ctx + cg1 * yc
            ctx = ctx + cg2 * swiglu_ffn(modulate(ctx, norm2_g[l], csh2, csc2), w_gate_up[l], w_down[l])
        x = x_new

    return rms_norm_2(x, final_norm_g)


def setup_inputs(seed=0):
    out = dict(first_inputs(seed))
    for name, value in second_inputs(seed + 1).items():
        if name != "x":
            out[name + "_2"] = value
    return out


def reference(
    x, mix_norm, ffn_norm, hy_w_in, hy_w_gate2, hy_b_gate, hy_gla_norm, hy_sb_q_norm,
    hy_sb_k_norm, hy_w_out, cv_w_pw1, cv_b_pw1, cv_w_dw, cv_b_dw, cv_ln_g, cv_ln_b, cv_w_pw2,
    cv_b_pw2, ffn_w_gate, ffn_w_up, ffn_w_down, c_2, ctx_2, c_ctx_2, w_mod_2, b_mod_2,
    norm1_g_2, norm2_g_2, w_in_2, q_norm_g_2, w_uq_2, kv_norm_g_2, w_ukv_2, lb_param_2,
    hg_norm_g_2, w_fourier_2, w_out_2, w_gate_up_2, w_down_2, final_norm_g_2,
):
    x = first_block(
        x, mix_norm, ffn_norm, hy_w_in, hy_w_gate2, hy_b_gate, hy_gla_norm, hy_sb_q_norm,
        hy_sb_k_norm, hy_w_out, cv_w_pw1, cv_b_pw1, cv_w_dw, cv_b_dw, cv_ln_g, cv_ln_b,
        cv_w_pw2, cv_b_pw2, ffn_w_gate, ffn_w_up, ffn_w_down,
    )
    return second_block(
        x, c_2, ctx_2, c_ctx_2, w_mod_2, b_mod_2, norm1_g_2, norm2_g_2, w_in_2, q_norm_g_2,
        w_uq_2, kv_norm_g_2, w_ukv_2, lb_param_2, hg_norm_g_2, w_fourier_2, w_out_2,
        w_gate_up_2, w_down_2, final_norm_g_2,
    )


_drawn_inputs = setup_inputs


def setup_inputs(seed=0):
    import zlib

    import numpy as np

    out = dict(_drawn_inputs(seed))
    spreads = {}
    factors = {'hy_sb_q_norm': 4.834,
     'hy_sb_k_norm': 5.265,
     'cv_b_pw1': 5.537,
     'cv_b_dw': 2.832,
     'cv_ln_b': 5.964,
     'cv_b_pw2': 3.645,
     'ctx_2': 3.852,
     'b_mod_2': 2.721,
     'norm1_g_2': 8.0,
     'norm2_g_2': 16.706,
     'q_norm_g_2': 8.0,
     'kv_norm_g_2': 8.0,
     'hg_norm_g_2': 8.0}
    for name, (base, spread) in spreads.items():
        noise = np.random.default_rng([zlib.crc32(name.encode()), seed]).standard_normal(out[name].shape)
        drawn = base * np.exp(spread * noise) if base else spread * noise
        out[name] = __import__('jax').numpy.asarray(drawn.astype(out[name].dtype))
    for name, factor in factors.items():
        out[name] = (out[name] * factor).astype(out[name].dtype)
    return out
```

```python
from contextlib import ExitStack

import numpy as np

P = 128
D, T, KT = 1024, 256, 8
FT = 22
BLK = 16
UNIT = BLK * P
SLOTS, RAW_SLOTS = 3, 2
CHUNK = 64
TAPS = 31
EPS = 1e-6
N_IN1, N_OUT, N_PW1, N_IN2 = 12, 4, 8, 11
N_FFN = 33
MODB = 48
LEVELS = (32, 16, 8, 4, 2, 1)

U_IN1 = 0
U_OUT1 = U_IN1 + N_IN1
U_FFN = [U_OUT1 + N_OUT, 0, 0]
U_PW1 = U_FFN[0] + N_FFN
U_PW2 = U_PW1 + N_PW1
U_FFN[1] = U_PW2 + N_OUT
U_IN2 = U_FFN[1] + N_FFN
U_OUT2 = U_IN2 + N_IN2
U_FFN[2] = U_OUT2 + N_OUT
UNITS = U_FFN[2] + N_FFN

PAR = {}
_at = 0
for _name, _n in (("mixn0", 8), ("mixn1", 8), ("ffnn0", 8), ("ffnn1", 8), ("glan", 1), ("sbq", 1), ("sbk", 1),
                  ("bgate", 2), ("bpw1", 16), ("bdw", 8), ("lng", 8), ("lnb", 8), ("bpw2", 8), ("wdw", 8 * TAPS),
                  ("c2", 16), ("bmod", 48), ("n1g", 8), ("n2g", 8), ("qng", 2), ("kvg", 1), ("hgg", 2), ("fing", 8),
                  ("wglr", 8 * 16), ("wgate2", 256)):
    PAR[_name] = (_at, _n)
    _at += _n
N_PAR = _at

CST = {"ones": (0, 128), "blk": (128, 128), "ident": (256, 128)}
N_CST = 384
CSB = {"tri": (0, 128), "sbmask": (128, 384)}
N_CSB = 512
CS2 = {}
_at = 0
for _name, _n in (("lmask", 13 * 128), ("fd", 256), ("ft", 4 * 256), ("cos", 256), ("sin", 256), ("rot", 128),
                  ("wfou", 512)):
    CS2[_name] = (_at, _n)
    _at += _n
N_CS2 = _at
N_MLW = 2 * 768 + 1024


def program(nc, A):
    import concourse.bass as bass
    from concourse import mybir

    F32, F32R, BF16, I32 = mybir.dt.float32, mybir.dt.float32r, mybir.dt.bfloat16, mybir.dt.int32
    ACT, ALU, AX = mybir.ActivationFunctionType, mybir.AluOpType, mybir.AxisListType

    with ExitStack() as ctx:
        sems = {}

        def S(name):
            if name not in sems:
                sems[name] = ctx.enter_context(nc.semaphore(name))
            return sems[name]

        base = -(-nc.sbuf_base // 64) * 64

        def at(name, kib, cols, dt=F32, parts=P):
            return nc.alloc_sbuf_tensor_at(name, [parts, cols], dt, offset=base + int(kib * 1024))

        raw = at("raw", 0, RAW_SLOTS * UNIT)[:, :].rearrange("p (s n) -> p s n", s=RAW_SLOTS)
        w_hi = at("w_hi", 16, SLOTS * UNIT, F32R)[:, :].rearrange("p (s n) -> p s n", s=SLOTS)
        w_lo = at("w_lo", 40, SLOTS * UNIT, F32R)[:, :].rearrange("p (s n) -> p s n", s=SLOTS)
        X = at("X", 64, KT * T)[:, :].rearrange("p (k t) -> p k t", k=KT)
        a_hi = at("a_hi", 72, KT * 2 * T, F32R)[:, :].rearrange("p (k s t) -> p k s t", k=KT, s=2)
        a_lo = at("a_lo", 88, KT * 2 * T, F32R)[:, :].rearrange("p (k s t) -> p k s t", k=KT, s=2)
        SQ = at("SQ", 104, KT * T)[:, :].rearrange("p (k t) -> p k t", k=KT)
        HN = at("HN", 112, KT * T)[:, :].rearrange("p (k t) -> p k t", k=KT)
        h_hi = at("h_hi", 120, 4 * T, F32R)[:, :].rearrange("p (j f t) -> p j f t", j=2, f=2)
        h_lo = at("h_lo", 124, 4 * T, F32R)[:, :].rearrange("p (j f t) -> p j f t", j=2, f=2)
        SG = at("SG", 128, 2 * T)[:, :].rearrange("p (f t) -> p f t", f=2)
        HF = at("HF", 130, 2 * T)[:, :].rearrange("p (f t) -> p f t", f=2)
        RS = at("RS", 132, T)[:, :]
        par = at("par", 133, N_PAR)[:, :]
        cst = at("cst", 137, N_CST)[:, :]
        zero = at("zero", 138.5, 512, BF16)[:, :]
        modraw = at("modraw", 140, 2 * 1024)[:, :].rearrange("p (s n) -> p s n", s=2)
        MIX = at("MIX", 148, KT * T)[:, :].rearrange("p (k t) -> p k t", k=KT)
        cst2 = at("cst2", 190, N_CS2)[:, :]
        CSL = at("CSL", 206.5, 16)[:, :].rearrange("p (k c) -> p k c", c=2)
        MOD = at("MOD", 206.5625, 96)[:, :].rearrange("p (n c) -> p n c", c=2)
        GSC = at("GSC", 206.9375, 24)[:, :].rearrange("p (n k) -> p n k", k=8)

        def prm(name, i=0, n=1):
            return par[:, PAR[name][0] + i:PAR[name][0] + i + n]

        ones, blk, ident = (cst[:, CST[n][0]:CST[n][0] + 128] for n in ("ones", "blk", "ident"))

        def c2(name):
            return cst2[:, CS2[name][0]:CS2[name][0] + CS2[name][1]]

        PS = ctx.enter_context(nc.psum_tensor("PS", [P, 8, 512], F32))[:, :, :]

        def banks(a, b):
            return PS[:, a:b, :].rearrange("p b n -> p (b n)")

        PROJ = at("PROJ", 156, N_IN1 * 512)[:, :].rearrange("p (u n) -> p u n", u=N_IN1)
        QKN = at("QKN", 180, 4 * 512)[:, :]
        csb = at("csb", 188, N_CSB)[:, :]
        tri, sbmask = csb[:, 0:128], csb[:, 128:512]
        GLR = at("GLR", 131, T, F32, 16)[:, :]
        LA = at("LA", 73, 512)[:, :]
        GE = at("GE", 75, 512)[:, :]
        CUM = at("CUM", 77, 512)[:, :]
        RESET = at("RESET", 120, 512)[:, :]
        KEND = at("KEND", 81, 512)[:, :]
        KTOK = at("KTOK", 83, 512)[:, :]
        DEC = at("DEC", 85, 8)[:, :]
        ST = at("ST", 86, 1024)[:, :].rearrange("p (n a v) -> p n a v", n=4, a=2)
        OG = at("OG", 90, 1024)[:, :]
        OR = at("OR", 94, 1024)[:, :]
        RSG = at("RSG", 98, 1024)[:, :]
        SQF = at("SQF", 104, 2048)[:, :]
        RSF = at("RSF", 112, 2048)[:, :]
        SBL = at("SBL", 120, 768)[:, :].rearrange("p (e n) -> p e n", e=2)
        SBK = at("SBK", 123, 768)[:, :].rearrange("p (e n) -> p e n", e=2)
        SBM = at("SBM", 126, 768)[:, :].rearrange("p (e n) -> p e n", e=2)
        SBZ = at("SBZ", 129, 768)[:, :].rearrange("p (e n) -> p e n", e=2)
        PADT = T + 32
        CU = at("CU", 156, KT * PADT)[:, :].rearrange("p (k t) -> p k t", k=KT)
        SIG = at("SIG", 166, 2 * T)[:, :].rearrange("p (f t) -> p f t", f=2)
        CTX = at("CTX", 168, KT * T)[:, :].rearrange("p (k t) -> p k t", k=KT)
        MU = at("MU", 176, T)[:, :]
        ZF = at("ZF", 156, 4096)[:, :].rearrange("p (d s h t) -> p d s h t", d=2, s=2, h=4)
        XO = at("XO", 172, 10 * T)[:, :].rearrange("p (n t) -> p n t", n=10)
        CKV = at("CKV", 182, 1024)[:, :].rearrange("p (n t) -> p n t", n=2)
        HI = at("HI", 186, 1024)[:, :].rearrange("p (s t n) -> p (s t) n", s=2, t=2)
        mlw = at("mlw", 120, N_MLW)[:, :]
        QN = at("QN", 72, 1024)[:, :].rearrange("p (h t) -> p h t", h=4)
        QP = at("QP", 76, 512)[:, :]
        QR = at("QR", 78, 512)[:, :]
        KPE = at("KPE", 80, 512)[:, :]
        CKN = at("CKN", 82, 512)[:, :]
        KN = at("KN", 84, 2048)[:, :].rearrange("p (h t) -> p h t", h=4)
        VT = at("VT", 92, 2048)[:, :].rearrange("p (t n) -> p t n", t=4)
        PR = at("PR", 100, 1024)[:, :].rearrange("p (b t) -> p b t", b=2)
        PT = at("PT", 104, 1024)[:, :].rearrange("p (b t) -> p b t", b=2)
        SQ2 = at("SQ2", 108, 1024)[:, :]
        RS2 = at("RS2", 112, 1024)[:, :]
        FC = at("FC", 116, 1024)[:, :]
        MXS = at("MXS", 130, 32)[:, :]
        CQN = at("CQN", 140, 512)[:, :].rearrange("p (k t) -> p k t", k=2)
        FM = at("FM", 142, 512)[:, :].rearrange("p (k t) -> p k t", k=2)
        GG = at("GG", 72, 2048)[:, :].rearrange("p (s h t) -> p s h t", s=2, h=4)
        KK = at("KK", 80, 2048)[:, :].rearrange("p (s h t) -> p s h t", s=2, h=4)
        CC = at("CC", 88, 2048)[:, :].rearrange("p (s h t) -> p s h t", s=2, h=4)
        KWT = at("KWT", 96, 2048)[:, :].rearrange("p (t h k) -> p t h k", t=4, h=4)
        SX = at("SX", 104, 2048)[:, :].rearrange("p (d n m) -> p d n m", d=2, n=4)
        QF = at("QF", 112, 2048)[:, :].rearrange("p (d m) -> p d m", d=2)
        KS = at("KS", 120, 1024)[:, :]
        SC = at("SC", 124, 1024)[:, :]
        QQ = at("QQ", 128, 1024)[:, :]
        EX = at("EX", 140, 2048)[:, :].rearrange("p (b m) -> p b m", b=2)
        QM0 = at("QM0", 96, 1024)[:, :]
        KM0 = at("KM0", 100, 1024)[:, :]
        AD = at("AD", 136.5, 64)[:, :].rearrange("p (d m) -> p d m", d=2)
        STT = at("STT", 152, T)[:, :]
        STU = at("STU", 153, T)[:, :]
        RST64 = at("RST64", 132, T)[:, :]
        assert 133 + N_PAR * 4 / 1024 <= 136.5

        def QMd(d):
            return ZF[:, d, 0, :, :].rearrange("p h t -> p (h t)")

        def KMd(d):
            return ZF[:, d, 1, :, :].rearrange("p h t -> p (h t)")

        SQO = at("SQO", 140, 512)[:, :]
        OH = at("OH", 142, 512)[:, :]
        ZG = at("ZG", 144, 512)[:, :]
        RSO = at("RSO", 146, 512)[:, :]

        OA = MIX[:, 0:4, :].rearrange("p k t -> p (k t)")

        def raw_ap(u):
            return A["wstream"][bass.ds(u, 1)].rearrange("a p n -> (a p) n")

        def split_hi(act, u, slot, rslot, n):
            act.wait_ge(S(f"raw_loaded{rslot}"), n * 16)
            if not (isinstance(u, int) and u < SLOTS):
                act.wait_ge(S("unit_done"), u - (SLOTS - 1))
            nc.scalar.activation(w_hi[:, slot, :], raw[:, rslot, :], ACT.Copy).then_inc(S("hi_done"), 1)

        def split_lo(dve, u, slot, rslot):
            dve.wait_ge(S("hi_done"), u + 1)
            dve.tensor_tensor(w_lo[:, slot, :], raw[:, rslot, :], w_hi[:, slot, :].bitcast(F32),
                              ALU.subtract).then_inc(S("lo_done"), 1)

        def hi(act, u):
            if u < UNITS:
                split_hi(act, u, u % SLOTS, u % RAW_SLOTS, u // RAW_SLOTS + 1)

        def lo(dve, u):
            if u < UNITS:
                split_lo(dve, u, u % SLOTS, u % RAW_SLOTS)

        def split_mm(out, H, L, xh, xl, start, stop, **kw):
            nc.tensor.matmul(out, H, xh, start=start, stop=False, **kw)
            nc.tensor.matmul(out, H, xl, start=False, stop=False, **kw)
            return nc.tensor.matmul(out, L, xh, start=False, stop=stop, **kw)

        def wblk(slot, b):
            return w_hi[:, slot, b * P:(b + 1) * P], w_lo[:, slot, b * P:(b + 1) * P]

        def feature_unit(slot, outs, src, wait_k=None):
            for nb in range(2):
                for k in range(KT):
                    if nb == 0 and wait_k is not None:
                        wait_k(k)
                    H, L = wblk(slot, nb * KT + k)
                    last = split_mm(outs[nb], H, L, a_hi[:, k, src, :], a_lo[:, k, src, :], k == 0, k == KT - 1)
            return last

        def token_unit(slot, outs):
            for s, t, out in outs:
                for k in range(KT):
                    wh, wl = (w[:, slot, k * 256:(k + 1) * 256] for w in (w_hi, w_lo))
                    xh, xl = (a[:, k, s, t * P:(t + 1) * P] for a in (a_hi, a_lo))
                    nc.tensor.matmul(out, xh, wh, start=k == 0, stop=False)
                    nc.tensor.matmul(out, xl, wh, start=False, stop=False)
                    last = nc.tensor.matmul(out, xh, wl, start=False, stop=k == KT - 1)
            return last

        NORMS = ["mix0", "ffn0", "mix1", "ffn1", "ctx", "mix2", "ffn2", "final"]

        def norm_src(n):
            return CTX if NORMS[n] == "ctx" else X

        def wait_x(eng, n, j):
            if n == 0:
                eng.wait_ge(S("x_loaded"), 16)
            elif NORMS[n] == "ctx":
                eng.wait_ge(S("ctx_loaded"), 16)
            else:
                eng.wait_ge(S("x_updated"), 4 * (RES[n]) + j + 1)

        RES = {1: 0, 2: 1, 3: 2, 5: 3, 6: 4, 7: 5}

        def norm_act(act, n, shift=None, split=True):
            x = norm_src(n)
            for j in range(4):
                wait_x(act, n, j)
                nc.scalar.activation(SQ[:, 2 * j:2 * j + 2, :], x[:, 2 * j:2 * j + 2, :], ACT.Square)\
                    .then_inc(S("norm_sq"), 1)
            act.wait_ge(S("norm_ss"), n + 1)
            nc.scalar.activation(RS, PS[:, 6, 0:T], ACT.Ln, scale=1.0 / D, bias=prm_eps).then_inc(S("norm_ln"), 1)
            act.wait_ge(S("norm_ln"), n + 1)
            nc.scalar.activation(RS, RS, ACT.Exp, scale=-0.5).then_inc(S("norm_rs"), 1)
            if not split:
                return
            s = 1 if NORMS[n] == "ctx" else 0
            for j in range(4):
                act.wait_ge(S("norm_hn"), 8 * n + 2 * j + 2)
                if shift is None:
                    nc.scalar.activation(a_hi[:, 2 * j:2 * j + 2, s, :], HN[:, 2 * j:2 * j + 2, :], ACT.Copy)\
                        .then_inc(S("norm_hi"), 1)
                else:
                    for k in (2 * j, 2 * j + 1):
                        i = nc.scalar.activation(a_hi[:, k, s, :], HN[:, k, :], ACT.Identity, bias=shift(k))
                    i.then_inc(S("norm_hi"), 1)

        def norm_pe(pe, n):
            for k in range(KT):
                pe.wait_ge(S("norm_sq"), 4 * n + k // 2 + 1)
                if k == 0 and n > 0:
                    pe.wait_ge(S("norm_rs"), n)
                i = nc.tensor.matmul(PS[:, 6, 0:T], ones, SQ[:, k, :], start=k == 0, stop=k == KT - 1)
            i.then_inc(S("norm_ss"), 1)

        def norm_dve(dve, n, gain, shift=None, split=True):
            x = norm_src(n)
            dve.wait_ge(S("norm_rs"), n + 1)
            if NORMS[n] == "mix2":
                dve.wait_ge(S("act_lo"), ACT_LO["mix2"])
            for k in range(KT):
                dve.scalar_tensor_tensor(HN[:, k, :], x[:, k, :], gain(k), RS, ALU.mult, ALU.mult)\
                    .then_inc(S("norm_hn"), 1)
            if not split:
                return
            s = 1 if NORMS[n] == "ctx" else 0
            for j in range(4):
                dve.wait_ge(S("norm_hi"), 4 * (n) + j + 1)
                ks = slice(2 * j, 2 * j + 2)
                if shift is None:
                    dve.tensor_tensor(a_lo[:, ks, s, :], HN[:, ks, :], a_hi[:, ks, s, :].bitcast(F32), ALU.subtract)\
                        .then_inc(S("act_lo"), 1)
                else:
                    for k in (2 * j, 2 * j + 1):
                        i = dve.scalar_tensor_tensor(a_lo[:, k, s, :], HN[:, k, :], shift(k),
                                                     a_hi[:, k, s, :].bitcast(F32), ALU.add, ALU.subtract)
                    i.then_inc(S("act_lo"), 1)

        ACT_LO = {"mix0": 0, "o1": 4, "ffn0": 8, "mix1": 12, "cv": 16, "ffn1": 20, "ctx": 24, "mix2": 28, "o2": 32,
                  "ffn2": 36}

        def wait_act(pe, event, k):
            pe.wait_ge(S("act_lo"), ACT_LO[event] + k // 2 + 1)

        def mix_split_act(act, m, ready):
            for j in range(4):
                ready(act, j)
                nc.scalar.activation(a_hi[:, 2 * j:2 * j + 2, 0, :], MIX[:, 2 * j:2 * j + 2, :], ACT.Copy)\
                    .then_inc(S("mix_hi"), 1)

        def mix_split_dve(dve, m):
            for j in range(4):
                ks = slice(2 * j, 2 * j + 2)
                dve.wait_ge(S("mix_hi"), 4 * m + j + 1)
                dve.tensor_tensor(a_lo[:, ks, 0, :], MIX[:, ks, :], a_hi[:, ks, 0, :].bitcast(F32), ALU.subtract)\
                    .then_inc(S("act_lo"), 1)

        def out_units_pe(pe, u0, event, update):
            for j in range(N_OUT):
                u = u0 + j
                pe.wait_ge(S("lo_done"), u + 1)
                if j >= 2:
                    pe.wait_ge(S("x_updated"), 4 * update + j - 1)
                outs = [PS[:, 4 + j % 2, nb * T:(nb + 1) * T] for nb in range(2)]
                feature_unit(u % SLOTS, outs, 0, (lambda k: wait_act(pe, event, k)) if j == 0 else None)\
                    .then_inc(S("unit_done"), 1)

        PAIRS = FT // 2

        def ffn_pe(pe, f, event):
            u0 = U_FFN[f]
            if f:
                pe.wait_ge(S("x_updated"), 4 * (2 * f - 1) + 4)
            for b in range(4):
                nc.tensor.matmul(PS[:, b, :], zero[:, 0:P], zero, start=True, stop=True)

            def gate_up(u, slot, fb, j, first=False):
                pe.wait_ge(S("lo_done"), u + 1)
                if j is not None:
                    pe.wait_ge(S("hf_done"), (j - 1 + f * PAIRS) * 2 + fb + 1)
                outs = [PS[:, 4 + fb, g * T:(g + 1) * T] for g in range(2)]
                feature_unit(slot, outs, 0, (lambda k: wait_act(pe, event, k)) if first else None)\
                    .then_inc(S("unit_done"), 1)

            def down(u, slot, j, par_):
                pe.wait_ge(S("lo_done"), u + 1)
                for kk in range(2):
                    pe.wait_ge(S("h_lo_done"), (j + f * PAIRS) * 2 + kk + 1)
                    for nb in range(KT):
                        H, L = wblk(slot, kk * KT + nb)
                        i = split_mm(PS[:, nb // 2, (nb % 2) * T:(nb % 2 + 1) * T], H, L, h_hi[:, par_, kk, :],
                                     h_lo[:, par_, kk, :], False, False, skip_group_check=True)
                i.then_inc(S("unit_done"), 1)

            gate_up(u0, u0 % SLOTS, 0, None, True)
            gate_up(u0 + 1, (u0 + 1) % SLOTS, 1, None)
            with pe.Fori(0, (PAIRS - 1) // 2) as i:
                for r in range(2):
                    for q in range(3):
                        u = i * 6 + (u0 + 2 + 3 * r + q)
                        slot = (u0 + 2 + 3 * r + q) % SLOTS
                        if q < 2:
                            gate_up(u, slot, q, i * 2 + (1 + r))
                        else:
                            down(u, slot, i * 2 + r, r)
            down(u0 + N_FFN - 1, (u0 + N_FFN - 1) % SLOTS, PAIRS - 1, (PAIRS - 1) % 2)

        def ffn_act(act, f):
            u0 = U_FFN[f]

            def evac(u, fb, par_, j):
                act.wait_ge(S("unit_done"), u + 1)
                nc.scalar.activation(SG[:, fb, :], PS[:, 4 + fb, 0:T], ACT.Silu).then_inc(S("silu_done"), 1)
                act.wait_ge(S("hf_done"), (j + f * PAIRS) * 2 + fb + 1)
                nc.scalar.activation(h_hi[:, par_, fb, :], HF[:, fb, :], ACT.Copy).then_inc(S("h_hi_done"), 1)

            for q in range(2):
                hi(act, u0 + q + 2)
                evac(u0 + q, q, 0, 0)
            def turn(i):
                for r in range(2):
                    for q in range(3):
                        v = u0 + 2 + 3 * r + q
                        w = v + 2
                        if not (isinstance(i, int) and i * 6 + w >= UNITS):
                            split_hi(act, i * 6 + w, w % SLOTS, w % RAW_SLOTS, i * 3 + (w // RAW_SLOTS + 1))
                        if q < 2:
                            evac(i * 6 + v, q, (1 + r) % 2, i * 2 + (1 + r))

            turns = (PAIRS - 1) // 2
            with act.Fori(0, turns - 1) as i:
                turn(i)
            turn(turns - 1)
            hi(act, u0 + N_FFN + 1)

        def ffn_dve(dve, f, gate=None):
            u0 = U_FFN[f]

            def evac(u, fb, par_, j):
                n = (j + f * PAIRS) * 2 + fb + 1
                dve.wait_ge(S("silu_done"), n)
                dve.tensor_tensor(HF[:, fb, :], SG[:, fb, :], PS[:, 4 + fb, T:2 * T], ALU.mult)\
                    .then_inc(S("hf_done"), 1)
                dve.wait_ge(S("h_hi_done"), n)
                dve.tensor_tensor(h_lo[:, par_, fb, :], HF[:, fb, :], h_hi[:, par_, fb, :].bitcast(F32),
                                  ALU.subtract).then_inc(S("h_lo_done"), 1)

            for q in range(2):
                lo(dve, u0 + q + 2)
                evac(u0 + q, q, 0, 0)
            def turn(i):
                for r in range(2):
                    for q in range(3):
                        v = u0 + 2 + 3 * r + q
                        w = v + 2
                        if not (isinstance(i, int) and i * 6 + w >= UNITS):
                            split_lo(dve, i * 6 + w, w % SLOTS, w % RAW_SLOTS)
                        if q < 2:
                            evac(i * 6 + v, q, (1 + r) % 2, i * 2 + (1 + r))

            turns = (PAIRS - 1) // 2
            with dve.Fori(0, turns - 1) as i:
                turn(i)
            turn(turns - 1)
            lo(dve, u0 + N_FFN + 1)
            dve.wait_ge(S("unit_done"), u0 + N_FFN)
            for j in range(4):
                if gate is None:
                    ks = slice(2 * j, 2 * j + 2)
                    dve.tensor_tensor(X[:, ks, :], X[:, ks, :], PS[:, j, :].rearrange("p (k t) -> p k t", k=2),
                                      ALU.add).then_inc(S("x_updated"), 1)
                else:
                    for e in range(2):
                        k = 2 * j + e
                        i = dve.scalar_tensor_tensor(X[:, k, :], PS[:, j, e * T:(e + 1) * T], gate(k), X[:, k, :],
                                                     ALU.mult, ALU.add)
                    i.then_inc(S("x_updated"), 1)

        tick = at("tick", 207.125, 8)[:, :]
        epsc = at("epsc", 207.1875, 2)[:, :]
        prm_eps = epsc[:, 0:1]

        def half(e):
            return slice(64 * e, 64 * e + 64)

        block = ctx.enter_context(nc.Block())

        @block.sync
        def _(sp):
            sp.dma_start(X.rearrange("p k t -> p (k t)"), A["xT"]).then_inc(S("x_loaded"), 16)
            for u in range(RAW_SLOTS):
                sp.dma_start(raw[:, u, :], raw_ap(u)).then_inc(S(f"raw_loaded{u}"), 16)
            with sp.Fori(0, UNITS // RAW_SLOTS - 1) as i:
                for s in range(RAW_SLOTS):
                    sp.wait_ge(S("lo_done"), i * RAW_SLOTS + (s + 1))
                    sp.dma_start(raw[:, s, :], raw_ap(i * RAW_SLOTS + (RAW_SLOTS + s)))\
                        .then_inc(S(f"raw_loaded{s}"), 16)
            sp.wait_ge(S("norm_hn"), 64)
            sp.dma_start(A["out"], HN.rearrange("p k t -> p (k t)")).then_inc(S("out_stored"), 16)
            sp.wait_ge(S("out_stored"), 16)

        @block.tensor
        def _(pe):
            def mod_blocks(a, b):
                for m in range(a, b):
                    pe.wait_ge(S(f"mod_loaded{m % 2}"), 16 * (m // 2 + 1))
                    if m == 0:
                        pe.wait_ge(S("csl_done"), 1)
                    for k in range(KT):
                        i = nc.tensor.matmul(PS[:, 7, 2 * m:2 * m + 2], modraw[:, m % 2, k * P:(k + 1) * P],
                                             CSL[:, k, :], start=k == 0, stop=k == KT - 1)
                    i.then_inc(S("mod_done"), 1)

            pe.wait_ge(S("cst_loaded"), 16)
            pe.wait_ge(S("memset_done"), 4)
            norm_pe(pe, 0)
            pe.wait_ge(S("par_loaded"), 16)
            for k in range(KT):
                pe.wait_ge(S("norm_hn"), k + 1)
                i = nc.tensor.matmul(PS[0:16, 3, 0:T], par[:, PAR["wglr"][0] + 16 * k:PAR["wglr"][0] + 16 * k + 16],
                                     HN[:, k, :], start=k == 0, stop=k == KT - 1)
            i.then_inc(S("glr_mm"), 1)
            with pe.Fori(0, 2) as i:
                for q in range(6):
                    pe.wait_ge(S("lo_done"), i * 6 + (q + 1))
                    pe.wait_ge(S(f"bank{4 + q % 2}_free"), i * 3 + (q // 2 + 1))
                    if q == 0:
                        pe.wait_ge(S("act_lo"), 4)
                    b = 4 + q % 2
                    outs = [PS[:, b, t * T:(t + 1) * T] for t in range(2)]
                    if q < 2:
                        last = token_unit(q % SLOTS, [(0, t, outs[t]) for t in range(2)])
                    else:
                        last = feature_unit(q % SLOTS, outs, 0)
                    last.then_inc(S("unit_done"), 1)
            pe.wait_ge(S("glr_done"), 1)
            for a in range(2):
                i = nc.tensor.matmul(PS[:, 3, a * T:(a + 1) * T],
                                     par[0:16, PAR["wgate2"][0] + a * P:PAR["wgate2"][0] + (a + 1) * P],
                                     GLR, start=True, stop=True)
            i.then_inc(S("gate_mm"), 1)
            for j in range(4):
                pe.wait_ge(S("qk_sq"), j + 1)
                if j == 3:
                    pe.wait_ge(S("gate_read"), 3)
                i = nc.tensor.matmul(PS[:, j, :], blk, SQF[:, j * 512:(j + 1) * 512], start=True, stop=True)
                i.then_inc(S("qk_ss"), 1)
            mod_blocks(0, 8)
            pe.wait_ge(S("kend_done"), 1)
            for t in range(2):
                for a in range(2):
                    i = nc.tensor.transpose(PS[:, 4, (t * 2 + a) * P:(t * 2 + a + 1) * P],
                                            KEND[:, a * T + t * P:a * T + (t + 1) * P], ident)
            i.then_inc(S("ktok_mm"), 1)
            pe.wait_ge(S("ktok_done"), 1)
            pe.wait_ge(S("qk_rs"), 1)
            for n in range(4):
                for h in range(4):
                    r = half(n % 2)
                    i = nc.tensor.matmul(
                        PS[half(h % 2), n % 2, ((n // 2) * 2 + h // 2) * P:((n // 2) * 2 + h // 2 + 1) * P],
                        KTOK[r, (n // 2) * T + h * 64:(n // 2) * T + h * 64 + 64],
                        PROJ[r, h // 2, (n // 2) * T + (h % 2) * P:(n // 2) * T + (h % 2 + 1) * P],
                        start=True, stop=True)
            i.then_inc(S("upd_mm"), 1)
            for n in range(4):
                pe.wait_ge(S("state_done"), 2 * n + 2)
                for h in range(4):
                    i = nc.tensor.matmul(PS[:, 2 + h % 2, (h // 2) * T + n * 64:(h // 2) * T + n * 64 + 64],
                                         ST[half(h % 2), n, h // 2, :],
                                         PROJ[half(h % 2), 3, (h // 2) * T + n * 64:(h // 2) * T + n * 64 + 64],
                                         start=True, stop=True)
            i.then_inc(S("og_mm"), 1)
            pe.wait_ge(S("og_sq"), 1)
            for e in range(2):
                i = nc.tensor.matmul(PS[:, e, :], ones, OR[:, e * 512:(e + 1) * 512], start=True, stop=True)
            i.then_inc(S("og_ss"), 1)

            def sb_z(g):
                if g == 0:
                    pe.wait_ge(S("qkn_done"), 2)
                    pe.wait_ge(S("og_rs"), 2)
                if g >= 2:
                    pe.wait_ge(S("sb_lz2"), g - 1)
                for e in range(2):
                    r, b = half(e), 2 * (g % 2) + e
                    kT, qT = QKN[r, g * T:(g + 1) * T], QKN[r, 1024 + g * T:1024 + (g + 1) * T]
                    nc.tensor.matmul(PS[:, b, 0:256], kT[:, 0:P], qT, start=True, stop=True)
                    i = nc.tensor.matmul(PS[:, b, 256:384], kT[:, P:T], qT[:, P:T], start=True, stop=True)
                i.then_inc(S("sb_z"), 1)

            sb_z(0)
            for g in range(4):
                if g < 3:
                    sb_z(g + 1)
                pe.wait_ge(S("sb_keep"), g + 1)
                if g == 0:
                    pe.wait_ge(S("bank5_free"), 7)
                    pe.wait_ge(S("ktok_done"), 1)
                else:
                    pe.wait_ge(S("sb_lz2"), g)
                for e in range(2):
                    nc.tensor.matmul(PS[:, 4 + e, 0:384], tri, SBM[:, e, :], start=True, stop=False)
                    i = nc.tensor.matmul(PS[:, 4 + e, 128:256], ones, SBM[:, e, 256:384], start=False, stop=True)
                i.then_inc(S("sb_between"), 1)
                pe.wait_ge(S("sb_w"), g + 1)
                if g:
                    pe.wait_ge(S("sb_o_read"), g)
                else:
                    pe.wait_ge(S("norm_rs"), 1)
                for e in range(2):
                    hcol = (g * 2 + e) * 64
                    v = [PROJ[:, 6 + hcol // 256, t * T + hcol % 256:t * T + hcol % 256 + 64] for t in range(2)]
                    nc.tensor.matmul(PS[half(e), 6, 0:256], v[0], SBZ[:, e, 0:256], start=True, stop=False)
                    i = nc.tensor.matmul(PS[half(e), 6, 128:256], v[1], SBZ[:, e, 256:384], start=False, stop=True)
                i.then_inc(S("sb_o"), 1)
            pe.wait_ge(S("sb_lz2"), 4)
            out_units_pe(pe, U_OUT1, "o1", 0)
            norm_pe(pe, 1)
            mod_blocks(8, 12)
            ffn_pe(pe, 0, "ffn0")
            norm_pe(pe, 2)
            mod_blocks(12, 16)
            for j in range(N_PW1):
                u = U_PW1 + j
                pe.wait_ge(S("lo_done"), u + 1)
                if j >= 2:
                    pe.wait_ge(S("cu_done"), j - 1)
                outs = [PS[:, 4 + j % 2, g * T:(g + 1) * T] for g in range(2)]
                feature_unit(u % SLOTS, outs, 0, (lambda k: wait_act(pe, "mix1", k)) if j == 0 else None)\
                    .then_inc(S("unit_done"), 1)
                mod_blocks(16 + 4 * j, 20 + 4 * j)
            for k in range(KT):
                pe.wait_ge(S("cv_done"), k + 1)
                i = nc.tensor.matmul(PS[:, 6, 0:T], ones, HN[:, k, :], start=k == 0, stop=k == KT - 1)
            i.then_inc(S("ln_sum"), 1)
            for k in range(KT):
                pe.wait_ge(S("ln_sq"), k // 4 + 1)
                i = nc.tensor.matmul(PS[:, 6, T:2 * T], ones, SQ[:, k, :], start=k == 0, stop=k == KT - 1)
            i.then_inc(S("ln_ss"), 1)
            out_units_pe(pe, U_PW2, "cv", 2)
            norm_pe(pe, 3)
            ffn_pe(pe, 1, "ffn1")
            norm_pe(pe, 4)
            norm_pe(pe, 5)
            pe.wait_ge(S("x_updated"), 16)
            for j in range(5):
                u = U_IN2 + j
                pe.wait_ge(S("lo_done"), u + 1)
                if j >= 2:
                    pe.wait_ge(S("in2_read"), j - 1)
                if j == 0:
                    pe.wait_ge(S("act_lo"), ACT_LO["mix2"] + 4)
                b = 2 * (j % 2)
                feature_unit(u % SLOTS, [PS[:, b + nb, :].rearrange("p (s t) -> p s t", s=2) for nb in range(2)],
                             slice(0, 2)).then_inc(S("unit_done"), 1)
            pe.wait_ge(S("lo_done"), U_IN2 + 6)
            pe.wait_ge(S("in2_read"), 4)
            token_unit((U_IN2 + 5) % SLOTS, [(s, t, PS[:, 2 + s, t * T:(t + 1) * T]) for s in range(2)
                                             for t in range(2)]).then_inc(S("unit_done"), 1)
            for j in range(5):
                u = U_IN2 + 6 + j
                pe.wait_ge(S("lo_done"), u + 1)
                if j >= 2:
                    pe.wait_ge(S("in2_read"), 6 + j - 1)
                feature_unit(u % SLOTS, [PS[:, 4 + j % 2, nb * T:(nb + 1) * T] for nb in range(2)], 0)\
                    .then_inc(S("unit_done"), 1)

            pe.wait_ge(S("in2_read"), 11)
            pe.wait_ge(S("cst2_loaded"), 16)
            fd = c2("fd")
            for t in range(2):
                for a in range(2):
                    i = nc.tensor.matmul(PS[:, t, a * T:(a + 1) * T], XO[:, 8 + a, t * P:(t + 1) * P], fd,
                                         start=True, stop=True)
            i.then_inc(S("fn_mm"), 1)
            pe.wait_ge(S("fc_done"), 1)
            ft = c2("ft").rearrange("p (c t n) -> p c t n", c=2, t=2)
            for a in range(2):
                for t in range(2):
                    for c in range(2):
                        i = nc.tensor.matmul(PS[:, 2, a * T:(a + 1) * T],
                                             FC[:, t * 512 + a * T + c * P:t * 512 + a * T + (c + 1) * P],
                                             ft[:, c, t, :], start=t + c == 0, stop=t + c == 2)
            i.then_inc(S("fn_mm"), 1)
            pe.wait_ge(S("fm_done"), 1)
            wf = c2("wfou").rearrange("p (k n) -> p k n", k=2)
            for a in range(2):
                for k in range(2):
                    i = nc.tensor.matmul(PS[:, 3, a * T:(a + 1) * T], wf[:, k, a * P:(a + 1) * P], FM[:, k, :],
                                         start=k == 0, stop=k == 1)
            i.then_inc(S("fn_mm"), 1)
            pe.wait_ge(S("ml_sq"), 1)
            for k in range(2):
                i = nc.tensor.matmul(PS[:, 4, 0:T], ones, SQ2[:, k * T:(k + 1) * T], start=k == 0, stop=k == 1)
            i = nc.tensor.matmul(PS[:, 5, :], ones, SQ2[:, 512:1024], start=True, stop=True)
            i.then_inc(S("ml_ss"), 1)
            pe.wait_ge(S("fn_read"), 3)
            pe.wait_ge(S("mlw_loaded"), 16)
            pe.wait_ge(S("ml_n"), 1)
            uq = mlw[:, 0:1536].rearrange("p (k n) -> p k n", k=2)
            for nb in range(6):
                for k in range(2):
                    i = nc.tensor.matmul(PS[:, nb // 2, (nb % 2) * T:(nb % 2 + 1) * T], uq[:, k, nb * P:(nb + 1) * P],
                                         CQN[:, k, :], start=k == 0, stop=k == 1)
            i.then_inc(S("ml_q"), 1)
            ukv = mlw[:, 1536:2560]
            pe.wait_ge(S("ml_n"), 2)
            for h in range(2):
                i = nc.tensor.matmul(PS[:, 4 + h, :], ukv[:, h * P:(h + 1) * P], CKN, start=True, stop=True)
                i.then_inc(S("ml_k"), 1)
            pe.wait_ge(S("ml_q_read"), 2)
            for h in range(2, 4):
                i = nc.tensor.matmul(PS[:, h - 2, :], ukv[:, h * P:(h + 1) * P], CKN, start=True, stop=True)
                i.then_inc(S("ml_k"), 1)
            i = nc.tensor.matmul(PS[:, 3, :], c2("rot"), QP, start=True, stop=True)
            i.then_inc(S("ml_rot"), 1)
            nc.tensor.matmul(PS[:, 6, 0:T], c2("rot"), CKV[:, 1, 0:T], start=True, stop=True).then_inc(S("ml_rot"), 1)
            for t in range(4):
                b = (2, 4, 5, 0)[t]
                if t == 1:
                    pe.wait_ge(S("ml_k_read"), 2)
                if t == 3:
                    pe.wait_ge(S("ml_k_read"), 4)
                nc.tensor.matmul(PS[:, b, :], CKN[:, t * P:(t + 1) * P], ukv[:, 512:1024], start=True, stop=True)\
                    .then_inc(S("ml_v"), 1)

            def ml_scores(i):
                h, t = i // 2, i % 2
                b = (1, 3)[i % 2]
                if i == 0:
                    pe.wait_ge(S("rope_done"), 2)
                    pe.wait_ge(S("ml_k_read"), 4)
                if i >= 2:
                    pe.wait_ge(S("ml_exp"), i - 1)
                nc.tensor.matmul(PS[:, b, :], QN[:, h, t * P:(t + 1) * P], KN[:, h, :], start=True, stop=False)
                r = half(h % 2)
                nc.tensor.matmul(PS[:, b, :], QR[r, (h // 2) * T + t * P:(h // 2) * T + (t + 1) * P], KPE[r, :],
                                 start=False, stop=True).then_inc(S("ml_s"), 1)

            ml_scores(0)
            for i in range(8):
                h, t = i // 2, i % 2
                if i < 7:
                    ml_scores(i + 1)
                pe.wait_ge(S("ml_p"), i + 1)
                if i == 0:
                    pe.wait_ge(S("ml_v_read"), 4)
                if i >= 2:
                    pe.wait_ge(S("ml_pt"), i - 1)
                for c in range(4):
                    j = nc.tensor.transpose(PS[:, 4 + i % 2, c * P:(c + 1) * P], PR[:, i % 2, c * P:(c + 1) * P], ident)
                j.then_inc(S("ml_tr"), 1)
                pe.wait_ge(S("ml_pt"), i + 1)
                b = 0 if h < 2 else 2
                for c in range(4):
                    j = nc.tensor.matmul(PS[:, b, (h % 2) * T + t * P:(h % 2) * T + (t + 1) * P],
                                         VT[:, c, h * P:(h + 1) * P], PT[:, i % 2, c * P:(c + 1) * P],
                                         start=c == 0, stop=c == 3)
                j.then_inc(S("ml_o"), 1)

            for d in range(2):
                pe.wait_ge(S("hg_kw"), d + 1)
                if d == 0:
                    pe.wait_ge(S("ml_o_read"), 2)
                for t in range(4):
                    if d == 1 or t >= 2:
                        pe.wait_ge(S("hg_kwt"), 4 * d + t - 1)
                    for h in range(4):
                        i = nc.tensor.transpose(PS[:, 4 + t % 2, h * P:(h + 1) * P],
                                                ZF[:, d, t // 2, h, (t % 2) * P:(t % 2 + 1) * P], ident)
                    i.then_inc(S("hg_tr"), 1)
                pe.wait_ge(S("hg_kwt"), 4 * d + 4)
                if d == 1:
                    pe.wait_ge(S("hg_copied"), 6)
                for s in (1, 0):
                    for n in range(4):
                        t, r = n // 2, half(n % 2)
                        for h in range(4):
                            i = nc.tensor.matmul(PS[:, 2 * (1 - s) + n % 2, t * T + h * 64:t * T + h * 64 + 64],
                                                 KWT[r, 2 * s + t, h, :], HI[r, 2 * s + t, h * 64:h * 64 + 64],
                                                 start=True, stop=True)
                    i.then_inc(S("hg_upd"), 1)
                for l in range(7):
                    st = 7 * d + l
                    if l < 6:
                        pe.wait_ge(S("hg_pair"), 6 * d + l + 1)
                        q, k = (QM0, KM0) if l % 2 == 0 else (QMd(d), KMd(d))
                    elif d == 0:
                        continue
                    else:
                        pe.wait_ge(S("hg_ks"), 2)
                        q, k = QQ, KS
                    bb = (4, 5) if l % 2 == 0 else (0, 1)
                    if l == 0:
                        pe.wait_ge(S("hg_kwt"), 4 * d + 4)
                    if l == 1:
                        pe.wait_ge(S("hg_state"), 7 * d + 7)
                    if l >= 2:
                        pe.wait_ge(S("hg_copied"), 6 * d + l - 1)
                    for m in range(8):
                        h, t = m // 2, m % 2
                        i = nc.tensor.matmul(PS[:, bb[m // 4], (m % 4) * P:(m % 4 + 1) * P],
                                             k[:, h * T + t * P:h * T + (t + 1) * P],
                                             q[:, h * T + t * P:h * T + (t + 1) * P], start=True, stop=True)
                    i.then_inc(S("hg_sc"), 1)
            pe.wait_ge(S("hg_copied"), 13)
            pe.wait_ge(S("hg_qf"), 2)
            for h in range(4):
                for t in range(2):
                    out = PS[half(h % 2), 2, (h // 2) * T + t * P:(h // 2) * T + (t + 1) * P]
                    nc.tensor.matmul(out, HI[:, t, h * 64:h * 64 + 64], SC[:, (2 * h + t) * P:(2 * h + t + 1) * P],
                                     start=True, stop=False, skip_group_check=True)
                    for d in range(2):
                        for n in (2 * t, 2 * t + 1):
                            i = nc.tensor.matmul(PS[half(h % 2), 2, (h // 2) * T + n * 64:(h // 2) * T + n * 64 + 64],
                                                 SX[:, d, n, h * 64:h * 64 + 64],
                                                 QF[:, d, h * T + n * 64:h * T + n * 64 + 64],
                                                 start=False, stop=d == 1, skip_group_check=True)
            i.then_inc(S("hg_o"), 1)
            pe.wait_ge(S("hg_osq"), 1)
            nc.tensor.matmul(PS[:, 3, :], blk, SQO, start=True, stop=True).then_inc(S("hg_oss"), 1)
            out_units_pe(pe, U_OUT2, "o2", 4)
            norm_pe(pe, 6)
            ffn_pe(pe, 2, "ffn2")
            norm_pe(pe, 7)

        @block.scalar
        def _(act):
            act.dma_start(par, A["par"]).then_inc(S("par_loaded"), 16)
            act.dma_start(cst, A["cst"]).then_inc(S("cst_loaded"), 16)
            act.dma_start(csb, A["csb"]).then_inc(S("csb_loaded"), 16)
            act.dma_start(cst2, A["cst2"]).then_inc(S("cst2_loaded"), 16)
            act.wait_ge(S("memset_done"), 4)
            act.wait_ge(S("par_loaded"), 16)
            nc.scalar.activation(CSL.rearrange("p k c -> p (k c)"), prm("c2", 0, 16), ACT.Silu).then_inc(S("csl_done"), 1)
            norm_act(act, 0)
            for u in range(3):
                hi(act, u)
            act.wait_ge(S("glr_mm"), 1)
            nc.scalar.activation(GLR, PS[0:16, 3, 0:T], ACT.Copy).then_inc(S("glr_done"), 1)
            with act.Fori(0, 2) as i:
                for q in range(6):
                    if q % 2 == 0:
                        act.wait_ge(S("unit_done"), i * 6 + (q + 1))
                        nc.scalar.activation(PROJ[:, bass.ds(i * 6 + q, 1), :].rearrange("p a n -> p (a n)"),
                                             PS[:, 4, :], ACT.Copy).then_inc(S("bank4_free"), 1)
                    w = q + 3
                    split_hi(act, i * 6 + w, w % SLOTS, w % RAW_SLOTS, i * 3 + (w // RAW_SLOTS + 1))
            act.wait_ge(S("gate_mm"), 1)
            for a in range(2):
                i = nc.scalar.activation(GE[:, a * T:(a + 1) * T], PS[:, 3, a * T:(a + 1) * T], ACT.Abs,
                                         bias=prm("bgate", a))
            i.then_inc(S("gate_read"), 1)
            act.wait_ge(S("gate_read"), 1)
            nc.scalar.activation(GE, GE, ACT.Exp, scale=-1.0).then_inc(S("gate_act"), 1)
            act.wait_ge(S("gate_act"), 1)
            nc.scalar.activation(GE, GE, ACT.Ln, bias=1.0).then_inc(S("gate_act"), 1)
            for j in range(4):
                if j == 0:
                    act.wait_ge(S("bank4_free"), 7)
                    act.wait_ge(S("bank5_free"), 7)
                nc.scalar.activation(SQF[:, j * 512:(j + 1) * 512], PROJ[:, 8 + j, :], ACT.Square)\
                    .then_inc(S("qk_sq"), 1)
            act.wait_ge(S("gla_diff"), 1)
            nc.scalar.activation(KEND, KEND, ACT.Exp, scale=1.0 / 16).then_inc(S("gla_exp"), 1)
            nc.scalar.activation(DEC, CUM.rearrange("p (m c) -> p m c", c=CHUNK)[:, :, CHUNK - 1], ACT.Exp,
                                 scale=1.0 / 16).then_inc(S("gla_exp"), 1)
            act.wait_ge(S("qk_ss"), 4)
            nc.scalar.activation(RSF, banks(0, 4), ACT.Ln, scale=1.0 / 64, bias=prm_eps).then_inc(S("qk_rs"), 1)
            act.wait_ge(S("qk_rs"), 1)
            nc.scalar.activation(RSF, RSF, ACT.Exp, scale=-0.5).then_inc(S("qk_rs"), 1)
            act.wait_ge(S("ktok_mm"), 1)
            nc.scalar.activation(KTOK, PS[:, 4, :], ACT.Copy).then_inc(S("ktok_done"), 1)
            nc.scalar.activation(RSG, PROJ[:, 4:6, :].rearrange("p a n -> p (a n)"), ACT.Exp, scale=-1.0)\
                .then_inc(S("r_exp"), 1)
            act.wait_ge(S("og_mm"), 1)
            nc.scalar.activation(OG, banks(2, 4), ACT.Copy, scale=CHUNK ** -0.5).then_inc(S("og_done"), 1)
            act.wait_ge(S("og_done"), 1)
            nc.scalar.activation(OR, OG, ACT.Square).then_inc(S("og_sq"), 1)
            act.wait_ge(S("og_ss"), 1)
            nc.scalar.activation(OR, banks(0, 2), ACT.Ln, scale=1.0 / P, bias=prm_eps).then_inc(S("og_rs"), 1)
            act.wait_ge(S("og_rs"), 1)
            nc.scalar.activation(OR, OR, ACT.Exp, scale=-0.5).then_inc(S("og_rs"), 1)

            def zps(g):
                b = 2 * (g % 2)
                return PS[:, b:b + 2, 0:384]

            for g in range(4):
                act.wait_ge(S("sb_z"), g + 1)
                if g:
                    act.wait_ge(S("sb_keep"), g)
                nc.scalar.activation(SBL, zps(g), ACT.Abs, scale=0.125).then_inc(S("sb_a"), 1)
                act.wait_ge(S("sb_a"), 3 * g + 1)
                nc.scalar.activation(SBL, SBL, ACT.Exp, scale=-1.0).then_inc(S("sb_a"), 1)
                act.wait_ge(S("sb_a"), 3 * g + 2)
                nc.scalar.activation(SBL, SBL, ACT.Ln, bias=1.0).then_inc(S("sb_a"), 1)
                act.wait_ge(S("sb_lz2"), g + 1)
                nc.scalar.activation(SBZ, SBZ, ACT.Exp).then_inc(S("sb_exp"), 1)
                act.wait_ge(S("sb_o"), g + 1)
                nc.scalar.activation(MIX[:, 4 + g, :], PS[:, 6, 0:T], ACT.Copy).then_inc(S("sb_o_read"), 1)

            def mix1_ready(act, j):
                if j < 2:
                    act.wait_ge(S("gla_out"), 1)
                    act.wait_ge(S("sb_o"), 4)
                else:
                    act.wait_ge(S("sb_o_read"), 2 * (j - 1))
            mix_split_act(act, 0, mix1_ready)
            for j in range(1, N_OUT):
                hi(act, U_OUT1 + j + 2)
            norm_act(act, 1)
            ffn_act(act, 0)
            norm_act(act, 2)
            for j in range(N_PW1):
                hi(act, U_PW1 + j + 2)
                act.wait_ge(S("unit_done"), U_PW1 + j + 1)
                if j >= 2:
                    act.wait_ge(S("cu_done"), j - 1)
                nc.scalar.activation(SIG[:, j % 2, :], PS[:, 4 + j % 2, T:2 * T], ACT.Sigmoid,
                                     bias=prm("bpw1", 8 + j)).then_inc(S("sig_done"), 1)
            act.wait_ge(S("ln_sum"), 1)
            nc.scalar.activation(MU, PS[:, 6, 0:T], ACT.Copy, scale=1.0 / D).then_inc(S("ln_mu"), 1)
            for j in range(2):
                act.wait_ge(S("ln_d"), j + 1)
                nc.scalar.activation(SQ[:, 4 * j:4 * j + 4, :], HN[:, 4 * j:4 * j + 4, :], ACT.Square)\
                    .then_inc(S("ln_sq"), 1)
            act.wait_ge(S("ln_ss"), 1)
            nc.scalar.activation(RS, PS[:, 6, T:2 * T], ACT.Ln, scale=1.0 / D, bias=prm_eps).then_inc(S("ln_a"), 1)
            act.wait_ge(S("ln_a"), 1)
            nc.scalar.activation(RS, RS, ACT.Exp, scale=-0.5).then_inc(S("ln_a"), 1)
            for j in range(4):
                for k in (2 * j, 2 * j + 1):
                    act.wait_ge(S("ln_n"), k + 1)
                    i = nc.scalar.activation(SQ[:, k, :], HN[:, k, :], ACT.Silu, bias=prm("lnb", k))
                i.then_inc(S("ln_silu"), 1)
                act.wait_ge(S("ln_silu"), j + 1)
                nc.scalar.activation(a_hi[:, 2 * j:2 * j + 2, 0, :], SQ[:, 2 * j:2 * j + 2, :], ACT.Copy)\
                    .then_inc(S("cv_hi"), 1)
            for j in range(N_OUT):
                hi(act, U_PW2 + j + 2)
            norm_act(act, 3)
            ffn_act(act, 1)
            act.wait_ge(S("unit_done"), U_FFN[1] + N_FFN)
            act.dma_start(mlw, A["mlw"]).then_inc(S("mlw_loaded"), 16)
            norm_act(act, 4, lambda k: MOD[:, k, 1:2])
            norm_act(act, 5, lambda k: MOD[:, k, 0:1])
            for j in range(N_IN2):
                u = U_IN2 + j
                hi(act, u + 2)
                act.wait_ge(S("unit_done"), u + 1)
                if j == 0:
                    nc.scalar.activation(CKV, PS[:, 0:2, :], ACT.Copy).then_inc(S("in2_read"), 1)
                elif j < 5:
                    b, dd, hh = 2 * (j % 2), (j - 1) // 2, 2 * ((j - 1) % 2)
                    for e in range(2):
                        i = nc.scalar.activation(ZF[:, dd, :, hh + e, :],
                                                 PS[:, b + e, :].rearrange("p (s t) -> p s t", s=2), ACT.Copy)
                    i.then_inc(S("in2_read"), 1)
                elif j == 5:
                    nc.scalar.activation(HI.rearrange("p a n -> p (a n)"), banks(2, 4), ACT.Copy)\
                        .then_inc(S("in2_read"), 1)
                else:
                    b = 4 + (j - 6) % 2
                    nc.scalar.activation(XO[:, 2 * (j - 6):2 * (j - 6) + 2, :].rearrange("p a n -> p (a n)"),
                                         PS[:, b, :], ACT.Copy).then_inc(S("in2_read"), 1)
            act.wait_ge(S("fn_mm"), 1)
            nc.scalar.activation(FC, banks(0, 2), ACT.Copy).then_inc(S("fc_done"), 1)
            act.wait_ge(S("fn_mm"), 2)
            nc.scalar.activation(FM.rearrange("p k t -> p (k t)"), PS[:, 2, :], ACT.Copy, scale=1.0 / 128)\
                .then_inc(S("fm_done"), 1)
            act.wait_ge(S("in2_read"), 11)
            nc.scalar.activation(SQ2[:, 0:512], XO[:, 0:2, :].rearrange("p k t -> p (k t)"), ACT.Square)
            nc.scalar.activation(SQ2[:, 512:1024], CKV[:, 0, :], ACT.Square).then_inc(S("ml_sq"), 1)
            act.wait_ge(S("fn_mm"), 3)
            nc.scalar.activation(MIX[:, 6:8, :].rearrange("p k t -> p (k t)"), PS[:, 3, :], ACT.Copy)\
                .then_inc(S("fn_read"), 3)
            act.wait_ge(S("ml_ss"), 1)
            nc.scalar.activation(RS2[:, 0:T], PS[:, 4, 0:T], ACT.Ln, scale=1.0 / 256, bias=prm_eps)
            nc.scalar.activation(RS2[:, 512:1024], PS[:, 5, :], ACT.Ln, scale=1.0 / 128, bias=prm_eps)\
                .then_inc(S("ml_ln"), 1)
            act.wait_ge(S("ml_ln"), 1)
            nc.scalar.activation(RS2[:, 0:T], RS2[:, 0:T], ACT.Exp, scale=-0.5)
            nc.scalar.activation(RS2[:, 512:1024], RS2[:, 512:1024], ACT.Exp, scale=-0.5).then_inc(S("ml_rs"), 1)
            act.wait_ge(S("ml_q"), 1)
            nc.scalar.activation(QP, PS[:, 2, :], ACT.Copy).then_inc(S("ml_q_read"), 1)
            nc.scalar.activation(QN.rearrange("p h t -> p (h t)"), banks(0, 2), ACT.Copy).then_inc(S("ml_q_read"), 1)
            for h in range(4):
                act.wait_ge(S("ml_k"), h + 1)
                nc.scalar.activation(KN[:, h, :], PS[:, (4, 5, 0, 1)[h], :], ACT.Copy).then_inc(S("ml_k_read"), 1)
            for t in range(4):
                act.wait_ge(S("ml_v"), t + 1)
                nc.scalar.activation(VT[:, t, :], PS[:, (2, 4, 5, 0)[t], :], ACT.Copy).then_inc(S("ml_v_read"), 1)
            scale = 192 ** -0.5

            def ml_exp(i):
                act.wait_ge(S("ml_max"), i + 1)
                nc.scalar.activation(MXS[:, i:i + 1], MXS[:, i:i + 1], ACT.Copy, scale=-scale).then_inc(S("ml_neg"), 1)
                act.wait_ge(S("ml_neg"), i + 1)
                if i >= 2:
                    act.wait_ge(S("ml_tr"), i - 1)
                nc.scalar.activation(PR[:, i % 2, :], PS[:, (1, 3)[i % 2], :], ACT.Exp, scale=scale,
                                     bias=MXS[:, i:i + 1], accum_out=MXS[:, 8 + i:9 + i]).then_inc(S("ml_exp"), 1)

            ml_exp(0)
            for i in range(8):
                if i < 7:
                    ml_exp(i + 1)
                act.wait_ge(S("ml_tr"), i + 1)
                if i >= 2:
                    act.wait_ge(S("ml_o"), i - 1)
                nc.scalar.activation(PT[:, i % 2, :], PS[:, 4 + i % 2, :], ACT.Copy).then_inc(S("ml_pt"), 1)
            for j in range(2):
                act.wait_ge(S("ml_o"), 8)
                nc.scalar.activation(OA[:, j * 512:(j + 1) * 512], PS[:, (0, 2)[j], :], ACT.Copy)\
                    .then_inc(S("ml_o_read"), 1)

            act.wait_ge(S("ml_o_read"), 2)
            nc.scalar.activation(QQ, XO[:, 2:6, :].rearrange("p k t -> p (k t)"), ACT.Exp, scale=-1.0)\
                .then_inc(S("hg_qe"), 1)
            for d in range(2):
                z = ZF[:, d].rearrange("p s h t -> p (s h t)")
                g = GG.rearrange("p s h t -> p (s h t)")
                kk = KK.rearrange("p s h t -> p (s h t)")
                if d == 1:
                    act.wait_ge(S("hg_copied"), 6)
                nc.scalar.activation(g, z, ACT.Abs).then_inc(S("hg_a"), 1)
                act.wait_ge(S("hg_a"), 3 * d + 1)
                nc.scalar.activation(g, g, ACT.Exp, scale=-1.0).then_inc(S("hg_a"), 1)
                act.wait_ge(S("hg_a"), 3 * d + 2)
                nc.scalar.activation(g, g, ACT.Ln, bias=1.0).then_inc(S("hg_a"), 1)
                act.wait_ge(S("hg_gz"), d + 1)
                nc.scalar.activation(kk, kk, ACT.Exp).then_inc(S("hg_k"), 1)
                act.wait_ge(S("hg_w"), d + 1)
                nc.scalar.activation(z, z if d == 0 else g, ACT.Exp).then_inc(S("hg_we"), 1)
                nc.scalar.activation(AD[:, d, :],
                                     CC.rearrange("p s h (n c) -> p (s h n) c", c=CHUNK)[:, :, CHUNK - 1], ACT.Exp)\
                    .then_inc(S("hg_ad"), 1)
                if d == 1:
                    act.wait_ge(S("hg_qx"), 1)
                nc.scalar.activation(QF[:, d, :], CC[:, 0].rearrange("p h t -> p (h t)") if d == 0 else QF[:, 1, :],
                                     ACT.Exp).then_inc(S("hg_qxe"), 1)
                for t in range(4):
                    act.wait_ge(S("hg_tr"), 4 * d + t + 1)
                    nc.scalar.activation(KWT[:, t].rearrange("p h k -> p (h k)"), PS[:, 4 + t % 2, :], ACT.Copy)\
                        .then_inc(S("hg_kwt"), 1)
                for l in range(6):
                    act.wait_ge(S("hg_e"), 6 * d + l + 1)
                    nc.scalar.activation(EX[:, l % 2, :], EX[:, l % 2, :], ACT.Exp).then_inc(S("hg_ee"), 1)
            act.wait_ge(S("hg_o"), 1)
            nc.scalar.activation(OH, PS[:, 2, :], ACT.Copy).then_inc(S("hg_r"), 1)
            act.wait_ge(S("hg_r"), 1)
            nc.scalar.activation(SQO, OH, ACT.Square).then_inc(S("hg_osq"), 1)
            nc.scalar.activation(ZG, XO[:, 6:8, :].rearrange("p k t -> p (k t)"), ACT.Exp, scale=-1.0)\
                .then_inc(S("hg_ze"), 1)
            act.wait_ge(S("hg_oss"), 1)
            nc.scalar.activation(RSO, PS[:, 3, :], ACT.Ln, scale=1.0 / 64, bias=prm_eps).then_inc(S("hg_r"), 1)
            act.wait_ge(S("hg_r"), 2)
            nc.scalar.activation(RSO, RSO, ACT.Exp, scale=-0.5).then_inc(S("hg_r"), 1)

            def mix2_ready(act, j):
                if j == 0:
                    act.wait_ge(S("hg_out"), 1)
            mix_split_act(act, 1, mix2_ready)
            for j in range(N_OUT):
                hi(act, U_OUT2 + j + 2)
            norm_act(act, 6, lambda k: MOD[:, 24 + k, 0:1])
            ffn_act(act, 2)
            norm_act(act, 7, split=False)

        @block.vector
        def _(dve):
            dve.memset(zero, 0.0).then_inc(S("memset_done"), 1)
            dve.memset(epsc, EPS).then_inc(S("memset_done"), 1)
            dve.memset(tick, 0.0).then_inc(S("memset_done"), 1)
            dve.memset(RESET, 1.0).then_inc(S("memset_done"), 1)
            dve.wait_ge(S("memset_done"), 4)
            dve.memset(RESET.rearrange("p (m c) -> p m c", c=CHUNK)[:, :, 0:1], 0.0).then_inc(S("memset_done"), 1)
            dve.wait_ge(S("memset_done"), 5)
            dve.memset(tick[:, 1:2], 0.0).then_inc(S("bank4_free"), 1)
            dve.memset(tick[:, 0:1], 0.0).then_inc(S("bank5_free"), 1)
            dve.wait_ge(S("par_loaded"), 16)
            norm_dve(dve, 0, lambda k: prm("mixn0", k))
            for u in range(3):
                lo(dve, u)
            with dve.Fori(0, 2) as i:
                for q in range(6):
                    if q % 2 == 1:
                        dve.wait_ge(S("unit_done"), i * 6 + (q + 1))
                        dve.tensor_copy(PROJ[:, bass.ds(i * 6 + q, 1), :].rearrange("p a n -> p (a n)"),
                                        PS[:, 5, :]).then_inc(S("bank5_free"), 1)
                    w = q + 3
                    split_lo(dve, i * 6 + w, w % SLOTS, w % RAW_SLOTS)
            dve.wait_ge(S("gate_mm"), 1)
            dve.wait_ge(S("gate_read"), 1)
            for a in range(2):
                dve.tensor_scalar(LA[:, a * T:(a + 1) * T], PS[:, 3, a * T:(a + 1) * T], prm("bgate", a), 0.0,
                                  ALU.add, ALU.min).then_inc(S("gate_read"), 1)
            dve.wait_ge(S("gate_read"), 3)
            dve.wait_ge(S("gate_act"), 2)
            dve.tensor_tensor(LA, LA, GE, ALU.subtract).then_inc(S("gla_dve"), 1)
            dve.wait_ge(S("gla_dve"), 1)
            dve.tensor_tensor_scan(CUM, RESET, LA, 0.0, ALU.mult, ALU.add).then_inc(S("gla_dve"), 1)
            dve.wait_ge(S("gla_dve"), 2)
            cum = CUM.rearrange("p (m c) -> p m c", c=CHUNK)
            dve.tensor_tensor(KEND.rearrange("p (m c) -> p m c", c=CHUNK),
                              cum[:, :, CHUNK - 1:CHUNK].to_broadcast([P, 8, CHUNK]), cum, ALU.subtract)\
                .then_inc(S("gla_diff"), 1)
            dve.wait_ge(S("gla_exp"), 1)
            dve.wait_ge(S("bank4_free"), 7)
            dve.tensor_tensor(KEND, KEND, PROJ[:, 2, :], ALU.mult).then_inc(S("kend_done"), 1)
            dve.wait_ge(S("qk_rs"), 2)
            for j, g in enumerate(("sbk", "sbq")):
                dve.scalar_tensor_tensor(QKN[:, j * 1024:(j + 1) * 1024],
                                         PROJ[:, 8 + 2 * j:10 + 2 * j, :].rearrange("p a n -> p (a n)"), prm(g),
                                         RSF[:, j * 1024:(j + 1) * 1024], ALU.mult, ALU.mult)\
                    .then_inc(S("qkn_done"), 1)
            dve.wait_ge(S("upd_mm"), 1)
            dve.wait_ge(S("gla_exp"), 2)
            for n in range(4):
                for a in range(2):
                    U = PS[:, n % 2, ((n // 2) * 2 + a) * P:((n // 2) * 2 + a + 1) * P]
                    if n == 0:
                        dve.tensor_copy(ST[:, 0, a, :], U).then_inc(S("state_done"), 1)
                    else:
                        dve.wait_ge(S("state_done"), 2 * n + a - 1)
                        dve.scalar_tensor_tensor(ST[:, n, a, :], ST[:, n - 1, a, :], DEC[:, a * 4 + n:a * 4 + n + 1], U,
                                                 ALU.mult, ALU.add).then_inc(S("state_done"), 1)
            dve.wait_ge(S("r_exp"), 1)
            dve.tensor_scalar(RSG, RSG, 1.0, None, ALU.add).then_inc(S("r_dve"), 1)
            dve.wait_ge(S("r_dve"), 1)
            dve.reciprocal(RSG, RSG).then_inc(S("r_dve"), 1)
            dve.wait_ge(S("r_dve"), 2)
            dve.tensor_tensor(RSG, RSG, PROJ[:, 4:6, :].rearrange("p a n -> p (a n)"), ALU.mult).then_inc(S("r_dve"), 1)
            dve.wait_ge(S("og_rs"), 2)
            dve.scalar_tensor_tensor(OG, OG, prm("glan"), OR, ALU.mult, ALU.mult).then_inc(S("r_dve"), 1)
            dve.wait_ge(S("r_dve"), 4)
            og = OG.rearrange("p (e a t) -> p a e t", e=2, a=2)
            mx = MIX[:, 0:4, :].rearrange("p (a e) t -> p a e t", a=2)
            rg = RSG.rearrange("p (a e t) -> p a e t", a=2, e=2)
            for a in range(2):
                i = dve.tensor_tensor(mx[:, a], og[:, a], rg[:, a], ALU.mult)
            i.then_inc(S("gla_out"), 1)
            dve.wait_ge(S("csb_loaded"), 16)
            mb = sbmask.unsqueeze(1).to_broadcast([P, 2, 384])
            for g in range(4):
                b = 2 * (g % 2)
                z = PS[:, b:b + 2, 0:384]
                dve.wait_ge(S("sb_a"), 3 * g + 3)
                dve.tensor_scalar(SBK, z, 0.125, 0.0, ALU.mult, ALU.max).then_inc(S("sb_v"), 1)
                dve.wait_ge(S("sb_v"), 3 * g + 1)
                dve.scalar_tensor_tensor(SBK, SBK, -1.0, SBL, ALU.mult, ALU.subtract).then_inc(S("sb_v"), 1)
                dve.wait_ge(S("sb_v"), 3 * g + 2)
                if g:
                    dve.wait_ge(S("sb_o"), g)
                dve.tensor_tensor(SBM, SBK, mb, ALU.mult).then_inc(S("sb_keep"), 1)
                dve.scalar_tensor_tensor(SBZ, z, 0.125, SBK, ALU.mult, ALU.add).then_inc(S("sb_v"), 1)
                dve.wait_ge(S("sb_v"), 3 * g + 3)
                dve.wait_ge(S("sb_between"), g + 1)
                dve.tensor_tensor(SBZ, SBZ, PS[:, 4:6, 0:384], ALU.add).then_inc(S("sb_lz2"), 1)
                dve.wait_ge(S("sb_exp"), g + 1)
                dve.tensor_tensor(SBZ, SBZ, mb, ALU.mult).then_inc(S("sb_w"), 1)
            mix_split_dve(dve, 0)

            def residual_units(u0, add):
                for j in range(N_OUT):
                    if not (u0 == U_OUT1 and j == 0):
                        lo(dve, u0 + j + 2)
                    dve.wait_ge(S("unit_done"), u0 + j + 1)
                    add(j)

            def plain(j):
                ks = slice(2 * j, 2 * j + 2)
                dve.tensor_tensor(X[:, ks, :], X[:, ks, :], PS[:, 4 + j % 2, :].rearrange("p (k t) -> p k t", k=2),
                                  ALU.add).then_inc(S("x_updated"), 1)

            residual_units(U_OUT1, plain)
            norm_dve(dve, 1, lambda k: prm("ffnn0", k))
            ffn_dve(dve, 0)
            norm_dve(dve, 2, lambda k: prm("mixn1", k))
            dve.memset(CU[:, :, 0:TAPS - 1], 0.0).then_inc(S("cu_zero"), 1)
            dve.wait_ge(S("cu_zero"), 1)
            for p in range(KT // 2):
                for k in (2 * p, 2 * p + 1):
                    lo(dve, U_PW1 + k + 2)
                    dve.wait_ge(S("sig_done"), k + 1)
                    dve.scalar_tensor_tensor(CU[:, k, TAPS - 1:TAPS - 1 + T], PS[:, 4 + k % 2, 0:T], prm("bpw1", k),
                                             SIG[:, k % 2, :], ALU.add, ALU.mult).then_inc(S("cu_done"), 1)
                for j in range(TAPS):
                    for k in (2 * p, 2 * p + 1):
                        n = 2 * TAPS * p + 2 * j + k % 2
                        u, w = CU[:, k, j:j + T], prm("wdw", k * TAPS + j)
                        if j == 0:
                            dve.wait_ge(S("cu_done"), k + 1)
                            dve.tensor_scalar(HN[:, k, :], u, w, prm("bdw", k), ALU.mult, ALU.add)\
                                .then_inc(S("tap_done"), 1)
                        else:
                            dve.wait_ge(S("tap_done"), n - 1 - 2 * p)
                            i = dve.scalar_tensor_tensor(HN[:, k, :], u, w, HN[:, k, :], ALU.mult, ALU.add)
                            i.then_inc(S("tap_done") if j < TAPS - 1 else S("cv_done"), 1)
            dve.wait_ge(S("ln_mu"), 1)
            for j in range(2):
                ks = slice(4 * j, 4 * j + 4)
                dve.tensor_tensor(HN[:, ks, :], HN[:, ks, :], MU.unsqueeze(1).to_broadcast([P, 4, T]), ALU.subtract)\
                    .then_inc(S("ln_d"), 1)
            dve.wait_ge(S("ln_a"), 2)
            for k in range(KT):
                dve.scalar_tensor_tensor(HN[:, k, :], HN[:, k, :], prm("lng", k), RS, ALU.mult, ALU.mult)\
                    .then_inc(S("ln_n"), 1)
            for j in range(4):
                ks = slice(2 * j, 2 * j + 2)
                dve.wait_ge(S("cv_hi"), j + 1)
                dve.tensor_tensor(a_lo[:, ks, 0, :], SQ[:, ks, :], a_hi[:, ks, 0, :].bitcast(F32), ALU.subtract)\
                    .then_inc(S("act_lo"), 1)

            def biased(j):
                for e in range(2):
                    k = 2 * j + e
                    i = dve.scalar_tensor_tensor(X[:, k, :], PS[:, 4 + j % 2, e * T:(e + 1) * T], prm("bpw2", k),
                                                 X[:, k, :], ALU.add, ALU.add)
                i.then_inc(S("x_updated"), 1)

            residual_units(U_PW2, biased)
            norm_dve(dve, 3, lambda k: prm("ffnn1", k))
            dve.wait_ge(S("mod_done"), MODB)
            dve.tensor_tensor(MOD, PS[:, 7, 0:96].rearrange("p (n c) -> p n c", c=2),
                              prm("bmod", 0, 48).unsqueeze(2).to_broadcast([P, 48, 2]), ALU.add)\
                .then_inc(S("modv"), 1)
            dve.wait_ge(S("modv"), 1)
            for n, (sc, c, g) in enumerate(((8, 0, "n1g"), (8, 1, "n1g"), (32, 0, "n2g"))):
                dve.scalar_tensor_tensor(GSC[:, n, :], MOD[:, sc:sc + 8, c], 1.0, prm(g, 0, 8), ALU.add, ALU.mult)\
                    .then_inc(S("modv"), 1)
            ffn_dve(dve, 1)
            dve.wait_ge(S("modv"), 4)
            norm_dve(dve, 4, lambda k: GSC[:, 1, k:k + 1], lambda k: MOD[:, k, 1:2])
            norm_dve(dve, 5, lambda k: GSC[:, 0, k:k + 1], lambda k: MOD[:, k, 0:1])
            for j in range(N_IN2):
                lo(dve, U_IN2 + j + 2)
            dve.wait_ge(S("cst2_loaded"), 16)
            dve.wait_ge(S("ml_rs"), 1)
            for k in range(2):
                i = dve.scalar_tensor_tensor(CQN[:, k, :], XO[:, k, :], prm("qng", k), RS2[:, 0:T], ALU.mult, ALU.mult)
            i.then_inc(S("ml_n"), 1)
            dve.scalar_tensor_tensor(CKN, CKV[:, 0, :], prm("kvg"), RS2[:, 512:1024], ALU.mult, ALU.mult)\
                .then_inc(S("ml_n"), 1)
            cos2 = c2("cos").unsqueeze(1).to_broadcast([P, 2, T])
            sin2 = c2("sin").unsqueeze(1).to_broadcast([P, 2, T])
            v2 = lambda ap: ap.rearrange("p (a t) -> p a t", a=2)
            dve.wait_ge(S("ml_q_read"), 1)
            dve.wait_ge(S("ml_rot"), 2)
            dve.tensor_tensor(v2(QR), v2(PS[:, 3, :]), sin2, ALU.mult).then_inc(S("rope"), 1)
            dve.tensor_tensor(v2(QP), v2(QP), cos2, ALU.mult).then_inc(S("rope"), 1)
            dve.tensor_tensor(KPE[:, 0:T], PS[:, 6, 0:T], c2("sin"), ALU.mult).then_inc(S("rope"), 1)
            dve.tensor_tensor(KPE[:, T:2 * T], CKV[:, 1, 0:T], c2("cos"), ALU.mult).then_inc(S("rope"), 1)
            dve.wait_ge(S("rope"), 4)
            dve.tensor_tensor(QR, QR, QP, ALU.add).then_inc(S("rope_done"), 1)
            dve.tensor_tensor(KPE[:, 0:T], KPE[:, 0:T], KPE[:, T:2 * T], ALU.add).then_inc(S("rope"), 1)
            dve.wait_ge(S("rope"), 5)
            dve.tensor_copy(KPE[:, T:2 * T], CKV[:, 1, T:2 * T]).then_inc(S("rope_done"), 1)

            def ml_max(i):
                dve.wait_ge(S("ml_s"), i + 1)
                dve.reduce_max(MXS[:, i:i + 1], PS[:, (1, 3)[i % 2], :], AX.X).then_inc(S("ml_max"), 1)

            ml_max(0)
            for i in range(8):
                if i < 7:
                    ml_max(i + 1)
                dve.wait_ge(S("ml_exp"), i + 1)
                dve.reciprocal(MXS[:, 16 + i:17 + i], MXS[:, 8 + i:9 + i]).then_inc(S("ml_rc"), 1)
                dve.wait_ge(S("ml_rc"), i + 1)
                dve.tensor_scalar(PR[:, i % 2, :], PR[:, i % 2, :], MXS[:, 16 + i:17 + i], None, ALU.mult)\
                    .then_inc(S("ml_p"), 1)

            dve.memset(RST64, 1.0).then_inc(S("hg_reset"), 1)
            dve.wait_ge(S("hg_reset"), 1)
            dve.memset(RST64.rearrange("p (m c) -> p m c", c=CHUNK)[:, :, 0:1], 0.0).then_inc(S("hg_reset"), 1)
            dve.wait_ge(S("hg_reset"), 2)
            dve.wait_ge(S("hg_qe"), 1)
            dve.tensor_scalar(QQ, QQ, 1.0, None, ALU.add).then_inc(S("hg_q"), 1)
            dve.wait_ge(S("hg_q"), 1)
            dve.reciprocal(QQ, QQ).then_inc(S("hg_q"), 1)
            dve.wait_ge(S("hg_q"), 2)
            dve.tensor_tensor(QQ, QQ, XO[:, 2:6, :].rearrange("p k t -> p (k t)"), ALU.mult).then_inc(S("hg_q"), 1)
            ch = lambda ap: ap.rearrange("p s h (n c) -> p (s h n) c", c=CHUNK)
            fl = lambda ap: ap.rearrange("p s h t -> p (s h t)")
            for d in range(2):
                z, g, kk, cc = ZF[:, d], GG, KK, CC
                dve.wait_ge(S("hg_a"), 3 * d + 3)
                dve.scalar_tensor_tensor(fl(g), fl(z), 0.0, fl(g), ALU.min, ALU.subtract).then_inc(S("hg_v"), 1)
                dve.wait_ge(S("hg_v"), 2 * d + 1)
                dve.tensor_tensor(fl(kk), fl(g), fl(z), ALU.subtract).then_inc(S("hg_gz"), 1)
                for s in range(2):
                    for h in range(4):
                        i = dve.tensor_tensor_scan(cc[:, s, h, :], RST64, g[:, s, h, :], 0.0, ALU.mult, ALU.add)
                i.then_inc(S("hg_v"), 1)
                dve.wait_ge(S("hg_v"), 2 * d + 2)
                dve.wait_ge(S("hg_gz"), d + 1)
                end = ch(cc)[:, :, CHUNK - 1:CHUNK].to_broadcast([P, 32, CHUNK])
                endx = ch(cc)[:, 0:16, CHUNK - 1:CHUNK].to_broadcast([P, 16, CHUNK])
                if d == 0:
                    dve.tensor_tensor(ch(z), end, ch(cc), ALU.subtract).then_inc(S("hg_w"), 1)
                    X_ = cc
                else:
                    dve.tensor_tensor(fl(g), fl(cc), fl(g), ALU.subtract).then_inc(S("hg_w"), 1)
                    dve.wait_ge(S("hg_w"), 2)
                    dve.tensor_tensor(QF[:, 1, :].rearrange("p (m c) -> p m c", c=CHUNK), endx, ch(g)[:, 0:16, :],
                                      ALU.subtract).then_inc(S("hg_qx"), 1)
                    X_ = g
                dve.wait_ge(S("hg_k"), d + 1)
                dve.wait_ge(S("hg_we"), d + 1)
                dve.tensor_tensor(fl(z), fl(z), fl(kk), ALU.mult).then_inc(S("hg_kw"), 1)
                if d == 0:
                    dve.tensor_copy(KS, fl(kk)[:, 0:1024]).then_inc(S("hg_ks"), 1)
                else:
                    dve.tensor_tensor(KS, KS, fl(kk)[:, 0:1024], ALU.add).then_inc(S("hg_ks"), 1)
                dve.wait_ge(S("hg_qxe"), d + 1)
                dve.wait_ge(S("hg_q"), 3)
                dve.tensor_tensor(QF[:, d, :], QF[:, d, :], QQ, ALU.mult).then_inc(S("hg_qf"), 1)
                order = [(1, n) for n in range(4)] + [(0, n) for n in range(4)]
                if d == 1:
                    order = [(s, 3 - n) for s, n in order]
                dve.wait_ge(S("hg_ad"), d + 1)
                prev = None
                ad = AD[:, d, :].rearrange("p (s h n) -> p s h n", s=2, h=4)
                for c, (s, n) in enumerate(order):
                    upd = PS[:, 2 * (1 - s) + n % 2, (n // 2) * T:(n // 2) * T + T]
                    if c < 7:
                        s2, n2 = order[c + 1]
                        dst = SX[:, d, n2, :] if s2 == 0 else (STT if c % 2 == 0 else STU)
                        dve.wait_ge(S("hg_upd"), 2 * d + (2 - s))
                        if prev is None:
                            dve.tensor_copy(dst, upd).then_inc(S("hg_state"), 1)
                        else:
                            dve.wait_ge(S("hg_state"), 7 * d + c)
                            v = lambda ap: ap.rearrange("p (h v) -> p h v", h=4)
                            dve.tensor_tensor(v(dst), v(prev), ad[:, s, :, n:n + 1].to_broadcast([P, 4, 64]), ALU.mult)\
                                .then_inc(S("hg_dec"), 1)
                            dve.wait_ge(S("hg_dec"), 6 * d + c)
                            dve.tensor_tensor(dst, dst, upd, ALU.add).then_inc(S("hg_state"), 1)
                        prev = dst
                if d == 0:
                    dve.wait_ge(S("hg_upd"), 2)
                    for buf in (QM0, KM0):
                        dve.memset(buf, 0.0).then_inc(S("hg_zero"), 1)
                    dve.memset(SC, 0.0).then_inc(S("hg_zero"), 1)
                dve.wait_ge(S("hg_upd"), 2 * d + 2)
                if d == 1:
                    for buf in (QM0, KM0):
                        dve.memset(buf, 0.0).then_inc(S("hg_zero"), 1)
                for buf in (QMd(d), KMd(d)):
                    dve.memset(buf, 0.0).then_inc(S("hg_zero"), 1)
                dve.wait_ge(S("hg_zero"), 5 if d == 0 else 9)
                xs = X_[:, 0].rearrange("p h t -> p (h t)")
                xk = kk[:, 0].rearrange("p h t -> p (h t)")

                def pair_exponents(l):
                    m = LEVELS[l]
                    w = lambda ap: ap.rearrange("p (a b m) -> p a b m", b=2, m=m)
                    a = 512 // m
                    ref = w(xs)[:, :, 0, m - 1:m] if d == 0 else w(xs)[:, :, 1, 0:1]
                    ref = ref.to_broadcast([P, a, m])
                    e = w(EX[:, l % 2, :])
                    if l >= 2:
                        dve.wait_ge(S("hg_pair"), 6 * d + l - 1)
                    dve.tensor_tensor(e[:, :, 1, :], w(xs)[:, :, 1, :], ref, ALU.subtract)
                    dve.tensor_tensor(e[:, :, 0, :], ref, w(xs)[:, :, 0, :], ALU.subtract).then_inc(S("hg_e"), 1)

                def pair_products(l):
                    m = LEVELS[l]
                    w = lambda ap: ap.rearrange("p (a b m) -> p a b m", b=2, m=m)
                    q, k = (QM0, KM0) if l % 2 == 0 else (QMd(d), KMd(d))
                    qs, ks_ = (1, 0) if d == 0 else (0, 1)
                    e = w(EX[:, l % 2, :])
                    dve.wait_ge(S("hg_ee"), 6 * d + l + 1)
                    if l >= 2:
                        dve.wait_ge(S("hg_sc"), 6 * d + l - 1)
                    dve.tensor_tensor(w(q)[:, :, qs, :], w(QQ)[:, :, qs, :], e[:, :, qs, :], ALU.mult)
                    dve.tensor_tensor(w(k)[:, :, ks_, :], w(xk)[:, :, ks_, :], e[:, :, ks_, :], ALU.mult)\
                        .then_inc(S("hg_pair"), 1)

                def pair_copy(l):
                    bb = 4 if l % 2 == 0 else 0
                    dve.wait_ge(S("hg_sc"), 6 * d + l + 1)
                    mi = 6 * d + l
                    mask = c2("lmask")[:, mi * P:(mi + 1) * P].bitcast(I32).unsqueeze(1).to_broadcast([P, 8, P])
                    if mi:
                        dve.wait_ge(S("hg_copied"), mi)
                    dve.copy_predicated(SC.rearrange("p (m t) -> p m t", m=8), mask,
                                        banks(bb, bb + 2).rearrange("p (m t) -> p m t", m=8))\
                        .then_inc(S("hg_copied"), 1)

                pair_exponents(0)
                for l in range(6):
                    if l < 5:
                        pair_exponents(l + 1)
                    pair_products(l)
                    if l:
                        pair_copy(l - 1)
                pair_copy(5)
                if d == 1:
                    pair_copy(6)
                else:
                    pass
            dve.wait_ge(S("hg_ze"), 1)
            dve.tensor_scalar(ZG, ZG, 1.0, None, ALU.add).then_inc(S("hg_f"), 1)
            dve.wait_ge(S("hg_f"), 1)
            dve.reciprocal(ZG, ZG).then_inc(S("hg_f"), 1)
            dve.wait_ge(S("hg_f"), 2)
            dve.tensor_tensor(ZG, ZG, XO[:, 6:8, :].rearrange("p k t -> p (k t)"), ALU.mult).then_inc(S("hg_f"), 1)
            dve.wait_ge(S("hg_r"), 3)
            for a in range(2):
                dve.scalar_tensor_tensor(OH[:, a * T:(a + 1) * T], OH[:, a * T:(a + 1) * T], prm("hgg", a),
                                         RSO[:, a * T:(a + 1) * T], ALU.mult, ALU.mult).then_inc(S("hg_f"), 1)
            dve.wait_ge(S("hg_f"), 5)
            dve.tensor_tensor(MIX[:, 4:6, :].rearrange("p k t -> p (k t)"), OH, ZG, ALU.mult).then_inc(S("hg_out"), 1)
            mix_split_dve(dve, 1)

            def gated(j):
                for e in range(2):
                    k = 2 * j + e
                    i = dve.scalar_tensor_tensor(X[:, k, :], PS[:, 4 + j % 2, e * T:(e + 1) * T], MOD[:, 16 + k, 0:1],
                                                 X[:, k, :], ALU.mult, ALU.add)
                i.then_inc(S("x_updated"), 1)

            residual_units(U_OUT2, gated)
            norm_dve(dve, 6, lambda k: GSC[:, 2, k:k + 1], lambda k: MOD[:, 24 + k, 0:1])
            ffn_dve(dve, 2, lambda k: MOD[:, 40 + k, 0:1])
            norm_dve(dve, 7, lambda k: prm("fing", k), split=False)

        @block.gpsimd
        def _(pool):
            for m in range(2):
                pool.dma_start(modraw[:, m, :], A["wmod"][m]).then_inc(S(f"mod_loaded{m}"), 16)
            with pool.Fori(0, MODB // 2 - 1) as i:
                for m in range(2):
                    pool.wait_ge(S("mod_done"), i * 2 + (m + 1))
                    pool.dma_start(modraw[:, m, :], A["wmod"][bass.ds(i * 2 + (2 + m), 1)].rearrange("a p n -> (a p) n"))\
                        .then_inc(S(f"mod_loaded{m}"), 16)
            pool.wait_ge(S("x_updated"), 4)
            pool.dma_start(CTX.rearrange("p k t -> p (k t)"), A["ctxT"]).then_inc(S("ctx_loaded"), 16)
    print("semaphores", len(sems))


def _tiles(a):
    k, n = a.shape
    return a.reshape(k // P, P, n // P, P).transpose(2, 0, 1, 3)


def _feature_units(blocks):
    b = np.stack(blocks)
    return b.reshape(-1, BLK, P, P).transpose(0, 2, 1, 3).reshape(-1, P, UNIT)


def _token_units(w):
    return w.reshape(KT, P, -1, 256).transpose(2, 1, 0, 3).reshape(-1, P, UNIT)


def _ffn_units(wg, wu, wd):
    g, u = _tiles(wg), _tiles(wu)
    d = wd.reshape(FT, P, KT, P).transpose(0, 2, 1, 3)
    gu = [_feature_units([g[f], u[f]])[0] for f in range(FT)]
    dn = [np.concatenate([d[2 * j], d[2 * j + 1]]).transpose(1, 0, 2).reshape(P, UNIT) for j in range(FT // 2)]
    out = [gu[0], gu[1]]
    for j in range(1, FT // 2):
        out += [gu[2 * j], gu[2 * j + 1], dn[j - 1]]
    return np.stack(out + [dn[-1]])


def _cols(a):
    return a.reshape(-1, P).T


def _constants():
    ones = np.ones((P, P), np.float32)
    blk = np.kron(np.eye(2, dtype=np.float32), np.ones((64, 64), np.float32))
    cst = np.concatenate([ones, blk, np.eye(P, dtype=np.float32)], 1)
    i = np.arange(P)
    after = (i[:, None] > i[None, :]).astype(np.float32)
    before = (i[:, None] < i[None, :]).astype(np.float32)
    csb = np.concatenate([after, before, ones, before], 1)
    masks = []
    for d in range(2):
        for m in LEVELS:
            pair, side = i // (2 * m), (i // m) % 2
            q, k = (1, 0) if d == 0 else (0, 1)
            masks.append((pair[:, None] == pair[None, :]) & (side[:, None] == k) & (side[None, :] == q))
    masks.append(np.eye(P, dtype=bool))
    lmask = np.concatenate([m.astype(np.float32) for m in masks], 1)
    f = np.arange(64)
    w = 2 * np.pi * np.outer(f, f) / 64
    e2 = np.eye(2)
    fd = np.concatenate([np.kron(e2, np.cos(w)), np.kron(e2, -np.sin(w))], 1).astype(np.float32)
    t = np.arange(T)
    w = 2 * np.pi * (np.outer(t, t) % T) / T
    ft = np.stack([np.cos(w), np.sin(w)]).reshape(2, 2, P, T).transpose(2, 0, 1, 3).reshape(P, -1).astype(np.float32)
    row, col = (np.arange(T) // 64).astype(np.float32), (np.arange(T) % 64).astype(np.float32)
    inv = (10000.0 ** (-np.arange(0, 32, 2, dtype=np.float32) / 32)).astype(np.float32)
    ar, ac = row[:, None] * inv, col[:, None] * inv
    ang = np.concatenate([ar, ar, ac, ac], 1).T
    cos, sin = (np.concatenate([g(ang)] * 2, 0).astype(np.float32) for g in (np.cos, np.sin))
    rot = np.zeros((64, 64), np.float32)
    for o in range(16):
        rot[16 + o, o] = -1.0
        rot[o, 16 + o] = 1.0
        rot[48 + o, 32 + o] = -1.0
        rot[32 + o, 48 + o] = 1.0
    rot = np.kron(np.eye(2, dtype=np.float32), rot)
    return cst, csb, np.concatenate([lmask, fd, ft, cos, sin, rot], 1)


def _lay_out(v):
    f = {k: np.asarray(a) for k, a in v.items()}
    w_in = f["hy_w_in"][0]
    c = np.cumsum([0, 256, 256, 512, 512, 16, 512, 512, 512])
    gq, gk, gv, gr, glr, sq, sk, sv = (w_in[:, a:b] for a, b in zip(c[:-1], c[1:]))
    fm = lambda *ws: _feature_units([t for w in ws for t in _tiles(w)])
    units = [_token_units(gv), fm(gk, gq, gr), _token_units(sv), fm(sk, sq), fm(f["hy_w_out"][0]),
             _ffn_units(f["ffn_w_gate"][0], f["ffn_w_up"][0], f["ffn_w_down"][0])]
    pw = _tiles(f["cv_w_pw1"][0])
    units += [_feature_units([t for j in range(8) for t in (pw[j], pw[8 + j])]), fm(f["cv_w_pw2"][0]),
              _ffn_units(f["ffn_w_gate"][1], f["ffn_w_up"][1], f["ffn_w_down"][1])]
    w2 = f["w_in_2"][0]
    c = np.cumsum([0, 256, 128, 64, 512, 512, 512, 256, 256, 256])
    cq, ckv, kr, hq, hff, hfb, hi, hg, fn = (w2[:, a:b] for a, b in zip(c[:-1], c[1:]))
    units += [fm(np.concatenate([ckv, kr, kr], 1), hff, hfb), _token_units(hi), fm(cq, hq, hg, fn),
              fm(f["w_out_2"][0])]
    gu = f["w_gate_up_2"][0]
    units += [_ffn_units(gu[:, :FT * P], gu[:, FT * P:], f["w_down_2"][0])]
    wstream = np.concatenate(units)
    cst, csb, cs2 = _constants()
    wf = f["w_fourier_2"][0].reshape(2, P, 256).transpose(1, 0, 2).reshape(P, 512)
    uq = f["w_uq_2"][0].reshape(256, 4, 192)
    uq = np.concatenate([uq[:, :, :128].reshape(256, 512), uq[:, :, 128:].reshape(256, 256)], 1)
    uq = uq.reshape(2, P, 768).transpose(1, 0, 2).reshape(P, 1536)
    ukv = f["w_ukv_2"][0].reshape(P, 4, 256)
    ukv = np.concatenate([ukv[:, :, :128].reshape(P, 512), ukv[:, :, 128:].reshape(P, 512)], 1)
    g2 = np.zeros((P, 256), np.float32)
    g2[:16] = f["hy_w_gate2"][0]
    cc = np.stack([_cols(f["c_2"][0]), _cols(f["c_ctx_2"])], 2).reshape(P, 16)
    par = np.concatenate([
        _cols(f["mix_norm"][0]), _cols(f["mix_norm"][1]), _cols(f["ffn_norm"][0]), _cols(f["ffn_norm"][1]),
        _cols(f["hy_gla_norm"][0]), _cols(np.tile(f["hy_sb_q_norm"][0], 2)), _cols(np.tile(f["hy_sb_k_norm"][0], 2)),
        _cols(f["hy_b_gate"][0]), _cols(f["cv_b_pw1"][0]), _cols(f["cv_b_dw"][0]), _cols(f["cv_ln_g"][0]),
        _cols(f["cv_ln_b"][0]), _cols(f["cv_b_pw2"][0]),
        f["cv_w_dw"][0].reshape(TAPS, KT, P).transpose(2, 1, 0).reshape(P, -1), cc, _cols(f["b_mod_2"][0]),
        _cols(f["norm1_g_2"][0]), _cols(f["norm2_g_2"][0]), _cols(f["q_norm_g_2"][0]), _cols(f["kv_norm_g_2"][0]),
        _cols(f["hg_norm_g_2"][0]), _cols(f["final_norm_g_2"]),
        glr.reshape(KT, P, 16).transpose(1, 0, 2).reshape(P, -1), g2], 1)
    act = lambda a: a[0].T.reshape(KT, P, T).transpose(1, 0, 2).reshape(P, KT * T)
    arrays = {
        "wstream": wstream, "wmod": _tiles(f["w_mod_2"][0]).transpose(0, 2, 1, 3).reshape(MODB, P, 1024),
        "xT": act(f["x"]), "ctxT": act(f["ctx_2"]), "par": par, "cst": cst, "csb": csb,
        "cst2": np.concatenate([cs2, wf], 1), "mlw": np.concatenate([uq, ukv], 1),
    }
    return {k: np.ascontiguousarray(a, dtype=np.float32) for k, a in arrays.items()}


def kernel(**inputs):
    import concourse.bacc as bacc
    from concourse import mybir
    from concourse.bass_utils import run_bass_kernel_spmd

    nc = bacc.Bacc("TRN2", target_bir_lowering=False, num_devices=1)
    arrays = _lay_out(inputs)
    A = {k: nc.dram_tensor(k, a.shape, mybir.dt.float32, kind="ExternalInput").ap() for k, a in arrays.items()}
    A["out"] = nc.dram_tensor("out", (P, KT * T), mybir.dt.float32, kind="ExternalOutput").ap()
    program(nc, A)
    r = run_bass_kernel_spmd(nc, [arrays], core_ids=[0])
    y = r.results[0]["out"]
    return np.ascontiguousarray(y.reshape(P, KT, T).transpose(1, 0, 2).reshape(D, T).T.reshape(1, T, D))
```

```python
from contextlib import ExitStack

import numpy as np

P = 128
D, T, KT = 1024, 256, 8
FT = 22
BLK = 16
UNIT = BLK * P
SLOTS, RAW_SLOTS = 3, 2
CHUNK = 64
TAPS = 31
EPS = 1e-6
N_IN1, N_OUT, N_PW1, N_IN2 = 12, 4, 8, 11
N_FFN = 33
MODB = 48
LEVELS = (32, 16, 8, 4, 2, 1)

U_IN1 = 0
U_OUT1 = U_IN1 + N_IN1
U_FFN = [U_OUT1 + N_OUT, 0, 0]
U_PW1 = U_FFN[0] + N_FFN
U_PW2 = U_PW1 + N_PW1
U_FFN[1] = U_PW2 + N_OUT
U_IN2 = U_FFN[1] + N_FFN
U_OUT2 = U_IN2 + N_IN2
U_FFN[2] = U_OUT2 + N_OUT
UNITS = U_FFN[2] + N_FFN

PAR = {}
_at = 0
for _name, _n in (("mixn0", 8), ("mixn1", 8), ("ffnn0", 8), ("ffnn1", 8), ("glan", 1), ("sbq", 1), ("sbk", 1),
                  ("bgate", 2), ("bpw1", 16), ("bdw", 8), ("lng", 8), ("lnb", 8), ("bpw2", 8), ("wdw", 8 * TAPS),
                  ("c2", 16), ("bmod", 48), ("n1g", 8), ("n2g", 8), ("qng", 2), ("kvg", 1), ("hgg", 2), ("fing", 8),
                  ("wglr", 8 * 16), ("wgate2", 256)):
    PAR[_name] = (_at, _n)
    _at += _n
N_PAR = _at

CST = {"ones": (0, 128), "blk": (128, 128), "ident": (256, 128)}
N_CST = 384
CSB = {"tri": (0, 128), "sbmask": (128, 384)}
N_CSB = 512
CS2 = {}
_at = 0
for _name, _n in (("lmask", 13 * 128), ("fd", 256), ("ft", 4 * 256), ("cos", 256), ("sin", 256), ("rot", 128),
                  ("wfou", 512)):
    CS2[_name] = (_at, _n)
    _at += _n
N_CS2 = _at
N_MLW = 2 * 768 + 1024


def program(nc, A):
    import concourse.bass as bass
    from concourse import mybir

    F32, F32R, BF16, I32 = mybir.dt.float32, mybir.dt.float32r, mybir.dt.bfloat16, mybir.dt.int32
    ACT, ALU, AX = mybir.ActivationFunctionType, mybir.AluOpType, mybir.AxisListType

    with ExitStack() as ctx:
        sems = {}

        def S(name):
            if name not in sems:
                sems[name] = ctx.enter_context(nc.semaphore(name))
            return sems[name]

        base = -(-nc.sbuf_base // 64) * 64

        def at(name, kib, cols, dt=F32, parts=P):
            return nc.alloc_sbuf_tensor_at(name, [parts, cols], dt, offset=base + int(kib * 1024))

        raw = at("raw", 0, RAW_SLOTS * UNIT)[:, :].rearrange("p (s n) -> p s n", s=RAW_SLOTS)
        w_hi = at("w_hi", 16, SLOTS * UNIT, F32R)[:, :].rearrange("p (s n) -> p s n", s=SLOTS)
        w_lo = at("w_lo", 40, SLOTS * UNIT, F32R)[:, :].rearrange("p (s n) -> p s n", s=SLOTS)
        X = at("X", 64, KT * T)[:, :].rearrange("p (k t) -> p k t", k=KT)
        a_hi = at("a_hi", 72, KT * 2 * T, F32R)[:, :].rearrange("p (k s t) -> p k s t", k=KT, s=2)
        a_lo = at("a_lo", 88, KT * 2 * T, F32R)[:, :].rearrange("p (k s t) -> p k s t", k=KT, s=2)
        SQ = at("SQ", 104, KT * T)[:, :].rearrange("p (k t) -> p k t", k=KT)
        HN = at("HN", 112, KT * T)[:, :].rearrange("p (k t) -> p k t", k=KT)
        h_hi = at("h_hi", 120, 4 * T, F32R)[:, :].rearrange("p (j f t) -> p j f t", j=2, f=2)
        h_lo = at("h_lo", 124, 4 * T, F32R)[:, :].rearrange("p (j f t) -> p j f t", j=2, f=2)
        GU = at("GU", 176, 4 * T)[:, :].rearrange("p (f t) -> p f t", f=2)
        SG = at("SG", 128, 2 * T)[:, :].rearrange("p (f t) -> p f t", f=2)
        HF = at("HF", 130, 2 * T)[:, :].rearrange("p (f t) -> p f t", f=2)
        RS = at("RS", 132, T)[:, :]
        RSC = at("RSC", 180, T)[:, :]
        par = at("par", 133, N_PAR)[:, :]
        cst = at("cst", 137, N_CST)[:, :]
        zero = at("zero", 138.5, 512, BF16)[:, :]
        modraw = at("modraw", 140, 2 * 1024)[:, :].rearrange("p (s n) -> p s n", s=2)
        MODACC = at("MODACC", 181, 4 * 1024)[:, :].rearrange("p (n f) -> p n f", n=4)
        MODTMP = at("MODTMP", 197, 1024)[:, :]
        MIX = at("MIX", 148, KT * T)[:, :].rearrange("p (k t) -> p k t", k=KT)
        cst2 = at("cst2", 190, N_CS2)[:, :]
        CSL = at("CSL", 206.5, 16)[:, :].rearrange("p (k c) -> p k c", c=2)
        MOD = at("MOD", 206.5625, 96)[:, :].rearrange("p (n c) -> p n c", c=2)
        GSC = at("GSC", 206.9375, 24)[:, :].rearrange("p (n k) -> p n k", k=8)

        def prm(name, i=0, n=1):
            return par[:, PAR[name][0] + i:PAR[name][0] + i + n]

        ones, blk, ident = (cst[:, CST[n][0]:CST[n][0] + 128] for n in ("ones", "blk", "ident"))

        def c2(name):
            return cst2[:, CS2[name][0]:CS2[name][0] + CS2[name][1]]

        PS = ctx.enter_context(nc.psum_tensor("PS", [P, 8, 512], F32))[:, :, :]

        def banks(a, b):
            return PS[:, a:b, :].rearrange("p b n -> p (b n)")

        PROJ = at("PROJ", 156, N_IN1 * 512)[:, :].rearrange("p (u n) -> p u n", u=N_IN1)
        QKN = at("QKN", 180, 4 * 512)[:, :]
        csb = at("csb", 188, N_CSB)[:, :]
        tri, sbmask = csb[:, 0:128], csb[:, 128:512]
        GLR = at("GLR", 131, T, F32, 16)[:, :]
        RESET = at("RESET", 120, 512)[:, :]
        LA = at("LA", 122, 512)[:, :]
        GE = at("GE", 124, 512)[:, :]
        CUM = at("CUM", 126, 512)[:, :]
        KEND = at("KEND", 128, 512)[:, :]
        KTOK = at("KTOK", 190, 512)[:, :]
        DEC = at("DEC", 192, 8)[:, :]
        ST = at("ST", 193, 1024)[:, :].rearrange("p (n a v) -> p n a v", n=4, a=2)
        OG = at("OG", 198, 1024)[:, :]
        OR = at("OR", 202, 1024)[:, :]
        RSG = at("RSG", 152, 1024)[:, :]
        SQF = at("SQF", 104, 2048)[:, :]
        RSF = at("RSF", 112, 2048)[:, :]
        SBZ = at("SBZ", 104, 3 * 768)[:, :].rearrange("p (g e n) -> p g e n", g=3, e=2)
        SBL = at("SBL", 114, 2 * 768)[:, :].rearrange("p (g e n) -> p g e n", g=2, e=2)
        SBK = at("SBK", 121, 768)[:, :].rearrange("p (e n) -> p e n", e=2)
        SBM = at("SBM", 125, 2 * 768)[:, :].rearrange("p (g e n) -> p g e n", g=2, e=2)
        PE_TILES = (5, 6, 7)
        RING = 24
        DG = at("DG", 120, RING * P)[:, :].rearrange("p (n m) -> p n m", n=RING)
        PADT = T + 32
        CU = at("CU", 156, KT * PADT)[:, :].rearrange("p (k t) -> p k t", k=KT)
        PWR = at("PWR", 177, 4 * T)[:, :].rearrange("p (f t) -> p f t", f=2)
        SIG = at("SIG", 166, 2 * T)[:, :].rearrange("p (f t) -> p f t", f=2)
        CTX = at("CTX", 168, KT * T)[:, :].rearrange("p (k t) -> p k t", k=KT)
        MU = at("MU", 176, T)[:, :]
        ZF = at("ZF", 156, 4096)[:, :].rearrange("p (d s h t) -> p d s h t", d=2, s=2, h=4)
        XO = at("XO", 172, 10 * T)[:, :].rearrange("p (n t) -> p n t", n=10)
        CKV = at("CKV", 182, 1024)[:, :].rearrange("p (n t) -> p n t", n=2)
        HI = at("HI", 186, 1024)[:, :].rearrange("p (s t n) -> p (s t) n", s=2, t=2)
        mlw = at("mlw", 120, N_MLW)[:, :]
        QN = at("QN", 72, 1024)[:, :].rearrange("p (h t) -> p h t", h=4)
        QP = at("QP", 76, 512)[:, :]
        QR = at("QR", 78, 512)[:, :]
        KPE = at("KPE", 80, 512)[:, :]
        CKN = at("CKN", 82, 512)[:, :]
        KN = at("KN", 84, 2048)[:, :].rearrange("p (h t) -> p h t", h=4)
        VT = at("VT", 92, 2048)[:, :].rearrange("p (t n) -> p t n", t=4)
        PR = at("PR", 100, 1024)[:, :].rearrange("p (b t) -> p b t", b=2)
        PT = at("PT", 104, 1024)[:, :].rearrange("p (b t) -> p b t", b=2)
        SQ2 = at("SQ2", 108, 1024)[:, :]
        RS2 = at("RS2", 112, 1024)[:, :]
        FC = at("FC", 116, 1024)[:, :]
        MXS = at("MXS", 130, 32)[:, :]
        CQN = at("CQN", 140, 512)[:, :].rearrange("p (k t) -> p k t", k=2)
        FM = at("FM", 142, 512)[:, :].rearrange("p (k t) -> p k t", k=2)
        GG = at("GG", 72, 2048)[:, :].rearrange("p (s h t) -> p s h t", s=2, h=4)
        KK = at("KK", 80, 2048)[:, :].rearrange("p (s h t) -> p s h t", s=2, h=4)
        CC = at("CC", 88, 2048)[:, :].rearrange("p (s h t) -> p s h t", s=2, h=4)
        KWT = at("KWT", 96, 2048)[:, :].rearrange("p (t h k) -> p t h k", t=4, h=4)
        SX = at("SX", 104, 2048)[:, :].rearrange("p (d n m) -> p d n m", d=2, n=4)
        QF = at("QF", 112, 2048)[:, :].rearrange("p (d m) -> p d m", d=2)
        KS = at("KS", 120, 1024)[:, :]
        SC = at("SC", 124, 1024)[:, :]
        QQ = at("QQ", 128, 1024)[:, :]
        EX = at("EX", 140, 2048)[:, :].rearrange("p (b m) -> p b m", b=2)
        QM0 = at("QM0", 96, 1024)[:, :]
        KM0 = at("KM0", 100, 1024)[:, :]
        AD = at("AD", 136.5, 64)[:, :].rearrange("p (d m) -> p d m", d=2)
        STT = at("STT", 152, T)[:, :]
        STU = at("STU", 153, T)[:, :]
        RST64 = at("RST64", 132, T)[:, :]
        assert 133 + N_PAR * 4 / 1024 <= 136.5

        def QMd(d):
            return ZF[:, d, 0, :, :].rearrange("p h t -> p (h t)")

        def KMd(d):
            return ZF[:, d, 1, :, :].rearrange("p h t -> p (h t)")

        SQO = at("SQO", 140, 512)[:, :]
        OH = at("OH", 142, 512)[:, :]
        ZG = at("ZG", 144, 512)[:, :]
        RSO = at("RSO", 146, 512)[:, :]

        OA = MIX[:, 0:4, :].rearrange("p k t -> p (k t)")

        def raw_ap(u):
            return A["wstream"][bass.ds(u, 1)].rearrange("a p n -> (a p) n")

        def split_hi(act, u, slot, rslot, n):
            act.wait_ge(S(f"raw_loaded{rslot}"), n * 16)
            if not (isinstance(u, int) and u < SLOTS):
                act.wait_ge(S("unit_done"), u - (SLOTS - 1))
            nc.scalar.activation(w_hi[:, slot, :], raw[:, rslot, :], ACT.Copy).then_inc(S("hi_done"), 1)

        def split_lo(dve, u, slot, rslot):
            dve.wait_ge(S("hi_done"), u + 1)
            dve.tensor_tensor(w_lo[:, slot, :], raw[:, rslot, :], w_hi[:, slot, :].bitcast(F32),
                              ALU.subtract).then_inc(S("lo_done"), 1)

        def hi(act, u):
            if u < UNITS:
                split_hi(act, u, u % SLOTS, u % RAW_SLOTS, u // RAW_SLOTS + 1)

        def lo(dve, u):
            if u < UNITS:
                split_lo(dve, u, u % SLOTS, u % RAW_SLOTS)

        def split_mm(out, H, L, xh, xl, start, stop, **kw):
            nc.tensor.matmul(out, H, xh, start=start, stop=False, **kw)
            nc.tensor.matmul(out, H, xl, start=False, stop=False, **kw)
            return nc.tensor.matmul(out, L, xh, start=False, stop=stop, **kw)

        def wblk(slot, b):
            return w_hi[:, slot, b * P:(b + 1) * P], w_lo[:, slot, b * P:(b + 1) * P]

        def feature_unit(slot, outs, src, wait_k=None):
            for nb in range(2):
                for k in range(KT):
                    if nb == 0 and wait_k is not None:
                        wait_k(k)
                    H, L = wblk(slot, nb * KT + k)
                    last = split_mm(outs[nb], H, L, a_hi[:, k, src, :], a_lo[:, k, src, :], k == 0, k == KT - 1)
            return last

        def token_unit(slot, outs):
            for s, t, out in outs:
                for k in range(KT):
                    wh, wl = (w[:, slot, k * 256:(k + 1) * 256] for w in (w_hi, w_lo))
                    xh, xl = (a[:, k, s, t * P:(t + 1) * P] for a in (a_hi, a_lo))
                    nc.tensor.matmul(out, xh, wh, start=k == 0, stop=False)
                    nc.tensor.matmul(out, xl, wh, start=False, stop=False)
                    last = nc.tensor.matmul(out, xh, wl, start=False, stop=k == KT - 1)
            return last

        NORMS = ["mix0", "ffn0", "mix1", "ffn1", "ctx", "mix2", "ffn2", "final"]

        def norm_src(n):
            return CTX if NORMS[n] == "ctx" else X

        def wait_x(eng, n, j):
            if n == 0:
                eng.wait_ge(S("x_loaded"), 16)
            elif NORMS[n] == "ctx":
                eng.wait_ge(S("ctx_loaded"), 16)
            else:
                eng.wait_ge(S("x_updated"), 4 * (RES[n]) + j + 1)

        FOLDED = {1: "ffnn0", 2: "mixn1", 3: "ffnn1"}
        HALF = {1: 1, 2: 0, 3: 0}
        NORM_HN = {0: 0, 4: 1, 5: 2, 6: 3, 7: 4}
        RES = {1: 0, 2: 1, 3: 2, 5: 3, 6: 4, 7: 5}

        LN_EXP, SILU, SIGMOID = "natural_log_exp_and_others", "silu_and_others", "sigmoid_and_others"

        def table(name):
            nc.scalar.preload_act_table_set(name)

        def norm_factor(act, n, after):
            act.wait_ge(S("norm_ss"), n + 1)
            rs = RSC if NORMS[n] == "ctx" else RS
            nc.scalar.activation(rs, PS[:, 6, 0:T], ACT.Ln, scale=1.0 / D, bias=prm_eps).then_inc(S("norm_ln"), 1)
            act.wait_ge(S("norm_ln"), n + 1)
            nc.scalar.activation(rs, rs, ACT.Exp, scale=-0.5).then_inc(S("norm_rs"), 1)
            if after:
                table(after)

        def norm_act(act, n, shift=None, split=True, before=None, after=None):
            x = norm_src(n)
            if before:
                table(before)
            for j in range(4):
                wait_x(act, n, j)
                nc.scalar.activation(SQ[:, 2 * j:2 * j + 2, :], x[:, 2 * j:2 * j + 2, :], ACT.Square)\
                    .then_inc(S("norm_sq"), 1)
            norm_factor(act, n, after)
            if not split:
                return
            s = 1 if NORMS[n] == "ctx" else 0
            for j in range(4):
                act.wait_ge(S("norm_hn"), 8 * NORM_HN[n] + 2 * j + 2)
                if shift is None:
                    nc.scalar.activation(a_hi[:, 2 * j:2 * j + 2, s, :], HN[:, 2 * j:2 * j + 2, :], ACT.Copy)\
                        .then_inc(S("norm_hi"), 1)
                else:
                    for k in (2 * j, 2 * j + 1):
                        i = nc.scalar.activation(a_hi[:, k, s, :], HN[:, k, :], ACT.Identity, bias=shift(k))
                    i.then_inc(S("norm_hi"), 1)

        def folded_act(act, n, before=None, after=None):
            g = prm(FOLDED[n], 0, KT)
            if before:
                table(before)
            for j in range(4):
                wait_x(act, n, j)
                for k in (2 * j, 2 * j + 1):
                    i = nc.scalar.activation(a_hi[:, k, HALF[n], :], X[:, k, :], ACT.Copy, scale=g[:, k:k + 1])
                i.then_inc(S("norm_hi"), 1)
                nc.scalar.activation(SQ[:, 2 * j:2 * j + 2, :], X[:, 2 * j:2 * j + 2, :], ACT.Square)\
                    .then_inc(S("norm_sq"), 1)
            norm_factor(act, n, after)

        def folded_lo(dve, n, j):
            g, s = prm(FOLDED[n], 0, KT), HALF[n]
            dve.wait_ge(S("norm_hi"), 4 * n + j + 1)
            for k in (2 * j, 2 * j + 1):
                i = dve.scalar_tensor_tensor(a_lo[:, k, s, :], X[:, k, :], g[:, k:k + 1], a_hi[:, k, s, :].bitcast(F32),
                                             ALU.mult, ALU.subtract)
            i.then_inc(S("act_lo"), 1)

        def norm_pe(pe, n):
            for k in range(KT):
                pe.wait_ge(S("norm_sq"), 4 * n + k // 2 + 1)
                if k == 0 and n > 0:
                    pe.wait_ge(S("norm_rs"), n)
                i = nc.tensor.matmul(PS[:, 6, 0:T], ones, SQ[:, k, :], start=k == 0, stop=k == KT - 1)
            i.then_inc(S("norm_ss"), 1)

        def norm_dve(dve, n, gain, shift=None, split=True):
            x = norm_src(n)
            dve.wait_ge(S("norm_rs"), n + 1)
            rs = RSC if NORMS[n] == "ctx" else RS
            for k in range(KT):
                dve.scalar_tensor_tensor(HN[:, k, :], x[:, k, :], gain(k), rs, ALU.mult, ALU.mult)\
                    .then_inc(S("norm_hn"), 1)
            if not split:
                return
            s = 1 if NORMS[n] == "ctx" else 0
            for j in range(4):
                dve.wait_ge(S("norm_hi"), 4 * (n) + j + 1)
                ks = slice(2 * j, 2 * j + 2)
                if shift is None:
                    dve.tensor_tensor(a_lo[:, ks, s, :], HN[:, ks, :], a_hi[:, ks, s, :].bitcast(F32), ALU.subtract)\
                        .then_inc(S("act_lo"), 1)
                else:
                    for k in (2 * j, 2 * j + 1):
                        i = dve.scalar_tensor_tensor(a_lo[:, k, s, :], HN[:, k, :], shift(k),
                                                     a_hi[:, k, s, :].bitcast(F32), ALU.add, ALU.subtract)
                    i.then_inc(S("act_lo"), 1)

        ACT_LO = {"mix0": 0, "o1": 4, "ffn0": 8, "mix1": 12, "cv": 16, "ffn1": 20, "ctx": 24, "mix2": 28, "o2": 32,
                  "ffn2": 36}

        def wait_act(pe, event, k):
            pe.wait_ge(S("act_lo"), ACT_LO[event] + k // 2 + 1)

        def mix_split_act(act, m, ready):
            for j in range(4):
                ready(act, j)
                nc.scalar.activation(a_hi[:, 2 * j:2 * j + 2, 0, :], MIX[:, 2 * j:2 * j + 2, :], ACT.Copy)\
                    .then_inc(S("mix_hi"), 1)

        def mix_split_dve(dve, m):
            for j in range(4):
                ks = slice(2 * j, 2 * j + 2)
                dve.wait_ge(S("mix_hi"), 4 * m + j + 1)
                dve.tensor_tensor(a_lo[:, ks, 0, :], MIX[:, ks, :], a_hi[:, ks, 0, :].bitcast(F32), ALU.subtract)\
                    .then_inc(S("act_lo"), 1)

        def out_units_pe(pe, u0, event, update, src=0):
            for j in range(N_OUT):
                u = u0 + j
                pe.wait_ge(S("lo_done"), u + 1)
                if j >= 2:
                    pe.wait_ge(S("x_updated"), 4 * update + j - 1)
                outs = [PS[:, 4 + j % 2, nb * T:(nb + 1) * T] for nb in range(2)]
                feature_unit(u % SLOTS, outs, src, (lambda k: wait_act(pe, event, k)) if j == 0 else None)\
                    .then_inc(S("unit_done"), 1)

        PAIRS = FT // 2

        def ffn_pe(pe, f, event, norm=None, behind=None):
            u0 = U_FFN[f]
            if f:
                pe.wait_ge(S("x_updated"), 4 * (2 * f - 1) + 4)
            for b in range(4):
                nc.tensor.matmul(PS[:, b, :], zero[:, 0:P], zero, start=True, stop=True)

            def gate_up(u, slot, fb, j, first=False):
                pe.wait_ge(S("lo_done"), u + 1)
                if j is not None:
                    pe.wait_ge(S("gu_done" if norm else "hf_done"), (j - 1 + f * PAIRS) * 2 + fb + 1)
                outs = [PS[:, 4 + fb, g * T:(g + 1) * T] for g in range(2)]
                feature_unit(slot, outs, HALF[norm] if norm else 0,
                             (lambda k: wait_act(pe, event, k)) if first else None)\
                    .then_inc(S("unit_done"), 1)

            def down(u, slot, j, par_):
                pe.wait_ge(S("lo_done"), u + 1)
                for kk in range(2):
                    pe.wait_ge(S("h_lo_done"), (j + f * PAIRS) * 2 + kk + 1)
                    for nb in range(KT):
                        H, L = wblk(slot, kk * KT + nb)
                        i = split_mm(PS[:, nb // 2, (nb % 2) * T:(nb % 2 + 1) * T], H, L, h_hi[:, par_, kk, :],
                                     h_lo[:, par_, kk, :], False, False, skip_group_check=True)
                i.then_inc(S("unit_done"), 1)

            if norm:
                pe.wait_ge(S("x_updated"), 4 * RES[norm] + 3)
            gate_up(u0, u0 % SLOTS, 0, None, True)
            if norm:
                pe.wait_ge(S("x_updated"), 4 * RES[norm] + 4)
                norm_pe(pe, norm)
            if behind:
                norm_pe(pe, behind)
            gate_up(u0 + 1, (u0 + 1) % SLOTS, 1, None)
            with pe.Fori(0, (PAIRS - 1) // 2) as i:
                for r in range(2):
                    for q in range(3):
                        u = i * 6 + (u0 + 2 + 3 * r + q)
                        slot = (u0 + 2 + 3 * r + q) % SLOTS
                        if q < 2:
                            gate_up(u, slot, q, i * 2 + (1 + r))
                        else:
                            down(u, slot, i * 2 + r, r)
            down(u0 + N_FFN - 1, (u0 + N_FFN - 1) % SLOTS, PAIRS - 1, (PAIRS - 1) % 2)

        def ffn_act(act, f, folded=False):
            u0 = U_FFN[f]

            def evac(u, fb, par_, j):
                if folded:
                    act.wait_ge(S("gu_done"), (j + f * PAIRS) * 2 + fb + 1)
                    nc.scalar.activation(SG[:, fb, :], GU[:, fb, 0:T], ACT.Silu).then_inc(S("silu_done"), 1)
                else:
                    act.wait_ge(S("unit_done"), u + 1)
                    nc.scalar.activation(SG[:, fb, :], PS[:, 4 + fb, 0:T], ACT.Silu).then_inc(S("silu_done"), 1)
                act.wait_ge(S("hf_done"), (j + f * PAIRS) * 2 + fb + 1)
                nc.scalar.activation(h_hi[:, par_, fb, :], HF[:, fb, :], ACT.Copy).then_inc(S("h_hi_done"), 1)

            for q in range(2):
                hi(act, u0 + q + 2)
                evac(u0 + q, q, 0, 0)
            def turn(i):
                for r in range(2):
                    for q in range(3):
                        v = u0 + 2 + 3 * r + q
                        w = v + 2
                        if not (isinstance(i, int) and i * 6 + w >= UNITS):
                            split_hi(act, i * 6 + w, w % SLOTS, w % RAW_SLOTS, i * 3 + (w // RAW_SLOTS + 1))
                        if q < 2:
                            evac(i * 6 + v, q, (1 + r) % 2, i * 2 + (1 + r))

            turns = (PAIRS - 1) // 2
            with act.Fori(0, turns - 1) as i:
                turn(i)
            turn(turns - 1)
            hi(act, u0 + N_FFN + 1)

        def ffn_dve(dve, f, gate=None, folded=False, behind=None):
            u0 = U_FFN[f]

            def evac(u, fb, par_, j):
                n = (j + f * PAIRS) * 2 + fb + 1
                up = PS[:, 4 + fb, T:2 * T]
                if folded:
                    dve.wait_ge(S("unit_done"), u + 1)
                    if isinstance(j, int) and j == 0 and fb == 0:
                        dve.wait_ge(S("norm_rs"), 2 * f + 2)
                    dve.tensor_tensor(GU[:, fb, :].rearrange("p (a t) -> p a t", a=2),
                                      PS[:, 4 + fb, :].rearrange("p (a t) -> p a t", a=2),
                                      RS.unsqueeze(1).to_broadcast([P, 2, T]), ALU.mult).then_inc(S("gu_done"), 1)
                    up = GU[:, fb, T:2 * T]
                dve.wait_ge(S("silu_done"), n)
                dve.tensor_tensor(HF[:, fb, :], SG[:, fb, :], up, ALU.mult).then_inc(S("hf_done"), 1)
                dve.wait_ge(S("h_hi_done"), n)
                dve.tensor_tensor(h_lo[:, par_, fb, :], HF[:, fb, :], h_hi[:, par_, fb, :].bitcast(F32),
                                  ALU.subtract).then_inc(S("h_lo_done"), 1)

            for q in range(2):
                lo(dve, u0 + q + 2)
                evac(u0 + q, q, 0, 0)
            def turn(i):
                for r in range(2):
                    for q in range(3):
                        v = u0 + 2 + 3 * r + q
                        w = v + 2
                        if not (isinstance(i, int) and i * 6 + w >= UNITS):
                            split_lo(dve, i * 6 + w, w % SLOTS, w % RAW_SLOTS)
                        if q < 2:
                            evac(i * 6 + v, q, (1 + r) % 2, i * 2 + (1 + r))

            turns = (PAIRS - 1) // 2
            with dve.Fori(0, turns - 1) as i:
                turn(i)
            turn(turns - 1)
            lo(dve, u0 + N_FFN + 1)
            dve.wait_ge(S("unit_done"), u0 + N_FFN)
            for j in range(4):
                if gate is None:
                    ks = slice(2 * j, 2 * j + 2)
                    dve.tensor_tensor(X[:, ks, :], X[:, ks, :], PS[:, j, :].rearrange("p (k t) -> p k t", k=2),
                                      ALU.add).then_inc(S("x_updated"), 1)
                    if behind is not None and j:
                        folded_lo(dve, behind, j - 1)
                else:
                    for e in range(2):
                        k = 2 * j + e
                        i = dve.scalar_tensor_tensor(X[:, k, :], PS[:, j, e * T:(e + 1) * T], gate(k), X[:, k, :],
                                                     ALU.mult, ALU.add)
                    i.then_inc(S("x_updated"), 1)
            if behind is not None:
                folded_lo(dve, behind, 3)

        epsc = at("epsc", 207.1875, 2)[:, :]
        prm_eps = epsc[:, 0:1]

        QK_BANK = (6, 6, 4, 5)
        TAP_GAP = 12

        def half(e):
            return slice(64 * e, 64 * e + 64)

        block = ctx.enter_context(nc.Block())

        @block.sync
        def _(sp):
            sp.dma_start(X.rearrange("p k t -> p (k t)"), A["xT"]).then_inc(S("x_loaded"), 16)
            for u in range(RAW_SLOTS):
                sp.dma_start(raw[:, u, :], raw_ap(u)).then_inc(S(f"raw_loaded{u}"), 16)
            with sp.Fori(0, UNITS // RAW_SLOTS - 1) as i:
                for s in range(RAW_SLOTS):
                    sp.wait_ge(S("lo_done"), i * RAW_SLOTS + (s + 1))
                    sp.dma_start(raw[:, s, :], raw_ap(i * RAW_SLOTS + (RAW_SLOTS + s)))\
                        .then_inc(S(f"raw_loaded{s}"), 16)
            sp.wait_ge(S("norm_hn"), 8 * len(NORM_HN))
            sp.dma_start(A["out"], HN.rearrange("p k t -> p (k t)")).then_inc(S("out_stored"), 16)
            sp.wait_ge(S("out_stored"), 16)

        @block.tensor
        def _(pe):
            def mod_sums(part):
                pe.wait_ge(S("mod_done"), (68, 136)[part])
                for n in range(4):
                    for b in range(8):
                        m, c = ((n % 2) * 8 + b, n // 2) if part == 0 else (16 + n * 8 + b, 0)
                        i = nc.tensor.matmul(PS[:, 7, 2 * m + c:2 * m + c + 1], MODACC[:, n, b * P:(b + 1) * P],
                                             ones[:, 0:1], start=True, stop=True)
                i.then_inc(S("mod_sum"), 1)

            pe.wait_ge(S("cst_loaded"), 16)
            pe.wait_ge(S("memset_done"), 3)
            norm_pe(pe, 0)
            pe.wait_ge(S("par_loaded"), 16)
            for k in range(KT):
                pe.wait_ge(S("norm_hn"), k + 1)
                i = nc.tensor.matmul(PS[0:16, 3, 0:T], par[:, PAR["wglr"][0] + 16 * k:PAR["wglr"][0] + 16 * k + 16],
                                     HN[:, k, :], start=k == 0, stop=k == KT - 1)
            i.then_inc(S("glr_mm"), 1)

            def in1(u):
                pe.wait_ge(S("lo_done"), u + 1)
                if u == 0:
                    pe.wait_ge(S("act_lo"), 4)
                if u >= 2:
                    pe.wait_ge(S(f"proj{u % 2}_copied"), u // 2)
                outs = [PS[:, 4 + u % 2, t * T:(t + 1) * T] for t in range(2)]
                if u in (0, 1, 6, 7):
                    last = token_unit(u % SLOTS, [(0, t, outs[t]) for t in range(2)])
                else:
                    last = feature_unit(u % SLOTS, outs, 0)
                last.then_inc(S("unit_done"), 1)

            def qk_ss(j):
                pe.wait_ge(S("qk_sq"), j + 1)
                if j == 0:
                    pe.wait_ge(S("norm_rs"), 1)
                if j == 1:
                    pe.wait_ge(S("qk_rs"), 1)
                if j >= 2:
                    pe.wait_ge(S(f"proj{j % 2}_copied"), 6)
                nc.tensor.matmul(PS[:, QK_BANK[j], :], blk, SQF[:, j * 512:(j + 1) * 512], start=True, stop=True)\
                    .then_inc(S("qk_ss"), 1)

            for u in range(6):
                in1(u)
            pe.wait_ge(S("glr_done"), 1)
            for a in range(2):
                i = nc.tensor.matmul(PS[:, 3, a * T:(a + 1) * T],
                                     par[0:16, PAR["wgate2"][0] + a * P:PAR["wgate2"][0] + (a + 1) * P],
                                     GLR, start=True, stop=True)
            i.then_inc(S("gate_mm"), 1)
            in1(6)
            in1(7)
            pe.wait_ge(S("kend_done"), 1)
            for t in range(2):
                for a in range(2):
                    i = nc.tensor.transpose(PS[:, 2, (t * 2 + a) * P:(t * 2 + a + 1) * P],
                                            KEND[:, a * T + t * P:a * T + (t + 1) * P], ident)
            i.then_inc(S("ktok_mm"), 1)
            in1(8)
            pe.wait_ge(S("ktok_done"), 1)
            for n in range(4):
                for h in range(4):
                    r = half(n % 2)
                    i = nc.tensor.matmul(
                        PS[half(h % 2), n % 2, ((n // 2) * 2 + h // 2) * P:((n // 2) * 2 + h // 2 + 1) * P],
                        KTOK[r, (n // 2) * T + h * 64:(n // 2) * T + h * 64 + 64],
                        PROJ[r, h // 2, (n // 2) * T + (h % 2) * P:(n // 2) * T + (h % 2 + 1) * P],
                        start=True, stop=True)
            i.then_inc(S("upd_mm"), 1)
            in1(9)
            pe.wait_ge(S("gate_read"), 3)
            for n in range(4):
                pe.wait_ge(S("state_done"), 2 * n + 2)
                for h in range(4):
                    i = nc.tensor.matmul(PS[:, 2 + h % 2, (h // 2) * T + n * 64:(h // 2) * T + n * 64 + 64],
                                         ST[half(h % 2), n, h // 2, :],
                                         PROJ[half(h % 2), 3, (h // 2) * T + n * 64:(h // 2) * T + n * 64 + 64],
                                         start=True, stop=True)
            i.then_inc(S("og_mm"), 1)
            qk_ss(0)
            in1(10)
            pe.wait_ge(S("og_sq"), 1)
            for e in range(2):
                i = nc.tensor.matmul(PS[:, e, :], ones, OR[:, e * 512:(e + 1) * 512], start=True, stop=True)
            i.then_inc(S("og_ss"), 1)
            qk_ss(1)
            in1(11)
            qk_ss(2)
            qk_ss(3)

            def sb_z(g):
                if g == 0:
                    pe.wait_ge(S("qkn_done"), 3)
                    pe.wait_ge(S("og_rs"), 1)
                if g == 1:
                    pe.wait_ge(S("og_done"), 1)
                if g == 2:
                    pe.wait_ge(S("qkn_done"), 4)
                if g >= 2:
                    pe.wait_ge(S("sb_v"), 3 * g - 3)
                for e in range(2):
                    r, b = half(e), 2 * (g % 2) + e
                    kT, qT = QKN[r, g * T:(g + 1) * T], QKN[r, 1024 + g * T:1024 + (g + 1) * T]
                    nc.tensor.matmul(PS[:, b, 0:256], kT[:, 0:P], qT, start=True, stop=True)
                    i = nc.tensor.matmul(PS[:, b, 256:384], kT[:, P:T], qT[:, P:T], start=True, stop=True)
                i.then_inc(S("sb_z"), 1)

            def sb_between(g):
                pe.wait_ge(S("sb_keep"), g + 1)
                if g == 0:
                    pe.wait_ge(S("qk_rs"), 7)
                else:
                    pe.wait_ge(S("sb_lz2"), g)
                for e in range(2):
                    nc.tensor.matmul(PS[:, 4 + e, 0:384], tri, SBM[:, g % 2, e, :], start=True, stop=False)
                    i = nc.tensor.matmul(PS[:, 4 + e, 128:256], ones, SBM[:, g % 2, e, 256:384],
                                         start=False, stop=True)
                i.then_inc(S("sb_between"), 1)

            def sb_out(g):
                pe.wait_ge(S("sb_w"), g + 1)
                if g:
                    pe.wait_ge(S("sb_o_read"), g)
                for e in range(2):
                    hcol = (g * 2 + e) * 64
                    v = [PROJ[:, 6 + hcol // 256, t * T + hcol % 256:t * T + hcol % 256 + 64] for t in range(2)]
                    nc.tensor.matmul(PS[half(e), 6, 0:256], v[0], SBZ[:, g % 3, e, 0:256], start=True, stop=False)
                    i = nc.tensor.matmul(PS[half(e), 6, 128:256], v[1], SBZ[:, g % 3, e, 256:384],
                                         start=False, stop=True)
                i.then_inc(S("sb_o"), 1)

            sb_z(0)
            sb_z(1)
            for g in range(6):
                if g < 4:
                    sb_between(g)
                if g < 2:
                    sb_z(g + 2)
                if 1 <= g < 5:
                    sb_out(g - 1)
            pe.wait_ge(S("sb_lz2"), 4)
            out_units_pe(pe, U_OUT1, "o1", 0)
            ffn_pe(pe, 0, "ffn0", 1)
            for j in range(N_PW1):
                u = U_PW1 + j
                pe.wait_ge(S("lo_done"), u + 1)
                if j >= 2:
                    pe.wait_ge(S("pw_done"), j - 1)
                outs = [PS[:, 4 + j % 2, g * T:(g + 1) * T] for g in range(2)]
                feature_unit(u % SLOTS, outs, 0, (lambda k: wait_act(pe, "mix1", k)) if j == 0 else None)\
                    .then_inc(S("unit_done"), 1)
                if j == 0:
                    norm_pe(pe, 2)
            for i_, k in enumerate(PE_TILES):
                pe.wait_ge(S("cu_done"), k + 1)
                for j in range(TAPS):
                    n = i_ * TAPS + j
                    pe.wait_ge(S("diag_built"), n + 1)
                    nc.tensor.matmul(PS[:, i_, 0:T], DG[:, n % RING, :], CU[:, k, j:j + T], start=j == 0,
                                     stop=j == TAPS - 1).then_inc(S("diag_used"), 1)
            for k in range(KT):
                if k in PE_TILES:
                    pe.wait_ge(S("cv_pe_done"), PE_TILES.index(k) + 1)
                elif k in (0, 2):
                    pe.wait_ge(S("tap_done"), (2 if k == 0 else 5) * TAPS)
                i = nc.tensor.matmul(PS[:, 6, 0:T], ones, HN[:, k, :], start=k == 0, stop=k == KT - 1)
            i.then_inc(S("ln_sum"), 1)
            mod_sums(0)
            for k in range(KT):
                pe.wait_ge(S("ln_sq"), k // 4 + 1)
                i = nc.tensor.matmul(PS[:, 6, T:2 * T], ones, SQ[:, k, :], start=k == 0, stop=k == KT - 1)
            i.then_inc(S("ln_ss"), 1)
            out_units_pe(pe, U_PW2, "cv", 2, 1)
            ffn_pe(pe, 1, "ffn1", 3, 4)
            norm_pe(pe, 5)
            mod_sums(1)
            pe.wait_ge(S("x_updated"), 16)
            for j in range(5):
                u = U_IN2 + j
                pe.wait_ge(S("lo_done"), u + 1)
                if j >= 2:
                    pe.wait_ge(S("in2_read"), j - 1)
                if j == 0:
                    pe.wait_ge(S("act_lo"), ACT_LO["mix2"] + 4)
                b = 2 * (j % 2)
                feature_unit(u % SLOTS, [PS[:, b + nb, :].rearrange("p (s t) -> p s t", s=2) for nb in range(2)],
                             slice(0, 2)).then_inc(S("unit_done"), 1)
            pe.wait_ge(S("lo_done"), U_IN2 + 6)
            pe.wait_ge(S("in2_read"), 4)
            token_unit((U_IN2 + 5) % SLOTS, [(s, t, PS[:, 2 + s, t * T:(t + 1) * T]) for s in range(2)
                                             for t in range(2)]).then_inc(S("unit_done"), 1)
            for j in range(5):
                u = U_IN2 + 6 + j
                pe.wait_ge(S("lo_done"), u + 1)
                if j >= 2:
                    pe.wait_ge(S("in2_read"), 6 + j - 1)
                feature_unit(u % SLOTS, [PS[:, 4 + j % 2, nb * T:(nb + 1) * T] for nb in range(2)], 0)\
                    .then_inc(S("unit_done"), 1)

            pe.wait_ge(S("in2_read"), 11)
            pe.wait_ge(S("cst2_loaded"), 16)
            fd = c2("fd")
            for t in range(2):
                for a in range(2):
                    i = nc.tensor.matmul(PS[:, t, a * T:(a + 1) * T], XO[:, 8 + a, t * P:(t + 1) * P], fd,
                                         start=True, stop=True)
            i.then_inc(S("fn_mm"), 1)
            pe.wait_ge(S("fc_done"), 1)
            ft = c2("ft").rearrange("p (c t n) -> p c t n", c=2, t=2)
            for a in range(2):
                for t in range(2):
                    for c in range(2):
                        i = nc.tensor.matmul(PS[:, 2, a * T:(a + 1) * T],
                                             FC[:, t * 512 + a * T + c * P:t * 512 + a * T + (c + 1) * P],
                                             ft[:, c, t, :], start=t + c == 0, stop=t + c == 2)
            i.then_inc(S("fn_mm"), 1)
            pe.wait_ge(S("fm_done"), 1)
            wf = c2("wfou").rearrange("p (k n) -> p k n", k=2)
            for a in range(2):
                for k in range(2):
                    i = nc.tensor.matmul(PS[:, 3, a * T:(a + 1) * T], wf[:, k, a * P:(a + 1) * P], FM[:, k, :],
                                         start=k == 0, stop=k == 1)
            i.then_inc(S("fn_mm"), 1)
            pe.wait_ge(S("ml_sq"), 1)
            for k in range(2):
                i = nc.tensor.matmul(PS[:, 4, 0:T], ones, SQ2[:, k * T:(k + 1) * T], start=k == 0, stop=k == 1)
            i = nc.tensor.matmul(PS[:, 5, :], ones, SQ2[:, 512:1024], start=True, stop=True)
            i.then_inc(S("ml_ss"), 1)
            pe.wait_ge(S("fn_read"), 3)
            pe.wait_ge(S("mlw_loaded"), 16)
            pe.wait_ge(S("ml_n"), 1)
            uq = mlw[:, 0:1536].rearrange("p (k n) -> p k n", k=2)
            for nb in range(6):
                for k in range(2):
                    i = nc.tensor.matmul(PS[:, nb // 2, (nb % 2) * T:(nb % 2 + 1) * T], uq[:, k, nb * P:(nb + 1) * P],
                                         CQN[:, k, :], start=k == 0, stop=k == 1)
            i.then_inc(S("ml_q"), 1)
            ukv = mlw[:, 1536:2560]
            pe.wait_ge(S("ml_n"), 2)
            for h in range(2):
                i = nc.tensor.matmul(PS[:, 4 + h, :], ukv[:, h * P:(h + 1) * P], CKN, start=True, stop=True)
                i.then_inc(S("ml_k"), 1)
            pe.wait_ge(S("ml_q_read"), 2)
            for h in range(2, 4):
                i = nc.tensor.matmul(PS[:, h - 2, :], ukv[:, h * P:(h + 1) * P], CKN, start=True, stop=True)
                i.then_inc(S("ml_k"), 1)
            i = nc.tensor.matmul(PS[:, 3, :], c2("rot"), QP, start=True, stop=True)
            i.then_inc(S("ml_rot"), 1)
            nc.tensor.matmul(PS[:, 6, 0:T], c2("rot"), CKV[:, 1, 0:T], start=True, stop=True).then_inc(S("ml_rot"), 1)
            for t in range(4):
                b = (2, 4, 5, 0)[t]
                if t == 1:
                    pe.wait_ge(S("ml_k_read"), 2)
                if t == 3:
                    pe.wait_ge(S("ml_k_read"), 4)
                nc.tensor.matmul(PS[:, b, :], CKN[:, t * P:(t + 1) * P], ukv[:, 512:1024], start=True, stop=True)\
                    .then_inc(S("ml_v"), 1)

            def ml_scores(i):
                h, t = i // 2, i % 2
                b = (1, 3)[i % 2]
                if i == 0:
                    pe.wait_ge(S("rope_done"), 2)
                    pe.wait_ge(S("ml_k_read"), 4)
                if i >= 2:
                    pe.wait_ge(S("ml_exp"), i - 1)
                nc.tensor.matmul(PS[:, b, :], QN[:, h, t * P:(t + 1) * P], KN[:, h, :], start=True, stop=False)
                r = half(h % 2)
                nc.tensor.matmul(PS[:, b, :], QR[r, (h // 2) * T + t * P:(h // 2) * T + (t + 1) * P], KPE[r, :],
                                 start=False, stop=True).then_inc(S("ml_s"), 1)

            ml_scores(0)
            for i in range(8):
                h, t = i // 2, i % 2
                if i < 7:
                    ml_scores(i + 1)
                pe.wait_ge(S("ml_p"), i + 1)
                if i == 0:
                    pe.wait_ge(S("ml_v_read"), 4)
                if i >= 2:
                    pe.wait_ge(S("ml_pt"), i - 1)
                for c in range(4):
                    j = nc.tensor.transpose(PS[:, 4 + i % 2, c * P:(c + 1) * P], PR[:, i % 2, c * P:(c + 1) * P], ident)
                j.then_inc(S("ml_tr"), 1)
                pe.wait_ge(S("ml_pt"), i + 1)
                b = 0 if h < 2 else 2
                for c in range(4):
                    j = nc.tensor.matmul(PS[:, b, (h % 2) * T + t * P:(h % 2) * T + (t + 1) * P],
                                         VT[:, c, h * P:(h + 1) * P], PT[:, i % 2, c * P:(c + 1) * P],
                                         start=c == 0, stop=c == 3)
                j.then_inc(S("ml_o"), 1)

            for d in range(2):
                pe.wait_ge(S("hg_kw"), d + 1)
                if d == 0:
                    pe.wait_ge(S("ml_o_read"), 2)
                for t in range(4):
                    if d == 1 or t >= 2:
                        pe.wait_ge(S("hg_kwt"), 4 * d + t - 1)
                    for h in range(4):
                        i = nc.tensor.transpose(PS[:, 4 + t % 2, h * P:(h + 1) * P],
                                                ZF[:, d, t // 2, h, (t % 2) * P:(t % 2 + 1) * P], ident)
                    i.then_inc(S("hg_tr"), 1)
                pe.wait_ge(S("hg_kwt"), 4 * d + 4)
                if d == 1:
                    pe.wait_ge(S("hg_copied"), 6)
                for s in (1, 0):
                    for n in range(4):
                        t, r = n // 2, half(n % 2)
                        for h in range(4):
                            i = nc.tensor.matmul(PS[:, 2 * (1 - s) + n % 2, t * T + h * 64:t * T + h * 64 + 64],
                                                 KWT[r, 2 * s + t, h, :], HI[r, 2 * s + t, h * 64:h * 64 + 64],
                                                 start=True, stop=True)
                    i.then_inc(S("hg_upd"), 1)
                for l in range(7):
                    st = 7 * d + l
                    if l < 6:
                        pe.wait_ge(S("hg_pair"), 6 * d + l + 1)
                        q, k = (QM0, KM0) if l % 2 == 0 else (QMd(d), KMd(d))
                    elif d == 0:
                        continue
                    else:
                        pe.wait_ge(S("hg_ks"), 2)
                        q, k = QQ, KS
                    bb = (4, 5) if l % 2 == 0 else (0, 1)
                    if l == 0:
                        pe.wait_ge(S("hg_kwt"), 4 * d + 4)
                    if l == 1:
                        pe.wait_ge(S("hg_state"), 7 * d + 7)
                    if l >= 2:
                        pe.wait_ge(S("hg_copied"), 6 * d + l - 1)
                    for m in range(8):
                        h, t = m // 2, m % 2
                        i = nc.tensor.matmul(PS[:, bb[m // 4], (m % 4) * P:(m % 4 + 1) * P],
                                             k[:, h * T + t * P:h * T + (t + 1) * P],
                                             q[:, h * T + t * P:h * T + (t + 1) * P], start=True, stop=True)
                    i.then_inc(S("hg_sc"), 1)
            pe.wait_ge(S("hg_copied"), 13)
            pe.wait_ge(S("hg_qf"), 2)
            for h in range(4):
                for t in range(2):
                    out = PS[half(h % 2), 2, (h // 2) * T + t * P:(h // 2) * T + (t + 1) * P]
                    nc.tensor.matmul(out, HI[:, t, h * 64:h * 64 + 64], SC[:, (2 * h + t) * P:(2 * h + t + 1) * P],
                                     start=True, stop=False, skip_group_check=True)
                    for d in range(2):
                        for n in (2 * t, 2 * t + 1):
                            i = nc.tensor.matmul(PS[half(h % 2), 2, (h // 2) * T + n * 64:(h // 2) * T + n * 64 + 64],
                                                 SX[:, d, n, h * 64:h * 64 + 64],
                                                 QF[:, d, h * T + n * 64:h * T + n * 64 + 64],
                                                 start=False, stop=d == 1, skip_group_check=True)
            i.then_inc(S("hg_o"), 1)
            pe.wait_ge(S("hg_osq"), 1)
            nc.tensor.matmul(PS[:, 3, :], blk, SQO, start=True, stop=True).then_inc(S("hg_oss"), 1)
            out_units_pe(pe, U_OUT2, "o2", 4)
            norm_pe(pe, 6)
            ffn_pe(pe, 2, "ffn2")
            norm_pe(pe, 7)

        @block.scalar
        def _(act):
            act.dma_start(par, A["par"]).then_inc(S("par_loaded"), 16)
            act.dma_start(cst, A["cst"]).then_inc(S("cst_loaded"), 16)
            act.dma_start(csb, A["csb"]).then_inc(S("csb_loaded"), 16)
            act.wait_ge(S("memset_done"), 3)
            act.wait_ge(S("par_loaded"), 16)
            nc.scalar.activation(CSL.rearrange("p k c -> p (k c)"), prm("c2", 0, 16), ACT.Silu).then_inc(S("csl_done"), 1)
            norm_act(act, 0, before=LN_EXP)
            for u in range(3):
                hi(act, u)
            act.wait_ge(S("glr_mm"), 1)
            nc.scalar.activation(GLR, PS[0:16, 3, 0:T], ACT.Copy).then_inc(S("glr_done"), 1)

            def copy_proj(u):
                act.wait_ge(S("unit_done"), u + 1)
                nc.scalar.activation(PROJ[:, u, :], PS[:, 4, :], ACT.Copy).then_inc(S("proj0_copied"), 1)

            def qk_square(j):
                act.wait_ge(S(f"proj{j % 2}_copied"), (8 + j) // 2 + 1)
                nc.scalar.activation(SQF[:, j * 512:(j + 1) * 512], PROJ[:, 8 + j, :], ACT.Square)\
                    .then_inc(S("qk_sq"), 1)

            def qk_rstd(j):
                r = RSF[:, j * 512:(j + 1) * 512]
                act.wait_ge(S("qk_ss"), j + 1)
                nc.scalar.activation(r, PS[:, QK_BANK[j], :], ACT.Ln, scale=1.0 / 64, bias=prm_eps)\
                    .then_inc(S("qk_rs"), 1)
                act.wait_ge(S("qk_rs"), 2 * j + 1)
                nc.scalar.activation(r, r, ACT.Exp, scale=-0.5).then_inc(S("qk_rs"), 1)

            for u in range(6):
                if u % 2 == 0:
                    copy_proj(u)
                hi(act, u + 3)
            act.wait_ge(S("gate_mm"), 1)
            for a in range(2):
                i = nc.scalar.activation(GE[:, a * T:(a + 1) * T], PS[:, 3, a * T:(a + 1) * T], ACT.Abs,
                                         bias=prm("bgate", a))
            i.then_inc(S("gate_read"), 1)
            act.wait_ge(S("gate_read"), 1)
            nc.scalar.activation(GE, GE, ACT.Exp, scale=-1.0).then_inc(S("gate_act"), 1)
            act.wait_ge(S("gate_act"), 1)
            nc.scalar.activation(GE, GE, ACT.Ln, bias=1.0).then_inc(S("gate_act"), 1)
            act.wait_ge(S("gla_diff"), 1)
            nc.scalar.activation(KEND, KEND, ACT.Exp, scale=1.0 / 16).then_inc(S("gla_exp"), 1)
            nc.scalar.activation(DEC, CUM.rearrange("p (m c) -> p m c", c=CHUNK)[:, :, CHUNK - 1], ACT.Exp,
                                 scale=1.0 / 16).then_inc(S("gla_exp"), 1)
            copy_proj(6)
            hi(act, 9)
            act.wait_ge(S("proj1_copied"), 3)
            nc.scalar.activation(RSG, PROJ[:, 4:6, :].rearrange("p a n -> p (a n)"), ACT.Exp, scale=-1.0)\
                .then_inc(S("r_exp"), 1)
            hi(act, 10)
            act.wait_ge(S("ktok_mm"), 1)
            nc.scalar.activation(KTOK, PS[:, 2, :], ACT.Copy).then_inc(S("ktok_done"), 1)
            copy_proj(8)
            qk_square(0)
            hi(act, 11)
            hi(act, 12)
            qk_square(1)
            act.wait_ge(S("og_mm"), 1)
            nc.scalar.activation(OG, banks(2, 4), ACT.Copy, scale=CHUNK ** -0.5).then_inc(S("og_done"), 1)
            act.wait_ge(S("og_done"), 1)
            nc.scalar.activation(OR, OG, ACT.Square).then_inc(S("og_sq"), 1)
            qk_rstd(0)
            copy_proj(10)
            qk_square(2)
            hi(act, 13)
            act.wait_ge(S("og_ss"), 1)
            nc.scalar.activation(OR, banks(0, 2), ACT.Ln, scale=1.0 / P, bias=prm_eps).then_inc(S("og_rs"), 1)
            act.wait_ge(S("og_rs"), 1)
            nc.scalar.activation(OR, OR, ACT.Exp, scale=-0.5).then_inc(S("og_rs"), 1)
            qk_rstd(1)
            qk_square(3)
            qk_rstd(2)
            qk_rstd(3)

            def sb_log(g):
                l = SBL[:, g % 2]
                act.wait_ge(S("sb_z"), g + 1)
                if g >= 2:
                    act.wait_ge(S("sb_keep"), g - 1)
                nc.scalar.activation(l, PS[:, 2 * (g % 2):2 * (g % 2) + 2, 0:384], ACT.Abs, scale=0.125)\
                    .then_inc(S("sb_a"), 1)
                act.wait_ge(S("sb_a"), 3 * g + 1)
                nc.scalar.activation(l, l, ACT.Exp, scale=-1.0).then_inc(S("sb_a"), 1)
                act.wait_ge(S("sb_a"), 3 * g + 2)
                nc.scalar.activation(l, l, ACT.Ln, bias=1.0).then_inc(S("sb_a"), 1)

            def sb_weights(g):
                act.wait_ge(S("sb_lz2"), g + 1)
                nc.scalar.activation(SBZ[:, g % 3], SBZ[:, g % 3], ACT.Exp).then_inc(S("sb_exp"), 1)

            def sb_store(g):
                act.wait_ge(S("sb_o"), g + 1)
                nc.scalar.activation(MIX[:, 4 + g, :], PS[:, 6, 0:T], ACT.Copy).then_inc(S("sb_o_read"), 1)

            act.wait_ge(S("qkn_done"), 4)
            act.wait_ge(S("gla_out"), 1)
            for g in range(6):
                if g < 4:
                    sb_log(g)
                if g == 0:
                    hi(act, 14)
                if 1 <= g < 5:
                    sb_weights(g - 1)
                if g >= 2:
                    sb_store(g - 2)

            def mix1_ready(act, j):
                if j < 2:
                    act.wait_ge(S("gla_out"), 1)
                    act.wait_ge(S("sb_o"), 4)
                else:
                    act.wait_ge(S("sb_o_read"), 2 * (j - 1))
            mix_split_act(act, 0, mix1_ready)
            for j in range(1, N_OUT):
                hi(act, U_OUT1 + j + 2)
            folded_act(act, 1, after=SILU)
            ffn_act(act, 0, True)
            folded_act(act, 2, before=LN_EXP, after=SIGMOID)
            def diagonal(n):
                k, j = PE_TILES[n // TAPS], n % TAPS
                if n >= RING:
                    act.wait_ge(S("diag_used"), n - RING + 1)
                nc.scalar.activation(DG[:, n % RING, :], ident, ACT.Copy, scale=prm("wdw", k * TAPS + j))\
                    .then_inc(S("diag_built"), 1)

            for j in range(N_PW1):
                hi(act, U_PW1 + j + 2)
                act.wait_ge(S("pw_done"), j + 1)
                if j >= 2:
                    act.wait_ge(S("cu_done"), j - 1)
                nc.scalar.activation(SIG[:, j % 2, :], PWR[:, j % 2, T:2 * T], ACT.Sigmoid,
                                     bias=prm("bpw1", 8 + j)).then_inc(S("sig_done"), 1)
                for n in range(RING // N_PW1 * j, RING // N_PW1 * (j + 1)):
                    diagonal(n)
            i_ = 0
            for n in range(RING, RING + len(PE_TILES) * TAPS):
                if n < len(PE_TILES) * TAPS:
                    diagonal(n)
                if n - RING + 1 == TAPS * (i_ + 1):
                    act.wait_ge(S("diag_used"), TAPS * (i_ + 1))
                    k = PE_TILES[i_]
                    nc.scalar.activation(HN[:, k, :], PS[:, i_, 0:T], ACT.Identity, bias=prm("bdw", k))\
                        .then_inc(S("cv_pe_done"), 1)
                    i_ += 1
            table(LN_EXP)
            act.wait_ge(S("ln_sum"), 1)
            nc.scalar.activation(MU, PS[:, 6, 0:T], ACT.Copy, scale=1.0 / D).then_inc(S("ln_mu"), 1)
            for j in range(2):
                act.wait_ge(S("ln_d"), j + 1)
                nc.scalar.activation(SQ[:, 4 * j:4 * j + 4, :], HN[:, 4 * j:4 * j + 4, :], ACT.Square)\
                    .then_inc(S("ln_sq"), 1)
            act.wait_ge(S("ln_ss"), 1)
            nc.scalar.activation(RS, PS[:, 6, T:2 * T], ACT.Ln, scale=1.0 / D, bias=prm_eps).then_inc(S("ln_a"), 1)
            act.wait_ge(S("ln_a"), 1)
            nc.scalar.activation(RS, RS, ACT.Exp, scale=-0.5).then_inc(S("ln_a"), 1)
            table(SILU)
            for j in range(4):
                for k in (2 * j, 2 * j + 1):
                    act.wait_ge(S("ln_n"), k + 1)
                    i = nc.scalar.activation(SQ[:, k, :], HN[:, k, :], ACT.Silu, bias=prm("lnb", k))
                i.then_inc(S("ln_silu"), 1)
                act.wait_ge(S("ln_silu"), j + 1)
                nc.scalar.activation(a_hi[:, 2 * j:2 * j + 2, 1, :], SQ[:, 2 * j:2 * j + 2, :], ACT.Copy)\
                    .then_inc(S("cv_hi"), 1)
            for j in range(N_OUT):
                hi(act, U_PW2 + j + 2)
            folded_act(act, 3, before=LN_EXP)
            norm_act(act, 4, lambda k: MOD[:, k, 1:2], after=SILU)
            ffn_act(act, 1, True)
            act.wait_ge(S("unit_done"), U_FFN[1] + N_FFN)
            act.dma_start(mlw, A["mlw"]).then_inc(S("mlw_loaded"), 16)
            norm_act(act, 5, lambda k: MOD[:, k, 0:1], before=LN_EXP)
            act.wait_ge(S("mod_sum"), 2)
            act.dma_start(cst2, A["cst2"]).then_inc(S("cst2_loaded"), 16)
            for j in range(N_IN2):
                u = U_IN2 + j
                hi(act, u + 2)
                act.wait_ge(S("unit_done"), u + 1)
                if j == 0:
                    nc.scalar.activation(CKV, PS[:, 0:2, :], ACT.Copy).then_inc(S("in2_read"), 1)
                elif j < 5:
                    b, dd, hh = 2 * (j % 2), (j - 1) // 2, 2 * ((j - 1) % 2)
                    for e in range(2):
                        i = nc.scalar.activation(ZF[:, dd, :, hh + e, :],
                                                 PS[:, b + e, :].rearrange("p (s t) -> p s t", s=2), ACT.Copy)
                    i.then_inc(S("in2_read"), 1)
                elif j == 5:
                    nc.scalar.activation(HI.rearrange("p a n -> p (a n)"), banks(2, 4), ACT.Copy)\
                        .then_inc(S("in2_read"), 1)
                else:
                    b = 4 + (j - 6) % 2
                    nc.scalar.activation(XO[:, 2 * (j - 6):2 * (j - 6) + 2, :].rearrange("p a n -> p (a n)"),
                                         PS[:, b, :], ACT.Copy).then_inc(S("in2_read"), 1)
            act.wait_ge(S("fn_mm"), 1)
            nc.scalar.activation(FC, banks(0, 2), ACT.Copy).then_inc(S("fc_done"), 1)
            act.wait_ge(S("fn_mm"), 2)
            nc.scalar.activation(FM.rearrange("p k t -> p (k t)"), PS[:, 2, :], ACT.Copy, scale=1.0 / 128)\
                .then_inc(S("fm_done"), 1)
            act.wait_ge(S("in2_read"), 11)
            nc.scalar.activation(SQ2[:, 0:512], XO[:, 0:2, :].rearrange("p k t -> p (k t)"), ACT.Square)
            nc.scalar.activation(SQ2[:, 512:1024], CKV[:, 0, :], ACT.Square).then_inc(S("ml_sq"), 1)
            act.wait_ge(S("fn_mm"), 3)
            nc.scalar.activation(MIX[:, 6:8, :].rearrange("p k t -> p (k t)"), PS[:, 3, :], ACT.Copy)\
                .then_inc(S("fn_read"), 3)
            act.wait_ge(S("ml_ss"), 1)
            nc.scalar.activation(RS2[:, 0:T], PS[:, 4, 0:T], ACT.Ln, scale=1.0 / 256, bias=prm_eps)
            nc.scalar.activation(RS2[:, 512:1024], PS[:, 5, :], ACT.Ln, scale=1.0 / 128, bias=prm_eps)\
                .then_inc(S("ml_ln"), 1)
            act.wait_ge(S("ml_ln"), 1)
            nc.scalar.activation(RS2[:, 0:T], RS2[:, 0:T], ACT.Exp, scale=-0.5)
            nc.scalar.activation(RS2[:, 512:1024], RS2[:, 512:1024], ACT.Exp, scale=-0.5).then_inc(S("ml_rs"), 1)
            act.wait_ge(S("ml_q"), 1)
            nc.scalar.activation(QP, PS[:, 2, :], ACT.Copy).then_inc(S("ml_q_read"), 1)
            nc.scalar.activation(QN.rearrange("p h t -> p (h t)"), banks(0, 2), ACT.Copy).then_inc(S("ml_q_read"), 1)
            for h in range(4):
                act.wait_ge(S("ml_k"), h + 1)
                nc.scalar.activation(KN[:, h, :], PS[:, (4, 5, 0, 1)[h], :], ACT.Copy).then_inc(S("ml_k_read"), 1)
            for t in range(4):
                act.wait_ge(S("ml_v"), t + 1)
                nc.scalar.activation(VT[:, t, :], PS[:, (2, 4, 5, 0)[t], :], ACT.Copy).then_inc(S("ml_v_read"), 1)
            scale = 192 ** -0.5

            def ml_exp(i):
                act.wait_ge(S("ml_max"), i + 1)
                nc.scalar.activation(MXS[:, i:i + 1], MXS[:, i:i + 1], ACT.Copy, scale=-scale).then_inc(S("ml_neg"), 1)
                act.wait_ge(S("ml_neg"), i + 1)
                if i >= 2:
                    act.wait_ge(S("ml_tr"), i - 1)
                nc.scalar.activation(PR[:, i % 2, :], PS[:, (1, 3)[i % 2], :], ACT.Exp, scale=scale,
                                     bias=MXS[:, i:i + 1], accum_out=MXS[:, 8 + i:9 + i]).then_inc(S("ml_exp"), 1)

            ml_exp(0)
            for i in range(8):
                if i < 7:
                    ml_exp(i + 1)
                act.wait_ge(S("ml_tr"), i + 1)
                if i >= 2:
                    act.wait_ge(S("ml_o"), i - 1)
                nc.scalar.activation(PT[:, i % 2, :], PS[:, 4 + i % 2, :], ACT.Copy).then_inc(S("ml_pt"), 1)
            for j in range(2):
                act.wait_ge(S("ml_o"), 8)
                nc.scalar.activation(OA[:, j * 512:(j + 1) * 512], PS[:, (0, 2)[j], :], ACT.Copy)\
                    .then_inc(S("ml_o_read"), 1)

            act.wait_ge(S("ml_o_read"), 2)
            nc.scalar.activation(QQ, XO[:, 2:6, :].rearrange("p k t -> p (k t)"), ACT.Exp, scale=-1.0)\
                .then_inc(S("hg_qe"), 1)
            for d in range(2):
                z = ZF[:, d].rearrange("p s h t -> p (s h t)")
                g = GG.rearrange("p s h t -> p (s h t)")
                kk = KK.rearrange("p s h t -> p (s h t)")
                if d == 1:
                    act.wait_ge(S("hg_copied"), 6)
                nc.scalar.activation(g, z, ACT.Abs).then_inc(S("hg_a"), 1)
                act.wait_ge(S("hg_a"), 3 * d + 1)
                nc.scalar.activation(g, g, ACT.Exp, scale=-1.0).then_inc(S("hg_a"), 1)
                act.wait_ge(S("hg_a"), 3 * d + 2)
                nc.scalar.activation(g, g, ACT.Ln, bias=1.0).then_inc(S("hg_a"), 1)
                act.wait_ge(S("hg_gz"), d + 1)
                nc.scalar.activation(kk, kk, ACT.Exp).then_inc(S("hg_k"), 1)
                act.wait_ge(S("hg_w"), d + 1)
                nc.scalar.activation(z, z if d == 0 else g, ACT.Exp).then_inc(S("hg_we"), 1)
                nc.scalar.activation(AD[:, d, :],
                                     CC.rearrange("p s h (n c) -> p (s h n) c", c=CHUNK)[:, :, CHUNK - 1], ACT.Exp)\
                    .then_inc(S("hg_ad"), 1)
                if d == 1:
                    act.wait_ge(S("hg_qx"), 1)
                nc.scalar.activation(QF[:, d, :], CC[:, 0].rearrange("p h t -> p (h t)") if d == 0 else QF[:, 1, :],
                                     ACT.Exp).then_inc(S("hg_qxe"), 1)
                for t in range(4):
                    act.wait_ge(S("hg_tr"), 4 * d + t + 1)
                    nc.scalar.activation(KWT[:, t].rearrange("p h k -> p (h k)"), PS[:, 4 + t % 2, :], ACT.Copy)\
                        .then_inc(S("hg_kwt"), 1)
                for l in range(6):
                    act.wait_ge(S("hg_e"), 6 * d + l + 1)
                    nc.scalar.activation(EX[:, l % 2, :], EX[:, l % 2, :], ACT.Exp).then_inc(S("hg_ee"), 1)
            act.wait_ge(S("hg_o"), 1)
            nc.scalar.activation(OH, PS[:, 2, :], ACT.Copy).then_inc(S("hg_r"), 1)
            act.wait_ge(S("hg_r"), 1)
            nc.scalar.activation(SQO, OH, ACT.Square).then_inc(S("hg_osq"), 1)
            nc.scalar.activation(ZG, XO[:, 6:8, :].rearrange("p k t -> p (k t)"), ACT.Exp, scale=-1.0)\
                .then_inc(S("hg_ze"), 1)
            act.wait_ge(S("hg_oss"), 1)
            nc.scalar.activation(RSO, PS[:, 3, :], ACT.Ln, scale=1.0 / 64, bias=prm_eps).then_inc(S("hg_r"), 1)
            act.wait_ge(S("hg_r"), 2)
            nc.scalar.activation(RSO, RSO, ACT.Exp, scale=-0.5).then_inc(S("hg_r"), 1)

            def mix2_ready(act, j):
                if j == 0:
                    act.wait_ge(S("hg_out"), 1)
            mix_split_act(act, 1, mix2_ready)
            for j in range(N_OUT):
                hi(act, U_OUT2 + j + 2)
            norm_act(act, 6, lambda k: MOD[:, 24 + k, 0:1], after=SILU)
            ffn_act(act, 2)
            norm_act(act, 7, split=False, before=LN_EXP)

        @block.vector
        def _(dve):
            dve.memset(zero, 0.0).then_inc(S("memset_done"), 1)
            dve.memset(epsc, EPS).then_inc(S("memset_done"), 1)
            dve.memset(RESET, 1.0).then_inc(S("memset_done"), 1)
            dve.wait_ge(S("memset_done"), 3)
            dve.memset(RESET.rearrange("p (m c) -> p m c", c=CHUNK)[:, :, 0:1], 0.0).then_inc(S("memset_done"), 1)
            dve.wait_ge(S("par_loaded"), 16)
            norm_dve(dve, 0, lambda k: prm("mixn0", k))
            for u in range(3):
                lo(dve, u)

            def copy_proj(u):
                dve.wait_ge(S("unit_done"), u + 1)
                dve.tensor_copy(PROJ[:, u, :], PS[:, 5, :]).then_inc(S("proj1_copied"), 1)

            def qk_norm(j):
                dve.wait_ge(S("qk_rs"), 2 * j + 2)
                dve.scalar_tensor_tensor(QKN[:, j * 512:(j + 1) * 512], PROJ[:, 8 + j, :],
                                         prm(("sbk", "sbq")[j // 2]), RSF[:, j * 512:(j + 1) * 512], ALU.mult,
                                         ALU.mult).then_inc(S("qkn_done"), 1)

            for u in range(6):
                if u % 2 == 1:
                    copy_proj(u)
                lo(dve, u + 3)
            dve.wait_ge(S("gate_mm"), 1)
            dve.wait_ge(S("gate_read"), 1)
            for a in range(2):
                dve.tensor_scalar(LA[:, a * T:(a + 1) * T], PS[:, 3, a * T:(a + 1) * T], prm("bgate", a), 0.0,
                                  ALU.add, ALU.min).then_inc(S("gate_read"), 1)
            dve.wait_ge(S("gate_read"), 3)
            dve.wait_ge(S("gate_act"), 2)
            dve.tensor_tensor(LA, LA, GE, ALU.subtract).then_inc(S("gla_dve"), 1)
            dve.wait_ge(S("gla_dve"), 1)
            dve.wait_ge(S("memset_done"), 4)
            dve.tensor_tensor_scan(CUM, RESET, LA, 0.0, ALU.mult, ALU.add).then_inc(S("gla_dve"), 1)
            dve.wait_ge(S("gla_dve"), 2)
            cum = CUM.rearrange("p (m c) -> p m c", c=CHUNK)
            dve.tensor_tensor(KEND.rearrange("p (m c) -> p m c", c=CHUNK),
                              cum[:, :, CHUNK - 1:CHUNK].to_broadcast([P, 8, CHUNK]), cum, ALU.subtract)\
                .then_inc(S("gla_diff"), 1)
            dve.wait_ge(S("gla_exp"), 1)
            dve.wait_ge(S("proj0_copied"), 2)
            dve.tensor_tensor(KEND, KEND, PROJ[:, 2, :], ALU.mult).then_inc(S("kend_done"), 1)
            lo(dve, 9)
            copy_proj(7)
            lo(dve, 10)
            dve.wait_ge(S("r_exp"), 1)
            dve.tensor_scalar(RSG, RSG, 1.0, None, ALU.add).then_inc(S("r_dve"), 1)
            dve.wait_ge(S("r_dve"), 1)
            dve.reciprocal(RSG, RSG).then_inc(S("r_dve"), 1)
            dve.wait_ge(S("r_dve"), 2)
            dve.tensor_tensor(RSG, RSG, PROJ[:, 4:6, :].rearrange("p a n -> p (a n)"), ALU.mult).then_inc(S("r_dve"), 1)
            dve.wait_ge(S("upd_mm"), 1)
            dve.wait_ge(S("gla_exp"), 2)
            for n in range(4):
                for a in range(2):
                    U = PS[:, n % 2, ((n // 2) * 2 + a) * P:((n // 2) * 2 + a + 1) * P]
                    if n == 0:
                        dve.tensor_copy(ST[:, 0, a, :], U).then_inc(S("state_done"), 1)
                    else:
                        dve.wait_ge(S("state_done"), 2 * n + a - 1)
                        dve.scalar_tensor_tensor(ST[:, n, a, :], ST[:, n - 1, a, :], DEC[:, a * 4 + n:a * 4 + n + 1], U,
                                                 ALU.mult, ALU.add).then_inc(S("state_done"), 1)
            lo(dve, 11)
            copy_proj(9)
            lo(dve, 12)
            qk_norm(0)
            lo(dve, 13)
            dve.wait_ge(S("og_rs"), 2)
            dve.scalar_tensor_tensor(OG, OG, prm("glan"), OR, ALU.mult, ALU.mult).then_inc(S("r_dve"), 1)
            qk_norm(1)
            copy_proj(11)
            dve.wait_ge(S("r_dve"), 4)
            og = OG.rearrange("p (e a t) -> p a e t", e=2, a=2)
            mx = MIX[:, 0:4, :].rearrange("p (a e) t -> p a e t", a=2)
            rg = RSG.rearrange("p (a e t) -> p a e t", a=2, e=2)
            for a in range(2):
                i = dve.tensor_tensor(mx[:, a], og[:, a], rg[:, a], ALU.mult)
            i.then_inc(S("gla_out"), 1)
            qk_norm(2)
            qk_norm(3)

            dve.wait_ge(S("csb_loaded"), 16)
            mb = sbmask.unsqueeze(1).to_broadcast([P, 2, 384])

            def sb_keep(g):
                z = PS[:, 2 * (g % 2):2 * (g % 2) + 2, 0:384]
                dve.wait_ge(S("sb_a"), 3 * g + 3)
                if g:
                    dve.wait_ge(S("sb_v"), 3 * g)
                    dve.wait_ge(S("sb_keep"), g)
                dve.tensor_scalar(SBK, z, 0.125, 0.0, ALU.mult, ALU.max).then_inc(S("sb_v"), 1)
                dve.wait_ge(S("sb_v"), 3 * g + 1)
                dve.scalar_tensor_tensor(SBK, SBK, -1.0, SBL[:, g % 2], ALU.mult, ALU.subtract).then_inc(S("sb_v"), 1)
                dve.wait_ge(S("sb_v"), 3 * g + 2)
                if g >= 2:
                    dve.wait_ge(S("sb_between"), g - 1)
                dve.tensor_tensor(SBM[:, g % 2], SBK, mb, ALU.mult).then_inc(S("sb_keep"), 1)
                if g == 3:
                    dve.wait_ge(S("sb_o"), 1)
                dve.scalar_tensor_tensor(SBZ[:, g % 3], z, 0.125, SBK, ALU.mult, ALU.add).then_inc(S("sb_v"), 1)

            def sb_add(g):
                dve.wait_ge(S("sb_v"), 3 * g + 3)
                dve.wait_ge(S("sb_between"), g + 1)
                dve.tensor_tensor(SBZ[:, g % 3], SBZ[:, g % 3], PS[:, 4:6, 0:384], ALU.add).then_inc(S("sb_lz2"), 1)

            def sb_mask(g):
                w = SBZ[:, g % 3].rearrange("p e (b n) -> p e b n", b=3)[:, :, 0:3:2, :]
                m = sbmask.rearrange("p (b n) -> p b n", b=3)[:, 0:3:2, :].unsqueeze(1).to_broadcast([P, 2, 2, P])
                dve.wait_ge(S("sb_exp"), g + 1)
                dve.tensor_tensor(w, w, m, ALU.mult).then_inc(S("sb_w"), 1)

            for g in range(6):
                if g < 4:
                    sb_keep(g)
                if g == 1:
                    lo(dve, 14)
                if g >= 2:
                    sb_mask(g - 2)
                if 1 <= g < 5:
                    sb_add(g - 1)
            mix_split_dve(dve, 0)

            def residual_units(u0, add, norm=None):
                for j in range(N_OUT):
                    if not (u0 == U_OUT1 and j == 0):
                        if u0 == U_PW2 and j == 0:
                            dve.wait_ge(S("lo_done"), u0 + 2)
                        lo(dve, u0 + j + 2)
                    dve.wait_ge(S("unit_done"), u0 + j + 1)
                    add(j)
                    if norm and j:
                        folded_lo(dve, norm, j - 1)
                if norm:
                    folded_lo(dve, norm, 3)

            def plain(j):
                ks = slice(2 * j, 2 * j + 2)
                dve.tensor_tensor(X[:, ks, :], X[:, ks, :], PS[:, 4 + j % 2, :].rearrange("p (k t) -> p k t", k=2),
                                  ALU.add).then_inc(S("x_updated"), 1)

            residual_units(U_OUT1, plain, 1)
            ffn_dve(dve, 0, folded=True, behind=2)
            dve.memset(CU[:, :, 0:TAPS - 1], 0.0).then_inc(S("cu_zero"), 1)
            dve.wait_ge(S("cu_zero"), 1)

            def scaled(k):
                dve.wait_ge(S("unit_done"), U_PW1 + k + 1)
                if k == 0:
                    dve.wait_ge(S("norm_rs"), 3)
                if k >= 2:
                    dve.wait_ge(S("cu_done"), k - 1)
                dve.tensor_tensor(PWR[:, k % 2, :].rearrange("p (a t) -> p a t", a=2),
                                  PS[:, 4 + k % 2, :].rearrange("p (a t) -> p a t", a=2),
                                  RS.unsqueeze(1).to_broadcast([P, 2, T]), ALU.mult).then_inc(S("pw_done"), 1)

            def gate(k):
                if k + 1 < KT:
                    scaled(k + 1)
                dve.wait_ge(S("sig_done"), k + 1)
                dve.scalar_tensor_tensor(CU[:, k, TAPS - 1:TAPS - 1 + T], PWR[:, k % 2, 0:T], prm("bpw1", k),
                                         SIG[:, k % 2, :], ALU.add, ALU.mult).then_inc(S("cu_done"), 1)

            scaled(0)
            n, gated_ = 0, 0
            for group in ((0, 1), (2, 3, 4)):
                while gated_ <= group[-1]:
                    gate(gated_)
                    gated_ += 1
                dve.wait_ge(S("cu_done"), group[-1] + 1)
                for j in range(TAPS):
                    for k in group:
                        u, w = CU[:, k, j:j + T], prm("wdw", k * TAPS + j)
                        if j == 0:
                            dve.tensor_scalar(HN[:, k, :], u, w, prm("bdw", k), ALU.mult, ALU.add)\
                                .then_inc(S("tap_done"), 1)
                        else:
                            dve.wait_ge(S("tap_done"), n - len(group) + 1)
                            i = dve.scalar_tensor_tensor(HN[:, k, :], u, w, HN[:, k, :], ALU.mult, ALU.add)
                            i.then_inc(S("tap_done"), 1)
                        n += 1
                        if n % TAP_GAP == 0 and gated_ < KT:
                            gate(gated_)
                            gated_ += 1
            dve.wait_ge(S("tap_done"), (KT - len(PE_TILES)) * TAPS)
            dve.wait_ge(S("ln_mu"), 1)
            for j in range(2):
                ks = slice(4 * j, 4 * j + 4)
                dve.tensor_tensor(HN[:, ks, :], HN[:, ks, :], MU.unsqueeze(1).to_broadcast([P, 4, T]), ALU.subtract)\
                    .then_inc(S("ln_d"), 1)
            dve.wait_ge(S("ln_a"), 2)
            for k in range(KT):
                dve.scalar_tensor_tensor(HN[:, k, :], HN[:, k, :], prm("lng", k), RS, ALU.mult, ALU.mult)\
                    .then_inc(S("ln_n"), 1)
            for j in range(4):
                ks = slice(2 * j, 2 * j + 2)
                dve.wait_ge(S("cv_hi"), j + 1)
                dve.tensor_tensor(a_lo[:, ks, 1, :], SQ[:, ks, :], a_hi[:, ks, 1, :].bitcast(F32), ALU.subtract)\
                    .then_inc(S("act_lo"), 1)

            def biased(j):
                for e in range(2):
                    k = 2 * j + e
                    i = dve.scalar_tensor_tensor(X[:, k, :], PS[:, 4 + j % 2, e * T:(e + 1) * T], prm("bpw2", k),
                                                 X[:, k, :], ALU.add, ALU.add)
                i.then_inc(S("x_updated"), 1)

            residual_units(U_PW2, biased, 3)
            modp = PS[:, 7, 0:96].rearrange("p (n c) -> p n c", c=2)
            dve.wait_ge(S("mod_sum"), 1)
            dve.tensor_tensor(MOD[:, 0:16, :], modp[:, 0:16, :], prm("bmod", 0, 16).unsqueeze(2).to_broadcast([P, 16, 2]),
                              ALU.add).then_inc(S("modv"), 1)
            dve.wait_ge(S("modv"), 1)
            for n, c in enumerate((0, 1)):
                dve.scalar_tensor_tensor(GSC[:, n, :], MOD[:, 8:16, c], 1.0, prm("n1g", 0, 8), ALU.add, ALU.mult)\
                    .then_inc(S("modv"), 1)
            dve.wait_ge(S("modv"), 3)
            norm_dve(dve, 4, lambda k: GSC[:, 1, k:k + 1], lambda k: MOD[:, k, 1:2])
            ffn_dve(dve, 1, folded=True)
            norm_dve(dve, 5, lambda k: GSC[:, 0, k:k + 1], lambda k: MOD[:, k, 0:1])
            dve.wait_ge(S("mod_sum"), 2)
            dve.tensor_tensor(MOD[:, 16:48, 0], modp[:, 16:48, 0], prm("bmod", 16, 32), ALU.add).then_inc(S("modv"), 1)
            dve.wait_ge(S("modv"), 4)
            dve.scalar_tensor_tensor(GSC[:, 2, :], MOD[:, 32:40, 0], 1.0, prm("n2g", 0, 8), ALU.add, ALU.mult)\
                .then_inc(S("modv"), 1)
            for j in range(N_IN2):
                lo(dve, U_IN2 + j + 2)
            dve.wait_ge(S("modv"), 5)
            dve.wait_ge(S("cst2_loaded"), 16)
            dve.wait_ge(S("ml_rs"), 1)
            for k in range(2):
                i = dve.scalar_tensor_tensor(CQN[:, k, :], XO[:, k, :], prm("qng", k), RS2[:, 0:T], ALU.mult, ALU.mult)
            i.then_inc(S("ml_n"), 1)
            dve.scalar_tensor_tensor(CKN, CKV[:, 0, :], prm("kvg"), RS2[:, 512:1024], ALU.mult, ALU.mult)\
                .then_inc(S("ml_n"), 1)
            cos2 = c2("cos").unsqueeze(1).to_broadcast([P, 2, T])
            sin2 = c2("sin").unsqueeze(1).to_broadcast([P, 2, T])
            v2 = lambda ap: ap.rearrange("p (a t) -> p a t", a=2)
            dve.wait_ge(S("ml_q_read"), 1)
            dve.wait_ge(S("ml_rot"), 2)
            dve.tensor_tensor(v2(QR), v2(PS[:, 3, :]), sin2, ALU.mult).then_inc(S("rope"), 1)
            dve.tensor_tensor(v2(QP), v2(QP), cos2, ALU.mult).then_inc(S("rope"), 1)
            dve.tensor_tensor(KPE[:, 0:T], PS[:, 6, 0:T], c2("sin"), ALU.mult).then_inc(S("rope"), 1)
            dve.tensor_tensor(KPE[:, T:2 * T], CKV[:, 1, 0:T], c2("cos"), ALU.mult).then_inc(S("rope"), 1)
            dve.wait_ge(S("rope"), 4)
            dve.tensor_tensor(QR, QR, QP, ALU.add).then_inc(S("rope_done"), 1)
            dve.tensor_tensor(KPE[:, 0:T], KPE[:, 0:T], KPE[:, T:2 * T], ALU.add).then_inc(S("rope"), 1)
            dve.wait_ge(S("rope"), 5)
            dve.tensor_copy(KPE[:, T:2 * T], CKV[:, 1, T:2 * T]).then_inc(S("rope_done"), 1)

            def ml_max(i):
                dve.wait_ge(S("ml_s"), i + 1)
                dve.reduce_max(MXS[:, i:i + 1], PS[:, (1, 3)[i % 2], :], AX.X).then_inc(S("ml_max"), 1)

            ml_max(0)
            for i in range(8):
                if i < 7:
                    ml_max(i + 1)
                dve.wait_ge(S("ml_exp"), i + 1)
                dve.reciprocal(MXS[:, 16 + i:17 + i], MXS[:, 8 + i:9 + i]).then_inc(S("ml_rc"), 1)
                dve.wait_ge(S("ml_rc"), i + 1)
                dve.tensor_scalar(PR[:, i % 2, :], PR[:, i % 2, :], MXS[:, 16 + i:17 + i], None, ALU.mult)\
                    .then_inc(S("ml_p"), 1)

            dve.memset(RST64, 1.0).then_inc(S("hg_reset"), 1)
            dve.wait_ge(S("hg_reset"), 1)
            dve.memset(RST64.rearrange("p (m c) -> p m c", c=CHUNK)[:, :, 0:1], 0.0).then_inc(S("hg_reset"), 1)
            dve.wait_ge(S("hg_reset"), 2)
            dve.wait_ge(S("hg_qe"), 1)
            dve.tensor_scalar(QQ, QQ, 1.0, None, ALU.add).then_inc(S("hg_q"), 1)
            dve.wait_ge(S("hg_q"), 1)
            dve.reciprocal(QQ, QQ).then_inc(S("hg_q"), 1)
            dve.wait_ge(S("hg_q"), 2)
            dve.tensor_tensor(QQ, QQ, XO[:, 2:6, :].rearrange("p k t -> p (k t)"), ALU.mult).then_inc(S("hg_q"), 1)
            ch = lambda ap: ap.rearrange("p s h (n c) -> p (s h n) c", c=CHUNK)
            fl = lambda ap: ap.rearrange("p s h t -> p (s h t)")
            for d in range(2):
                z, g, kk, cc = ZF[:, d], GG, KK, CC
                dve.wait_ge(S("hg_a"), 3 * d + 3)
                dve.scalar_tensor_tensor(fl(g), fl(z), 0.0, fl(g), ALU.min, ALU.subtract).then_inc(S("hg_v"), 1)
                dve.wait_ge(S("hg_v"), 2 * d + 1)
                dve.tensor_tensor(fl(kk), fl(g), fl(z), ALU.subtract).then_inc(S("hg_gz"), 1)
                for s in range(2):
                    for h in range(4):
                        i = dve.tensor_tensor_scan(cc[:, s, h, :], RST64, g[:, s, h, :], 0.0, ALU.mult, ALU.add)
                i.then_inc(S("hg_v"), 1)
                dve.wait_ge(S("hg_v"), 2 * d + 2)
                dve.wait_ge(S("hg_gz"), d + 1)
                end = ch(cc)[:, :, CHUNK - 1:CHUNK].to_broadcast([P, 32, CHUNK])
                endx = ch(cc)[:, 0:16, CHUNK - 1:CHUNK].to_broadcast([P, 16, CHUNK])
                if d == 0:
                    dve.tensor_tensor(ch(z), end, ch(cc), ALU.subtract).then_inc(S("hg_w"), 1)
                    X_ = cc
                else:
                    dve.tensor_tensor(fl(g), fl(cc), fl(g), ALU.subtract).then_inc(S("hg_w"), 1)
                    dve.wait_ge(S("hg_w"), 2)
                    dve.tensor_tensor(QF[:, 1, :].rearrange("p (m c) -> p m c", c=CHUNK), endx, ch(g)[:, 0:16, :],
                                      ALU.subtract).then_inc(S("hg_qx"), 1)
                    X_ = g
                dve.wait_ge(S("hg_k"), d + 1)
                dve.wait_ge(S("hg_we"), d + 1)
                dve.tensor_tensor(fl(z), fl(z), fl(kk), ALU.mult).then_inc(S("hg_kw"), 1)
                if d == 0:
                    dve.tensor_copy(KS, fl(kk)[:, 0:1024]).then_inc(S("hg_ks"), 1)
                else:
                    dve.tensor_tensor(KS, KS, fl(kk)[:, 0:1024], ALU.add).then_inc(S("hg_ks"), 1)
                dve.wait_ge(S("hg_qxe"), d + 1)
                dve.wait_ge(S("hg_q"), 3)
                dve.tensor_tensor(QF[:, d, :], QF[:, d, :], QQ, ALU.mult).then_inc(S("hg_qf"), 1)
                order = [(1, n) for n in range(4)] + [(0, n) for n in range(4)]
                if d == 1:
                    order = [(s, 3 - n) for s, n in order]
                dve.wait_ge(S("hg_ad"), d + 1)
                prev = None
                ad = AD[:, d, :].rearrange("p (s h n) -> p s h n", s=2, h=4)
                for c, (s, n) in enumerate(order):
                    upd = PS[:, 2 * (1 - s) + n % 2, (n // 2) * T:(n // 2) * T + T]
                    if c < 7:
                        s2, n2 = order[c + 1]
                        dst = SX[:, d, n2, :] if s2 == 0 else (STT if c % 2 == 0 else STU)
                        dve.wait_ge(S("hg_upd"), 2 * d + (2 - s))
                        if prev is None:
                            dve.tensor_copy(dst, upd).then_inc(S("hg_state"), 1)
                        else:
                            dve.wait_ge(S("hg_state"), 7 * d + c)
                            v = lambda ap: ap.rearrange("p (h v) -> p h v", h=4)
                            dve.tensor_tensor(v(dst), v(prev), ad[:, s, :, n:n + 1].to_broadcast([P, 4, 64]), ALU.mult)\
                                .then_inc(S("hg_dec"), 1)
                            dve.wait_ge(S("hg_dec"), 6 * d + c)
                            dve.tensor_tensor(dst, dst, upd, ALU.add).then_inc(S("hg_state"), 1)
                        prev = dst
                if d == 0:
                    dve.wait_ge(S("hg_upd"), 2)
                    for buf in (QM0, KM0):
                        dve.memset(buf, 0.0).then_inc(S("hg_zero"), 1)
                    dve.memset(SC, 0.0).then_inc(S("hg_zero"), 1)
                dve.wait_ge(S("hg_upd"), 2 * d + 2)
                if d == 1:
                    for buf in (QM0, KM0):
                        dve.memset(buf, 0.0).then_inc(S("hg_zero"), 1)
                for buf in (QMd(d), KMd(d)):
                    dve.memset(buf, 0.0).then_inc(S("hg_zero"), 1)
                dve.wait_ge(S("hg_zero"), 5 if d == 0 else 9)
                xs = X_[:, 0].rearrange("p h t -> p (h t)")
                xk = kk[:, 0].rearrange("p h t -> p (h t)")

                def pair_exponents(l):
                    m = LEVELS[l]
                    w = lambda ap: ap.rearrange("p (a b m) -> p a b m", b=2, m=m)
                    a = 512 // m
                    ref = w(xs)[:, :, 0, m - 1:m] if d == 0 else w(xs)[:, :, 1, 0:1]
                    ref = ref.to_broadcast([P, a, m])
                    e = w(EX[:, l % 2, :])
                    if l >= 2:
                        dve.wait_ge(S("hg_pair"), 6 * d + l - 1)
                    dve.tensor_tensor(e[:, :, 1, :], w(xs)[:, :, 1, :], ref, ALU.subtract)
                    dve.tensor_tensor(e[:, :, 0, :], ref, w(xs)[:, :, 0, :], ALU.subtract).then_inc(S("hg_e"), 1)

                def pair_products(l):
                    m = LEVELS[l]
                    w = lambda ap: ap.rearrange("p (a b m) -> p a b m", b=2, m=m)
                    q, k = (QM0, KM0) if l % 2 == 0 else (QMd(d), KMd(d))
                    qs, ks_ = (1, 0) if d == 0 else (0, 1)
                    e = w(EX[:, l % 2, :])
                    dve.wait_ge(S("hg_ee"), 6 * d + l + 1)
                    if l >= 2:
                        dve.wait_ge(S("hg_sc"), 6 * d + l - 1)
                    dve.tensor_tensor(w(q)[:, :, qs, :], w(QQ)[:, :, qs, :], e[:, :, qs, :], ALU.mult)
                    dve.tensor_tensor(w(k)[:, :, ks_, :], w(xk)[:, :, ks_, :], e[:, :, ks_, :], ALU.mult)\
                        .then_inc(S("hg_pair"), 1)

                def pair_copy(l):
                    bb = 4 if l % 2 == 0 else 0
                    dve.wait_ge(S("hg_sc"), 6 * d + l + 1)
                    mi = 6 * d + l
                    mask = c2("lmask")[:, mi * P:(mi + 1) * P].bitcast(I32).unsqueeze(1).to_broadcast([P, 8, P])
                    if mi:
                        dve.wait_ge(S("hg_copied"), mi)
                    dve.copy_predicated(SC.rearrange("p (m t) -> p m t", m=8), mask,
                                        banks(bb, bb + 2).rearrange("p (m t) -> p m t", m=8))\
                        .then_inc(S("hg_copied"), 1)

                pair_exponents(0)
                for l in range(6):
                    if l < 5:
                        pair_exponents(l + 1)
                    pair_products(l)
                    if l:
                        pair_copy(l - 1)
                pair_copy(5)
                if d == 1:
                    pair_copy(6)
                else:
                    pass
            dve.wait_ge(S("hg_ze"), 1)
            dve.tensor_scalar(ZG, ZG, 1.0, None, ALU.add).then_inc(S("hg_f"), 1)
            dve.wait_ge(S("hg_f"), 1)
            dve.reciprocal(ZG, ZG).then_inc(S("hg_f"), 1)
            dve.wait_ge(S("hg_f"), 2)
            dve.tensor_tensor(ZG, ZG, XO[:, 6:8, :].rearrange("p k t -> p (k t)"), ALU.mult).then_inc(S("hg_f"), 1)
            dve.wait_ge(S("hg_r"), 3)
            for a in range(2):
                dve.scalar_tensor_tensor(OH[:, a * T:(a + 1) * T], OH[:, a * T:(a + 1) * T], prm("hgg", a),
                                         RSO[:, a * T:(a + 1) * T], ALU.mult, ALU.mult).then_inc(S("hg_f"), 1)
            dve.wait_ge(S("hg_f"), 5)
            dve.tensor_tensor(MIX[:, 4:6, :].rearrange("p k t -> p (k t)"), OH, ZG, ALU.mult).then_inc(S("hg_out"), 1)
            mix_split_dve(dve, 1)

            def gated(j):
                for e in range(2):
                    k = 2 * j + e
                    i = dve.scalar_tensor_tensor(X[:, k, :], PS[:, 4 + j % 2, e * T:(e + 1) * T], MOD[:, 16 + k, 0:1],
                                                 X[:, k, :], ALU.mult, ALU.add)
                i.then_inc(S("x_updated"), 1)

            residual_units(U_OUT2, gated)
            norm_dve(dve, 6, lambda k: GSC[:, 2, k:k + 1], lambda k: MOD[:, 24 + k, 0:1])
            ffn_dve(dve, 2, lambda k: MOD[:, 40 + k, 0:1])
            norm_dve(dve, 7, lambda k: prm("fing", k), split=False)

        @block.gpsimd
        def _(pool):
            pool.wait_ge(S("csl_done"), 1)
            pool.wait_ge(S("act_lo"), 8)
            for n in range(4):
                pool.memset(MODACC[:, n, :], 0.0).then_inc(S("mod_done"), 1)
            for m in range(2):
                pool.dma_start(modraw[:, m, :], A["wmod"][m]).then_inc(S(f"mod_loaded{m}"), 16)
            pool.dma_start(CTX.rearrange("p k t -> p (k t)"), A["ctxT"]).then_inc(S("ctx_loaded"), 16)

            def mod_product(out, k, c, n):
                pool.wait_ge(S("mod_done"), n)
                pool.tensor_tensor(out, modraw[:, k % 2, :], CSL[:, k, c:c + 1].to_broadcast([P, 1024]), ALU.mult)\
                    .then_inc(S("mod_done"), 1)

            def mod_add(acc, x, n):
                pool.wait_ge(S("mod_done"), n)
                pool.tensor_tensor(acc, acc, x, ALU.add).then_inc(S("mod_done"), 1)

            def mod_next(g, k, n):
                pool.wait_ge(S("mod_done"), n)
                pool.dma_start(modraw[:, k % 2, :], A["wmod"][g * KT + k + 2])\
                    .then_inc(S(f"mod_loaded{k % 2}"), 16)

            acc_of = lambda g: MODACC[:, g, :]
            for g in range(2):
                for k in range(KT):
                    n = g * 32 + (4 + 4 * k)
                    pool.wait_ge(S(f"mod_loaded{k % 2}"), g * 64 + 16 * (k // 2 + 1))
                    mod_product(MODTMP, k, 0, n)
                    mod_add(acc_of(g), MODTMP, n + 1)
                    mod_product(modraw[:, k % 2, :], k, 1, n + 2)
                    mod_add(acc_of(g + 2), modraw[:, k % 2, :], n + 3)
                    mod_next(g, k, n + 4)
            for u in range(U_PW1 + 2, U_PW1 + N_PW1 + 2):
                pool.wait_ge(S("hi_done"), u + 1)
                pool.wait_ge(S("lo_done"), u)
                pool.tensor_tensor(w_lo[:, u % SLOTS, :], raw[:, u % RAW_SLOTS, :], w_hi[:, u % SLOTS, :].bitcast(F32),
                                   ALU.subtract).then_inc(S("lo_done"), 1)
            pool.wait_ge(S("mod_sum"), 1)
            for n in range(4):
                pool.memset(MODACC[:, n, :], 0.0).then_inc(S("mod_done"), 1)

            def mod_group(g, last=False):
                for k in range(KT):
                    n = g * 16 + (72 + 2 * k)
                    pool.wait_ge(S(f"mod_loaded{k % 2}"), g * 64 + (128 + 16 * (k // 2 + 1)))
                    mod_product(modraw[:, k % 2, :], k, 0, n)
                    mod_add(acc_of(g), modraw[:, k % 2, :], n + 1)
                    if not (last and k >= KT - 2):
                        mod_next(g + 2, k, n + 2)

            for g in range(4):
                mod_group(g, g == 3)
    print("semaphores", len(sems))


def _tiles(a):
    k, n = a.shape
    return a.reshape(k // P, P, n // P, P).transpose(2, 0, 1, 3)


def _feature_units(blocks):
    b = np.stack(blocks)
    return b.reshape(-1, BLK, P, P).transpose(0, 2, 1, 3).reshape(-1, P, UNIT)


def _token_units(w):
    return w.reshape(KT, P, -1, 256).transpose(2, 1, 0, 3).reshape(-1, P, UNIT)


def _ffn_units(wg, wu, wd):
    g, u = _tiles(wg), _tiles(wu)
    d = wd.reshape(FT, P, KT, P).transpose(0, 2, 1, 3)
    gu = [_feature_units([g[f], u[f]])[0] for f in range(FT)]
    dn = [np.concatenate([d[2 * j], d[2 * j + 1]]).transpose(1, 0, 2).reshape(P, UNIT) for j in range(FT // 2)]
    out = [gu[0], gu[1]]
    for j in range(1, FT // 2):
        out += [gu[2 * j], gu[2 * j + 1], dn[j - 1]]
    return np.stack(out + [dn[-1]])


def _cols(a):
    return a.reshape(-1, P).T


def _constants():
    ones = np.ones((P, P), np.float32)
    blk = np.kron(np.eye(2, dtype=np.float32), np.ones((64, 64), np.float32))
    cst = np.concatenate([ones, blk, np.eye(P, dtype=np.float32)], 1)
    i = np.arange(P)
    after = (i[:, None] > i[None, :]).astype(np.float32)
    before = (i[:, None] < i[None, :]).astype(np.float32)
    csb = np.concatenate([after, before, ones, before], 1)
    masks = []
    for d in range(2):
        for m in LEVELS:
            pair, side = i // (2 * m), (i // m) % 2
            q, k = (1, 0) if d == 0 else (0, 1)
            masks.append((pair[:, None] == pair[None, :]) & (side[:, None] == k) & (side[None, :] == q))
    masks.append(np.eye(P, dtype=bool))
    lmask = np.concatenate([m.astype(np.float32) for m in masks], 1)
    f = np.arange(64)
    w = 2 * np.pi * np.outer(f, f) / 64
    e2 = np.eye(2)
    fd = np.concatenate([np.kron(e2, np.cos(w)), np.kron(e2, -np.sin(w))], 1).astype(np.float32)
    t = np.arange(T)
    w = 2 * np.pi * (np.outer(t, t) % T) / T
    ft = np.stack([np.cos(w), np.sin(w)]).reshape(2, 2, P, T).transpose(2, 0, 1, 3).reshape(P, -1).astype(np.float32)
    row, col = (np.arange(T) // 64).astype(np.float32), (np.arange(T) % 64).astype(np.float32)
    inv = (10000.0 ** (-np.arange(0, 32, 2, dtype=np.float32) / 32)).astype(np.float32)
    ar, ac = row[:, None] * inv, col[:, None] * inv
    ang = np.concatenate([ar, ar, ac, ac], 1).T
    cos, sin = (np.concatenate([g(ang)] * 2, 0).astype(np.float32) for g in (np.cos, np.sin))
    rot = np.zeros((64, 64), np.float32)
    for o in range(16):
        rot[16 + o, o] = -1.0
        rot[o, 16 + o] = 1.0
        rot[48 + o, 32 + o] = -1.0
        rot[32 + o, 48 + o] = 1.0
    rot = np.kron(np.eye(2, dtype=np.float32), rot)
    return cst, csb, np.concatenate([lmask, fd, ft, cos, sin, rot], 1)


def _lay_out(v):
    f = {k: np.asarray(a) for k, a in v.items()}
    w_in = f["hy_w_in"][0]
    c = np.cumsum([0, 256, 256, 512, 512, 16, 512, 512, 512])
    gq, gk, gv, gr, glr, sq, sk, sv = (w_in[:, a:b] for a, b in zip(c[:-1], c[1:]))
    fm = lambda *ws: _feature_units([t for w in ws for t in _tiles(w)])
    units = [_token_units(gv), fm(gk, gq, gr), _token_units(sv), fm(sk, sq), fm(f["hy_w_out"][0]),
             _ffn_units(f["ffn_w_gate"][0], f["ffn_w_up"][0], f["ffn_w_down"][0])]
    pw = _tiles(f["cv_w_pw1"][0])
    units += [_feature_units([t for j in range(8) for t in (pw[j], pw[8 + j])]), fm(f["cv_w_pw2"][0]),
              _ffn_units(f["ffn_w_gate"][1], f["ffn_w_up"][1], f["ffn_w_down"][1])]
    w2 = f["w_in_2"][0]
    c = np.cumsum([0, 256, 128, 64, 512, 512, 512, 256, 256, 256])
    cq, ckv, kr, hq, hff, hfb, hi, hg, fn = (w2[:, a:b] for a, b in zip(c[:-1], c[1:]))
    units += [fm(np.concatenate([ckv, kr, kr], 1), hff, hfb), _token_units(hi), fm(cq, hq, hg, fn),
              fm(f["w_out_2"][0])]
    gu = f["w_gate_up_2"][0]
    units += [_ffn_units(gu[:, :FT * P], gu[:, FT * P:], f["w_down_2"][0])]
    wstream = np.concatenate(units)
    cst, csb, cs2 = _constants()
    wf = f["w_fourier_2"][0].reshape(2, P, 256).transpose(1, 0, 2).reshape(P, 512)
    uq = f["w_uq_2"][0].reshape(256, 4, 192)
    uq = np.concatenate([uq[:, :, :128].reshape(256, 512), uq[:, :, 128:].reshape(256, 256)], 1)
    uq = uq.reshape(2, P, 768).transpose(1, 0, 2).reshape(P, 1536)
    ukv = f["w_ukv_2"][0].reshape(P, 4, 256)
    ukv = np.concatenate([ukv[:, :, :128].reshape(P, 512), ukv[:, :, 128:].reshape(P, 512)], 1)
    g2 = np.zeros((P, 256), np.float32)
    g2[:16] = f["hy_w_gate2"][0]
    cc = np.stack([_cols(f["c_2"][0]), _cols(f["c_ctx_2"])], 2).reshape(P, 16)
    par = np.concatenate([
        _cols(f["mix_norm"][0]), _cols(f["mix_norm"][1]), _cols(f["ffn_norm"][0]), _cols(f["ffn_norm"][1]),
        _cols(f["hy_gla_norm"][0]), _cols(np.tile(f["hy_sb_q_norm"][0], 2)), _cols(np.tile(f["hy_sb_k_norm"][0], 2)),
        _cols(f["hy_b_gate"][0]), _cols(f["cv_b_pw1"][0]), _cols(f["cv_b_dw"][0]), _cols(f["cv_ln_g"][0]),
        _cols(f["cv_ln_b"][0]), _cols(f["cv_b_pw2"][0]),
        f["cv_w_dw"][0].reshape(TAPS, KT, P).transpose(2, 1, 0).reshape(P, -1), cc, _cols(f["b_mod_2"][0]),
        _cols(f["norm1_g_2"][0]), _cols(f["norm2_g_2"][0]), _cols(f["q_norm_g_2"][0]), _cols(f["kv_norm_g_2"][0]),
        _cols(f["hg_norm_g_2"][0]), _cols(f["final_norm_g_2"]),
        glr.reshape(KT, P, 16).transpose(1, 0, 2).reshape(P, -1), g2], 1)
    act = lambda a: a[0].T.reshape(KT, P, T).transpose(1, 0, 2).reshape(P, KT * T)
    arrays = {
        "wstream": wstream, "wmod": f["w_mod_2"][0].reshape(KT, P, 6, 1024).transpose(2, 0, 1, 3).reshape(MODB, P, 1024),
        "xT": act(f["x"]), "ctxT": act(f["ctx_2"]), "par": par, "cst": cst, "csb": csb,
        "cst2": np.concatenate([cs2, wf], 1), "mlw": np.concatenate([uq, ukv], 1),
    }
    return {k: np.ascontiguousarray(a, dtype=np.float32) for k, a in arrays.items()}


def kernel(**inputs):
    import concourse.bacc as bacc
    from concourse import mybir
    from concourse.bass_utils import run_bass_kernel_spmd

    nc = bacc.Bacc("TRN2", target_bir_lowering=False, num_devices=1)
    arrays = _lay_out(inputs)
    A = {k: nc.dram_tensor(k, a.shape, mybir.dt.float32, kind="ExternalInput").ap() for k, a in arrays.items()}
    A["out"] = nc.dram_tensor("out", (P, KT * T), mybir.dt.float32, kind="ExternalOutput").ap()
    program(nc, A)
    r = run_bass_kernel_spmd(nc, [arrays], core_ids=[0])
    y = r.results[0]["out"]
    return np.ascontiguousarray(y.reshape(P, KT, T).transpose(1, 0, 2).reshape(D, T).T.reshape(1, T, D))
```

```python
from contextlib import ExitStack

import numpy as np

P = 128
D, T, KT = 1024, 256, 8
FT = 22
BLK = 16
UNIT = BLK * P
SLOTS, RAW_SLOTS = 3, 2
CHUNK = 64
TAPS = 31
EPS = 1e-6
N_IN1, N_OUT, N_PW1, N_IN2 = 12, 4, 8, 11
N_FFN = 33
MODB = 48
LEVELS = (32, 16, 8, 4, 2, 1)

U_IN1 = 0
U_OUT1 = U_IN1 + N_IN1
U_FFN = [U_OUT1 + N_OUT, 0, 0]
U_PW1 = U_FFN[0] + N_FFN
U_PW2 = U_PW1 + N_PW1
U_FFN[1] = U_PW2 + N_OUT
U_IN2 = U_FFN[1] + N_FFN
U_OUT2 = U_IN2 + N_IN2
U_FFN[2] = U_OUT2 + N_OUT
UNITS = U_FFN[2] + N_FFN

PAR = {}
_at = 0
for _name, _n in (("mixn0", 8), ("mixn1", 8), ("ffnn0", 8), ("ffnn1", 8), ("glan", 1), ("sbq", 1), ("sbk", 1),
                  ("bgate", 2), ("bpw1", 16), ("bdw", 8), ("lng", 8), ("lnb", 8), ("bpw2", 8), ("wdw", 8 * TAPS),
                  ("c2", 16), ("bmod", 48), ("n1g", 8), ("n2g", 8), ("qng", 2), ("kvg", 1), ("hgg", 2), ("fing", 8),
                  ("wglr", 8 * 16), ("wgate2", 256)):
    PAR[_name] = (_at, _n)
    _at += _n
N_PAR = _at

CST = {"ones": (0, 128), "blk": (128, 128), "ident": (256, 128)}
N_CST = 384
CSB = {"tri": (0, 128), "sbmask": (128, 384)}
N_CSB = 512
CS2 = {}
_at = 0
for _name, _n in (("lmask", 13 * 128), ("fd", 256), ("ft", 4 * 256), ("cos", 256), ("sin", 256), ("rot", 128),
                  ("wfou", 512)):
    CS2[_name] = (_at, _n)
    _at += _n
N_CS2 = _at
N_MLW = 2 * 768 + 1024


def program(nc, A):
    import concourse.bass as bass
    from concourse import mybir

    F32, F32R, BF16, I32 = mybir.dt.float32, mybir.dt.float32r, mybir.dt.bfloat16, mybir.dt.int32
    ACT, ALU, AX = mybir.ActivationFunctionType, mybir.AluOpType, mybir.AxisListType

    with ExitStack() as ctx:
        sems = {}

        def S(name):
            if name not in sems:
                sems[name] = ctx.enter_context(nc.semaphore(name))
            return sems[name]

        base = -(-nc.sbuf_base // 64) * 64

        def at(name, kib, cols, dt=F32, parts=P):
            return nc.alloc_sbuf_tensor_at(name, [parts, cols], dt, offset=base + int(kib * 1024))

        raw = at("raw", 0, RAW_SLOTS * UNIT)[:, :].rearrange("p (s n) -> p s n", s=RAW_SLOTS)
        w_hi = at("w_hi", 16, SLOTS * UNIT, F32R)[:, :].rearrange("p (s n) -> p s n", s=SLOTS)
        w_lo = at("w_lo", 40, SLOTS * UNIT, F32R)[:, :].rearrange("p (s n) -> p s n", s=SLOTS)
        X = at("X", 64, KT * T)[:, :].rearrange("p (k t) -> p k t", k=KT)
        a_hi = at("a_hi", 72, KT * 2 * T, F32R)[:, :].rearrange("p (k s t) -> p k s t", k=KT, s=2)
        a_lo = at("a_lo", 88, KT * 2 * T, F32R)[:, :].rearrange("p (k s t) -> p k s t", k=KT, s=2)
        SQ = at("SQ", 104, KT * T)[:, :].rearrange("p (k t) -> p k t", k=KT)
        HN = at("HN", 112, KT * T)[:, :].rearrange("p (k t) -> p k t", k=KT)
        h_hi = at("h_hi", 120, 4 * T, F32R)[:, :].rearrange("p (j f t) -> p j f t", j=2, f=2)
        h_lo = at("h_lo", 124, 4 * T, F32R)[:, :].rearrange("p (j f t) -> p j f t", j=2, f=2)
        GU = at("GU", 176, 4 * T)[:, :].rearrange("p (f t) -> p f t", f=2)
        SG = at("SG", 128, 2 * T)[:, :].rearrange("p (f t) -> p f t", f=2)
        HF = at("HF", 130, 2 * T)[:, :].rearrange("p (f t) -> p f t", f=2)
        RS = at("RS", 132, T)[:, :]
        RSC = at("RSC", 180, T)[:, :]
        par = at("par", 133, N_PAR)[:, :]
        cst = at("cst", 137, N_CST)[:, :]
        zero = at("zero", 138.5, 512, BF16)[:, :]
        modraw = at("modraw", 140, 2 * 1024)[:, :].rearrange("p (s n) -> p s n", s=2)
        MODACC = at("MODACC", 181, 4 * 1024)[:, :].rearrange("p (n f) -> p n f", n=4)
        MODTMP = at("MODTMP", 197, 1024)[:, :]
        MIX = at("MIX", 148, KT * T)[:, :].rearrange("p (k t) -> p k t", k=KT)
        cst2 = at("cst2", 190, N_CS2)[:, :]
        CSL = at("CSL", 206.5, 16)[:, :].rearrange("p (k c) -> p k c", c=2)
        MOD = at("MOD", 206.5625, 96)[:, :].rearrange("p (n c) -> p n c", c=2)
        GSC = at("GSC", 206.9375, 24)[:, :].rearrange("p (n k) -> p n k", k=8)

        def prm(name, i=0, n=1):
            return par[:, PAR[name][0] + i:PAR[name][0] + i + n]

        ones, blk, ident = (cst[:, CST[n][0]:CST[n][0] + 128] for n in ("ones", "blk", "ident"))

        def c2(name):
            return cst2[:, CS2[name][0]:CS2[name][0] + CS2[name][1]]

        PS = ctx.enter_context(nc.psum_tensor("PS", [P, 8, 512], F32))[:, :, :]

        def banks(a, b):
            return PS[:, a:b, :].rearrange("p b n -> p (b n)")

        PROJ = at("PROJ", 156, N_IN1 * 512)[:, :].rearrange("p (u n) -> p u n", u=N_IN1)
        QKN = at("QKN", 180, 4 * 512)[:, :]
        csb = at("csb", 188, N_CSB)[:, :]
        tri, sbmask = csb[:, 0:128], csb[:, 128:512]
        GLR = at("GLR", 131, T, F32, 16)[:, :]
        RESET = at("RESET", 120, 512)[:, :]
        LA = at("LA", 122, 512)[:, :]
        GE = at("GE", 124, 512)[:, :]
        CUM = at("CUM", 126, 512)[:, :]
        KEND = at("KEND", 128, 512)[:, :]
        KTOK = at("KTOK", 190, 512)[:, :]
        DEC = at("DEC", 192, 8)[:, :]
        ST = at("ST", 193, 1024)[:, :].rearrange("p (n a v) -> p n a v", n=4, a=2)
        OG = at("OG", 198, 1024)[:, :]
        OR = at("OR", 202, 1024)[:, :]
        RSG = at("RSG", 152, 1024)[:, :]
        SQF = at("SQF", 104, 2048)[:, :]
        RSF = at("RSF", 112, 2048)[:, :]
        SBZ = at("SBZ", 104, 3 * 768)[:, :].rearrange("p (g e n) -> p g e n", g=3, e=2)
        SBL = at("SBL", 114, 2 * 768)[:, :].rearrange("p (g e n) -> p g e n", g=2, e=2)
        SBK = at("SBK", 121, 768)[:, :].rearrange("p (e n) -> p e n", e=2)
        SBM = at("SBM", 125, 2 * 768)[:, :].rearrange("p (g e n) -> p g e n", g=2, e=2)
        PE_TILES = (5, 6, 7)
        RING = 24
        DG = at("DG", 120, RING * P)[:, :].rearrange("p (n m) -> p n m", n=RING)
        PADT = T + 32
        CU = at("CU", 156, KT * PADT)[:, :].rearrange("p (k t) -> p k t", k=KT)
        PWR = at("PWR", 177, 4 * T)[:, :].rearrange("p (f t) -> p f t", f=2)
        SIG = at("SIG", 166, 2 * T)[:, :].rearrange("p (f t) -> p f t", f=2)
        CTX = at("CTX", 168, KT * T)[:, :].rearrange("p (k t) -> p k t", k=KT)
        MU = at("MU", 176, T)[:, :]
        ZF = at("ZF", 156, 4096)[:, :].rearrange("p (d s h t) -> p d s h t", d=2, s=2, h=4)
        XO = at("XO", 172, 10 * T)[:, :].rearrange("p (n t) -> p n t", n=10)
        CKV = at("CKV", 182, 1024)[:, :].rearrange("p (n t) -> p n t", n=2)
        HI = at("HI", 186, 1024)[:, :].rearrange("p (s t n) -> p (s t) n", s=2, t=2)
        mlw = at("mlw", 140, N_MLW)[:, :]
        QN = at("QN", 16, 1024)[:, :].rearrange("p (h t) -> p h t", h=4)
        QP = at("QP", 20, 512)[:, :]
        QR = at("QR", 22, 512)[:, :]
        KPE = at("KPE", 24, 512)[:, :]
        CKN = at("CKN", 120, 512)[:, :]
        KN = at("KN", 28, 2048)[:, :].rearrange("p (h t) -> p h t", h=4)
        VT = at("VT", 36, 2048)[:, :].rearrange("p (t n) -> p t n", t=4)
        PR = at("PR", 44, 1024)[:, :].rearrange("p (b t) -> p b t", b=2)
        PT = at("PT", 48, 1024)[:, :].rearrange("p (b t) -> p b t", b=2)
        SQ2 = at("SQ2", 120, 1024)[:, :]
        RS2 = at("RS2", 150, 1024)[:, :]
        FC = at("FC", 60, 1024)[:, :]
        MXS = at("MXS", 136.75, 32)[:, :]
        CQN = at("CQN", 124, 512)[:, :].rearrange("p (k t) -> p k t", k=2)
        FM = at("FM", 126, 512)[:, :].rearrange("p (k t) -> p k t", k=2)
        GG = [at(f"GG{d}", o, 2048)[:, :].rearrange("p (s h t) -> p s h t", s=2, h=4) for d, o in enumerate((104, 104))]
        KK = [at(f"KK{d}", o, 2048)[:, :].rearrange("p (s h t) -> p s h t", s=2, h=4) for d, o in enumerate((112, 32))]
        CC = [at(f"CC{d}", o, 2048)[:, :].rearrange("p (s h t) -> p s h t", s=2, h=4) for d, o in enumerate((72, 56))]
        KWT = at("KWT", 96, 2048)[:, :].rearrange("p (t h k) -> p t h k", t=4, h=4)
        SX = at("SX", 24, 2048)[:, :].rearrange("p (d n m) -> p d n m", d=2, n=4)
        QF = at("QF", 80, 2048)[:, :].rearrange("p (d m) -> p d m", d=2)
        KS = at("KS", 120, 1024)[:, :]
        SC = at("SC", 124, 1024)[:, :]
        QQ = at("QQ", 128, 1024)[:, :]
        EX = at("EX", 140, 2048)[:, :].rearrange("p (b m) -> p b m", b=2)
        QM0 = at("QM0", 48, 1024)[:, :]
        KM0 = at("KM0", 52, 1024)[:, :]
        AD = at("AD", 136.5, 64)[:, :].rearrange("p (d m) -> p d m", d=2)
        STT = at("STT", 152, T)[:, :]
        STU = at("STU", 153, T)[:, :]
        RST64 = at("RST64", 132, T)[:, :]
        assert 133 + N_PAR * 4 / 1024 <= 136.5

        def QMd(d):
            return ZF[:, d, 0, :, :].rearrange("p h t -> p (h t)")

        def KMd(d):
            return ZF[:, d, 1, :, :].rearrange("p h t -> p (h t)")

        SQO = at("SQO", 140, 512)[:, :]
        OH = at("OH", 142, 512)[:, :]
        RSO = at("RSO", 146, 512)[:, :]

        def fl(ap):
            return ap.rearrange("p s h t -> p (s h t)")

        OA = MIX[:, 0:4, :].rearrange("p k t -> p (k t)")

        def raw_ap(u):
            return A["wstream"][bass.ds(u, 1)].rearrange("a p n -> (a p) n")

        def split_hi(act, u, slot, rslot, n):
            act.wait_ge(S(f"raw_loaded{rslot}"), n * 16)
            if not (isinstance(u, int) and u < SLOTS):
                act.wait_ge(S("unit_done"), u - (SLOTS - 1))
            nc.scalar.activation(w_hi[:, slot, :], raw[:, rslot, :], ACT.Copy).then_inc(S("hi_done"), 1)

        def split_lo(dve, u, slot, rslot):
            dve.wait_ge(S("hi_done"), u + 1)
            dve.tensor_tensor(w_lo[:, slot, :], raw[:, rslot, :], w_hi[:, slot, :].bitcast(F32),
                              ALU.subtract).then_inc(S("lo_done"), 1)

        def hi(act, u):
            if u < UNITS:
                split_hi(act, u, u % SLOTS, u % RAW_SLOTS, u // RAW_SLOTS + 1)

        def lo(dve, u):
            if u < UNITS:
                split_lo(dve, u, u % SLOTS, u % RAW_SLOTS)

        def split_mm(out, H, L, xh, xl, start, stop, **kw):
            nc.tensor.matmul(out, H, xh, start=start, stop=False, **kw)
            nc.tensor.matmul(out, H, xl, start=False, stop=False, **kw)
            return nc.tensor.matmul(out, L, xh, start=False, stop=stop, **kw)

        def wblk(slot, b):
            return w_hi[:, slot, b * P:(b + 1) * P], w_lo[:, slot, b * P:(b + 1) * P]

        def feature_unit(slot, outs, src, wait_k=None):
            for nb in range(2):
                for k in range(KT):
                    if nb == 0 and wait_k is not None:
                        wait_k(k)
                    H, L = wblk(slot, nb * KT + k)
                    last = split_mm(outs[nb], H, L, a_hi[:, k, src, :], a_lo[:, k, src, :], k == 0, k == KT - 1)
            return last

        def token_unit(slot, outs):
            for s, t, out in outs:
                for k in range(KT):
                    wh, wl = (w[:, slot, k * 256:(k + 1) * 256] for w in (w_hi, w_lo))
                    xh, xl = (a[:, k, s, t * P:(t + 1) * P] for a in (a_hi, a_lo))
                    nc.tensor.matmul(out, xh, wh, start=k == 0, stop=False)
                    nc.tensor.matmul(out, xl, wh, start=False, stop=False)
                    last = nc.tensor.matmul(out, xh, wl, start=False, stop=k == KT - 1)
            return last

        NORMS = ["mix0", "ffn0", "mix1", "ffn1", "ctx", "mix2", "ffn2", "final"]

        def norm_src(n):
            return CTX if NORMS[n] == "ctx" else X

        def wait_x(eng, n, j):
            if n == 0:
                eng.wait_ge(S("x_loaded"), 16)
            elif NORMS[n] == "ctx":
                eng.wait_ge(S("ctx_loaded"), 16)
            else:
                eng.wait_ge(S("x_updated"), 4 * (RES[n]) + j + 1)

        FOLDED = {1: "ffnn0", 2: "mixn1", 3: "ffnn1"}
        HALF = {1: 1, 2: 0, 3: 0}
        NORM_HN = {0: 0, 4: 1, 5: 2, 6: 3, 7: 4}
        RES = {1: 0, 2: 1, 3: 2, 5: 3, 6: 4, 7: 5}

        LN_EXP, SILU, SIGMOID = "natural_log_exp_and_others", "silu_and_others", "sigmoid_and_others"

        def table(name):
            nc.scalar.preload_act_table_set(name)

        def norm_factor(act, n, after):
            act.wait_ge(S("norm_ss"), n + 1)
            rs = RSC if NORMS[n] == "ctx" else RS
            nc.scalar.activation(rs, PS[:, 6, 0:T], ACT.Ln, scale=1.0 / D, bias=prm_eps).then_inc(S("norm_ln"), 1)
            act.wait_ge(S("norm_ln"), n + 1)
            nc.scalar.activation(rs, rs, ACT.Exp, scale=-0.5).then_inc(S("norm_rs"), 1)
            if after:
                table(after)

        def norm_act(act, n, shift=None, split=True, before=None, after=None, meanwhile=None):
            x = norm_src(n)
            if before:
                table(before)
            for j in range(4):
                wait_x(act, n, j)
                nc.scalar.activation(SQ[:, 2 * j:2 * j + 2, :], x[:, 2 * j:2 * j + 2, :], ACT.Square)\
                    .then_inc(S("norm_sq"), 1)
            if meanwhile:
                meanwhile()
            norm_factor(act, n, after)
            if not split:
                return
            s = 1 if NORMS[n] == "ctx" else 0
            for j in range(4):
                act.wait_ge(S("norm_hn"), 8 * NORM_HN[n] + 2 * j + 2)
                if shift is None:
                    nc.scalar.activation(a_hi[:, 2 * j:2 * j + 2, s, :], HN[:, 2 * j:2 * j + 2, :], ACT.Copy)\
                        .then_inc(S("norm_hi"), 1)
                else:
                    for k in (2 * j, 2 * j + 1):
                        i = nc.scalar.activation(a_hi[:, k, s, :], HN[:, k, :], ACT.Identity, bias=shift(k))
                    i.then_inc(S("norm_hi"), 1)

        def folded_act(act, n, before=None, after=None):
            g = prm(FOLDED[n], 0, KT)
            if before:
                table(before)
            for j in range(4):
                wait_x(act, n, j)
                for k in (2 * j, 2 * j + 1):
                    i = nc.scalar.activation(a_hi[:, k, HALF[n], :], X[:, k, :], ACT.Copy, scale=g[:, k:k + 1])
                i.then_inc(S("norm_hi"), 1)
                nc.scalar.activation(SQ[:, 2 * j:2 * j + 2, :], X[:, 2 * j:2 * j + 2, :], ACT.Square)\
                    .then_inc(S("norm_sq"), 1)
            norm_factor(act, n, after)

        def folded_lo(dve, n, j):
            g, s = prm(FOLDED[n], 0, KT), HALF[n]
            dve.wait_ge(S("norm_hi"), 4 * n + j + 1)
            for k in (2 * j, 2 * j + 1):
                i = dve.scalar_tensor_tensor(a_lo[:, k, s, :], X[:, k, :], g[:, k:k + 1], a_hi[:, k, s, :].bitcast(F32),
                                             ALU.mult, ALU.subtract)
            i.then_inc(S("act_lo"), 1)

        def norm_pe(pe, n):
            for k in range(KT):
                pe.wait_ge(S("norm_sq"), 4 * n + k // 2 + 1)
                if k == 0 and n > 0:
                    pe.wait_ge(S("norm_rs"), n)
                i = nc.tensor.matmul(PS[:, 6, 0:T], ones, SQ[:, k, :], start=k == 0, stop=k == KT - 1)
            i.then_inc(S("norm_ss"), 1)

        def norm_dve(dve, n, gain, shift=None, split=True):
            x = norm_src(n)
            dve.wait_ge(S("norm_rs"), n + 1)
            rs = RSC if NORMS[n] == "ctx" else RS
            for k in range(KT):
                dve.scalar_tensor_tensor(HN[:, k, :], x[:, k, :], gain(k), rs, ALU.mult, ALU.mult)\
                    .then_inc(S("norm_hn"), 1)
            if not split:
                return
            s = 1 if NORMS[n] == "ctx" else 0
            for j in range(4):
                dve.wait_ge(S("norm_hi"), 4 * (n) + j + 1)
                ks = slice(2 * j, 2 * j + 2)
                if shift is None:
                    dve.tensor_tensor(a_lo[:, ks, s, :], HN[:, ks, :], a_hi[:, ks, s, :].bitcast(F32), ALU.subtract)\
                        .then_inc(S("act_lo"), 1)
                else:
                    for k in (2 * j, 2 * j + 1):
                        i = dve.scalar_tensor_tensor(a_lo[:, k, s, :], HN[:, k, :], shift(k),
                                                     a_hi[:, k, s, :].bitcast(F32), ALU.add, ALU.subtract)
                    i.then_inc(S("act_lo"), 1)

        ACT_LO = {"mix0": 0, "o1": 4, "ffn0": 8, "mix1": 12, "cv": 16, "ffn1": 20, "ctx": 24, "mix2": 28, "o2": 32,
                  "ffn2": 36}

        def wait_act(pe, event, k):
            pe.wait_ge(S("act_lo"), ACT_LO[event] + k // 2 + 1)

        def mix_split_act(act, m, ready, quarters=range(4)):
            for j in quarters:
                ready(act, j)
                nc.scalar.activation(a_hi[:, 2 * j:2 * j + 2, 0, :], MIX[:, 2 * j:2 * j + 2, :], ACT.Copy)\
                    .then_inc(S("mix_hi"), 1)

        def mix_split_dve(dve, m, quarters=range(4)):
            for j in quarters:
                ks = slice(2 * j, 2 * j + 2)
                dve.wait_ge(S("mix_hi"), 4 * m + j + 1)
                dve.tensor_tensor(a_lo[:, ks, 0, :], MIX[:, ks, :], a_hi[:, ks, 0, :].bitcast(F32), ALU.subtract)\
                    .then_inc(S("act_lo"), 1)

        def out_units_pe(pe, u0, event, update, src=0):
            for j in range(N_OUT):
                u = u0 + j
                pe.wait_ge(S("lo_done"), u + 1)
                if j >= 2:
                    pe.wait_ge(S("x_updated"), 4 * update + j - 1)
                outs = [PS[:, 4 + j % 2, nb * T:(nb + 1) * T] for nb in range(2)]
                feature_unit(u % SLOTS, outs, src, (lambda k: wait_act(pe, event, k)) if j == 0 else None)\
                    .then_inc(S("unit_done"), 1)

        PAIRS = FT // 2

        def ffn_pe(pe, f, event, norm=None, behind=None):
            u0 = U_FFN[f]
            if f:
                pe.wait_ge(S("x_updated"), 4 * (2 * f - 1) + 4)
            for b in range(4):
                nc.tensor.matmul(PS[:, b, :], zero[:, 0:P], zero, start=True, stop=True)

            def gate_up(u, slot, fb, j, first=False):
                pe.wait_ge(S("lo_done"), u + 1)
                if j is not None:
                    pe.wait_ge(S("gu_done" if norm else "hf_done"), (j - 1 + f * PAIRS) * 2 + fb + 1)
                outs = [PS[:, 4 + fb, g * T:(g + 1) * T] for g in range(2)]
                feature_unit(slot, outs, HALF[norm] if norm else 0,
                             (lambda k: wait_act(pe, event, k)) if first else None)\
                    .then_inc(S("unit_done"), 1)

            def down(u, slot, j, par_):
                pe.wait_ge(S("lo_done"), u + 1)
                for kk in range(2):
                    pe.wait_ge(S("h_lo_done"), (j + f * PAIRS) * 2 + kk + 1)
                    for nb in range(KT):
                        H, L = wblk(slot, kk * KT + nb)
                        i = split_mm(PS[:, nb // 2, (nb % 2) * T:(nb % 2 + 1) * T], H, L, h_hi[:, par_, kk, :],
                                     h_lo[:, par_, kk, :], False, False, skip_group_check=True)
                i.then_inc(S("unit_done"), 1)

            if norm:
                pe.wait_ge(S("x_updated"), 4 * RES[norm] + 3)
            gate_up(u0, u0 % SLOTS, 0, None, True)
            if norm:
                pe.wait_ge(S("x_updated"), 4 * RES[norm] + 4)
                norm_pe(pe, norm)
            gate_up(u0 + 1, (u0 + 1) % SLOTS, 1, None)
            if behind:
                norm_pe(pe, behind)
            with pe.Fori(0, (PAIRS - 1) // 2) as i:
                for r in range(2):
                    for q in range(3):
                        u = i * 6 + (u0 + 2 + 3 * r + q)
                        slot = (u0 + 2 + 3 * r + q) % SLOTS
                        if q < 2:
                            gate_up(u, slot, q, i * 2 + (1 + r))
                        else:
                            down(u, slot, i * 2 + r, r)
            down(u0 + N_FFN - 1, (u0 + N_FFN - 1) % SLOTS, PAIRS - 1, (PAIRS - 1) % 2)

        def ffn_act(act, f, folded=False, behind=None):
            u0 = U_FFN[f]

            def evac(u, fb, par_, j):
                if folded:
                    act.wait_ge(S("gu_done"), (j + f * PAIRS) * 2 + fb + 1)
                    nc.scalar.activation(SG[:, fb, :], GU[:, fb, 0:T], ACT.Silu).then_inc(S("silu_done"), 1)
                else:
                    act.wait_ge(S("unit_done"), u + 1)
                    nc.scalar.activation(SG[:, fb, :], PS[:, 4 + fb, 0:T], ACT.Silu).then_inc(S("silu_done"), 1)
                act.wait_ge(S("hf_done"), (j + f * PAIRS) * 2 + fb + 1)
                nc.scalar.activation(h_hi[:, par_, fb, :], HF[:, fb, :], ACT.Copy).then_inc(S("h_hi_done"), 1)

            if behind:
                hi(act, u0 + 2)
                hi(act, u0 + 3)
                behind()
            for q in range(2):
                if not behind:
                    hi(act, u0 + q + 2)
                evac(u0 + q, q, 0, 0)
            def turn(i):
                for r in range(2):
                    for q in range(3):
                        v = u0 + 2 + 3 * r + q
                        w = v + 2
                        if not (isinstance(i, int) and i * 6 + w >= UNITS):
                            split_hi(act, i * 6 + w, w % SLOTS, w % RAW_SLOTS, i * 3 + (w // RAW_SLOTS + 1))
                        if q < 2:
                            evac(i * 6 + v, q, (1 + r) % 2, i * 2 + (1 + r))

            turns = (PAIRS - 1) // 2
            with act.Fori(0, turns - 1) as i:
                turn(i)
            turn(turns - 1)
            hi(act, u0 + N_FFN + 1)

        def ffn_dve(dve, f, gate=None, folded=False, behind=None, between=None):
            u0 = U_FFN[f]

            def scaled(u, fb, j):
                if folded:
                    dve.wait_ge(S("unit_done"), u + 1)
                    if isinstance(j, int) and j == 0 and fb == 0:
                        dve.wait_ge(S("norm_rs"), 2 * f + 2)
                    dve.tensor_tensor(GU[:, fb, :].rearrange("p (a t) -> p a t", a=2),
                                      PS[:, 4 + fb, :].rearrange("p (a t) -> p a t", a=2),
                                      RS.unsqueeze(1).to_broadcast([P, 2, T]), ALU.mult).then_inc(S("gu_done"), 1)

            def evac(u, fb, par_, j, scale=True):
                n = (j + f * PAIRS) * 2 + fb + 1
                if scale:
                    scaled(u, fb, j)
                up = GU[:, fb, T:2 * T] if folded else PS[:, 4 + fb, T:2 * T]
                dve.wait_ge(S("silu_done"), n)
                dve.tensor_tensor(HF[:, fb, :], SG[:, fb, :], up, ALU.mult).then_inc(S("hf_done"), 1)
                dve.wait_ge(S("h_hi_done"), n)
                dve.tensor_tensor(h_lo[:, par_, fb, :], HF[:, fb, :], h_hi[:, par_, fb, :].bitcast(F32),
                                  ALU.subtract).then_inc(S("h_lo_done"), 1)

            for q in range(2):
                lo(dve, u0 + q + 2)
                scaled(u0 + q, q, 0)
                if not between:
                    evac(u0 + q, q, 0, 0, False)
            if between:
                between()
                for q in range(2):
                    evac(u0 + q, q, 0, 0, False)
            def turn(i):
                for r in range(2):
                    for q in range(3):
                        v = u0 + 2 + 3 * r + q
                        w = v + 2
                        if not (isinstance(i, int) and i * 6 + w >= UNITS):
                            split_lo(dve, i * 6 + w, w % SLOTS, w % RAW_SLOTS)
                        if q < 2:
                            evac(i * 6 + v, q, (1 + r) % 2, i * 2 + (1 + r))

            turns = (PAIRS - 1) // 2
            with dve.Fori(0, turns - 1) as i:
                turn(i)
            turn(turns - 1)
            lo(dve, u0 + N_FFN + 1)
            dve.wait_ge(S("unit_done"), u0 + N_FFN)
            for j in range(4):
                if gate is None:
                    ks = slice(2 * j, 2 * j + 2)
                    dve.tensor_tensor(X[:, ks, :], X[:, ks, :], PS[:, j, :].rearrange("p (k t) -> p k t", k=2),
                                      ALU.add).then_inc(S("x_updated"), 1)
                    if behind is not None and j:
                        folded_lo(dve, behind, j - 1)
                else:
                    for e in range(2):
                        k = 2 * j + e
                        i = dve.scalar_tensor_tensor(X[:, k, :], PS[:, j, e * T:(e + 1) * T], gate(k), X[:, k, :],
                                                     ALU.mult, ALU.add)
                    i.then_inc(S("x_updated"), 1)
            if behind is not None:
                folded_lo(dve, behind, 3)

        epsc = at("epsc", 207.1875, 2)[:, :]
        prm_eps = epsc[:, 0:1]

        QK_BANK = (6, 6, 4, 5)
        TAP_GAP = 12

        def half(e):
            return slice(64 * e, 64 * e + 64)

        block = ctx.enter_context(nc.Block())

        @block.sync
        def _(sp):
            sp.dma_start(X.rearrange("p k t -> p (k t)"), A["xT"]).then_inc(S("x_loaded"), 16)
            for u in range(RAW_SLOTS):
                sp.dma_start(raw[:, u, :], raw_ap(u)).then_inc(S(f"raw_loaded{u}"), 16)
            with sp.Fori(0, UNITS // RAW_SLOTS - 1) as i:
                for s in range(RAW_SLOTS):
                    sp.wait_ge(S("lo_done"), i * RAW_SLOTS + (s + 1))
                    sp.dma_start(raw[:, s, :], raw_ap(i * RAW_SLOTS + (RAW_SLOTS + s)))\
                        .then_inc(S(f"raw_loaded{s}"), 16)
            sp.wait_ge(S("norm_hn"), 8 * len(NORM_HN))
            sp.dma_start(A["out"], HN.rearrange("p k t -> p (k t)")).then_inc(S("out_stored"), 16)
            sp.wait_ge(S("out_stored"), 16)

        @block.tensor
        def _(pe):
            def mod_sums(part):
                pe.wait_ge(S("mod_done"), (68, 136)[part])
                for n in range(4):
                    for b in range(8):
                        m, c = ((n % 2) * 8 + b, n // 2) if part == 0 else (16 + n * 8 + b, 0)
                        i = nc.tensor.matmul(PS[:, 7, 2 * m + c:2 * m + c + 1], MODACC[:, n, b * P:(b + 1) * P],
                                             ones[:, 0:1], start=True, stop=True)
                i.then_inc(S("mod_sum"), 1)

            pe.wait_ge(S("cst_loaded"), 16)
            pe.wait_ge(S("memset_done"), 3)
            norm_pe(pe, 0)
            pe.wait_ge(S("par_loaded"), 16)
            for k in range(KT):
                pe.wait_ge(S("norm_hn"), k + 1)
                i = nc.tensor.matmul(PS[0:16, 3, 0:T], par[:, PAR["wglr"][0] + 16 * k:PAR["wglr"][0] + 16 * k + 16],
                                     HN[:, k, :], start=k == 0, stop=k == KT - 1)
            i.then_inc(S("glr_mm"), 1)

            def in1(u):
                pe.wait_ge(S("lo_done"), u + 1)
                if u == 0:
                    pe.wait_ge(S("act_lo"), 4)
                if u >= 2:
                    pe.wait_ge(S(f"proj{u % 2}_copied"), u // 2)
                outs = [PS[:, 4 + u % 2, t * T:(t + 1) * T] for t in range(2)]
                if u in (0, 1, 6, 7):
                    last = token_unit(u % SLOTS, [(0, t, outs[t]) for t in range(2)])
                else:
                    last = feature_unit(u % SLOTS, outs, 0)
                last.then_inc(S("unit_done"), 1)

            def qk_ss(j):
                pe.wait_ge(S("qk_sq"), j + 1)
                if j == 0:
                    pe.wait_ge(S("norm_rs"), 1)
                if j == 1:
                    pe.wait_ge(S("qk_rs"), 1)
                if j >= 2:
                    pe.wait_ge(S(f"proj{j % 2}_copied"), 6)
                nc.tensor.matmul(PS[:, QK_BANK[j], :], blk, SQF[:, j * 512:(j + 1) * 512], start=True, stop=True)\
                    .then_inc(S("qk_ss"), 1)

            for u in range(6):
                in1(u)
            pe.wait_ge(S("glr_done"), 1)
            for a in range(2):
                i = nc.tensor.matmul(PS[:, 3, a * T:(a + 1) * T],
                                     par[0:16, PAR["wgate2"][0] + a * P:PAR["wgate2"][0] + (a + 1) * P],
                                     GLR, start=True, stop=True)
            i.then_inc(S("gate_mm"), 1)
            in1(6)
            in1(7)
            pe.wait_ge(S("kend_done"), 1)
            for t in range(2):
                for a in range(2):
                    i = nc.tensor.transpose(PS[:, 2, (t * 2 + a) * P:(t * 2 + a + 1) * P],
                                            KEND[:, a * T + t * P:a * T + (t + 1) * P], ident)
            i.then_inc(S("ktok_mm"), 1)
            in1(8)
            pe.wait_ge(S("ktok_done"), 1)
            for n in range(4):
                for h in range(4):
                    r = half(n % 2)
                    i = nc.tensor.matmul(
                        PS[half(h % 2), n % 2, ((n // 2) * 2 + h // 2) * P:((n // 2) * 2 + h // 2 + 1) * P],
                        KTOK[r, (n // 2) * T + h * 64:(n // 2) * T + h * 64 + 64],
                        PROJ[r, h // 2, (n // 2) * T + (h % 2) * P:(n // 2) * T + (h % 2 + 1) * P],
                        start=True, stop=True)
            i.then_inc(S("upd_mm"), 1)
            in1(9)
            pe.wait_ge(S("gate_read"), 3)
            for n in range(4):
                pe.wait_ge(S("state_done"), 2 * n + 2)
                for h in range(4):
                    i = nc.tensor.matmul(PS[:, 2 + h % 2, (h // 2) * T + n * 64:(h // 2) * T + n * 64 + 64],
                                         ST[half(h % 2), n, h // 2, :],
                                         PROJ[half(h % 2), 3, (h // 2) * T + n * 64:(h // 2) * T + n * 64 + 64],
                                         start=True, stop=True)
            i.then_inc(S("og_mm"), 1)
            qk_ss(0)
            in1(10)
            pe.wait_ge(S("og_sq"), 1)
            for e in range(2):
                i = nc.tensor.matmul(PS[:, e, :], ones, OR[:, e * 512:(e + 1) * 512], start=True, stop=True)
            i.then_inc(S("og_ss"), 1)
            qk_ss(1)
            in1(11)
            qk_ss(2)
            qk_ss(3)

            def sb_z(g):
                if g == 0:
                    pe.wait_ge(S("qkn_done"), 3)
                    pe.wait_ge(S("og_rs"), 1)
                if g == 1:
                    pe.wait_ge(S("og_done"), 1)
                if g == 2:
                    pe.wait_ge(S("qkn_done"), 4)
                if g >= 2:
                    pe.wait_ge(S("sb_v"), 3 * g - 3)
                for e in range(2):
                    r, b = half(e), 2 * (g % 2) + e
                    kT, qT = QKN[r, g * T:(g + 1) * T], QKN[r, 1024 + g * T:1024 + (g + 1) * T]
                    nc.tensor.matmul(PS[:, b, 0:256], kT[:, 0:P], qT, start=True, stop=True)
                    i = nc.tensor.matmul(PS[:, b, 256:384], kT[:, P:T], qT[:, P:T], start=True, stop=True)
                i.then_inc(S("sb_z"), 1)

            def sb_between(g):
                pe.wait_ge(S("sb_keep"), g + 1)
                if g == 0:
                    pe.wait_ge(S("qk_rs"), 7)
                else:
                    pe.wait_ge(S("sb_lz2"), g)
                for e in range(2):
                    nc.tensor.matmul(PS[:, 4 + e, 0:384], tri, SBM[:, g % 2, e, :], start=True, stop=False)
                    i = nc.tensor.matmul(PS[:, 4 + e, 128:256], ones, SBM[:, g % 2, e, 256:384],
                                         start=False, stop=True)
                i.then_inc(S("sb_between"), 1)

            def sb_out(g):
                pe.wait_ge(S("sb_w"), g + 1)
                if g:
                    pe.wait_ge(S("sb_o_read"), g)
                for e in range(2):
                    hcol = (g * 2 + e) * 64
                    v = [PROJ[:, 6 + hcol // 256, t * T + hcol % 256:t * T + hcol % 256 + 64] for t in range(2)]
                    nc.tensor.matmul(PS[half(e), 6, 0:256], v[0], SBZ[:, g % 3, e, 0:256], start=True, stop=False)
                    i = nc.tensor.matmul(PS[half(e), 6, 128:256], v[1], SBZ[:, g % 3, e, 256:384],
                                         start=False, stop=True)
                i.then_inc(S("sb_o"), 1)

            sb_z(0)
            sb_z(1)
            for g in range(6):
                if g < 4:
                    sb_between(g)
                if g < 2:
                    sb_z(g + 2)
                if 1 <= g < 5:
                    sb_out(g - 1)
            pe.wait_ge(S("sb_lz2"), 4)
            out_units_pe(pe, U_OUT1, "o1", 0)
            ffn_pe(pe, 0, "ffn0", 1)
            for j in range(N_PW1):
                u = U_PW1 + j
                pe.wait_ge(S("lo_done"), u + 1)
                if j >= 2:
                    pe.wait_ge(S("pw_done"), j - 1)
                outs = [PS[:, 4 + j % 2, g * T:(g + 1) * T] for g in range(2)]
                feature_unit(u % SLOTS, outs, 0, (lambda k: wait_act(pe, "mix1", k)) if j == 0 else None)\
                    .then_inc(S("unit_done"), 1)
                if j == 0:
                    norm_pe(pe, 2)
            for nth, k in enumerate(PE_TILES):
                pe.wait_ge(S("cu_done"), k + 1)
                for j in range(TAPS):
                    n = nth * TAPS + j
                    pe.wait_ge(S("diag_built"), n + 1)
                    nc.tensor.matmul(PS[:, nth, 0:T], DG[:, n % RING, :], CU[:, k, j:j + T], start=j == 0,
                                     stop=j == TAPS - 1).then_inc(S("diag_used"), 1)
            for k in range(KT):
                if k in PE_TILES:
                    pe.wait_ge(S("cv_pe_done"), PE_TILES.index(k) + 1)
                elif k in (0, 2):
                    pe.wait_ge(S("tap_done"), (2 if k == 0 else 5) * TAPS)
                i = nc.tensor.matmul(PS[:, 6, 0:T], ones, HN[:, k, :], start=k == 0, stop=k == KT - 1)
            i.then_inc(S("ln_sum"), 1)
            for k in range(KT):
                pe.wait_ge(S("ln_sq"), k // 4 + 1)
                i = nc.tensor.matmul(PS[:, 6, T:2 * T], ones, SQ[:, k, :], start=k == 0, stop=k == KT - 1)
            i.then_inc(S("ln_ss"), 1)
            mod_sums(0)
            out_units_pe(pe, U_PW2, "cv", 2, 1)
            ffn_pe(pe, 1, "ffn1", 3, 4)
            norm_pe(pe, 5)
            mod_sums(1)
            pe.wait_ge(S("x_updated"), 16)
            for j in range(5):
                u = U_IN2 + j
                pe.wait_ge(S("lo_done"), u + 1)
                if j >= 2:
                    pe.wait_ge(S("in2_read"), j - 1)
                if j == 0:
                    pe.wait_ge(S("act_lo"), ACT_LO["mix2"] + 4)
                b = 2 * (j % 2)
                feature_unit(u % SLOTS, [PS[:, b + nb, :].rearrange("p (s t) -> p s t", s=2) for nb in range(2)],
                             slice(0, 2)).then_inc(S("unit_done"), 1)
            pe.wait_ge(S("lo_done"), U_IN2 + 6)
            pe.wait_ge(S("in2_read"), 4)
            token_unit((U_IN2 + 5) % SLOTS, [(s, t, PS[:, 2 + s, t * T:(t + 1) * T]) for s in range(2)
                                             for t in range(2)]).then_inc(S("unit_done"), 1)
            for j in range(5):
                u = U_IN2 + 6 + j
                pe.wait_ge(S("lo_done"), u + 1)
                if j >= 2:
                    pe.wait_ge(S("in2_read"), 6 + j - 1)
                feature_unit(u % SLOTS, [PS[:, 4 + j % 2, nb * T:(nb + 1) * T] for nb in range(2)], 0)\
                    .then_inc(S("unit_done"), 1)
                if j == 3:
                    pe.wait_ge(S("ml_sq"), 1)
                    pe.wait_ge(S("norm_rs"), 6)
                    pe.wait_ge(S("modv"), 4)
                    for k in range(2):
                        nc.tensor.matmul(PS[:, 6, 0:T], ones, SQ2[:, k * T:(k + 1) * T], start=k == 0, stop=k == 1)
                    nc.tensor.matmul(PS[:, 7, :], ones, SQ2[:, 512:1024], start=True, stop=True)\
                        .then_inc(S("ml_ss"), 1)

            pe.wait_ge(S("in2_read"), 11)
            pe.wait_ge(S("cst2_loaded"), 16)
            fd = c2("fd")
            for t in range(2):
                for a in range(2):
                    i = nc.tensor.matmul(PS[:, t, a * T:(a + 1) * T], XO[:, 8 + a, t * P:(t + 1) * P], fd,
                                         start=True, stop=True)
            i.then_inc(S("fn_mm"), 1)
            pe.wait_ge(S("mlw_loaded"), 16)
            pe.wait_ge(S("ml_n"), 2)
            uq = mlw[:, 0:1536].rearrange("p (k n) -> p k n", k=2)
            ukv = mlw[:, 1536:2560]

            def ml_keys(h, b):
                nc.tensor.matmul(PS[:, b, :], ukv[:, h * P:(h + 1) * P], CKN, start=True, stop=True)\
                    .then_inc(S("ml_k"), 1)

            def ml_queries(blocks):
                for nb in blocks:
                    for k in range(2):
                        i = nc.tensor.matmul(PS[:, nb // 2, (nb % 2) * T:(nb % 2 + 1) * T],
                                             uq[:, k, nb * P:(nb + 1) * P], CQN[:, k, :], start=k == 0, stop=k == 1)
                i.then_inc(S("ml_q"), 1)

            ml_keys(0, 4)
            ml_keys(1, 5)
            pe.wait_ge(S("fc_done"), 1)
            ft = c2("ft").rearrange("p (c t n) -> p c t n", c=2, t=2)
            for a in range(2):
                for t in range(2):
                    for c in range(2):
                        i = nc.tensor.matmul(PS[:, 2, a * T:(a + 1) * T],
                                             FC[:, t * 512 + a * T + c * P:t * 512 + a * T + (c + 1) * P],
                                             ft[:, c, t, :], start=t + c == 0, stop=t + c == 2)
            i.then_inc(S("fn_mm"), 1)
            ml_queries(range(4))
            pe.wait_ge(S("fm_done"), 1)
            ml_queries(range(4, 6))
            wf = c2("wfou").rearrange("p (k n) -> p k n", k=2)
            for a in range(2):
                for k in range(2):
                    i = nc.tensor.matmul(PS[:, 3, a * T:(a + 1) * T], wf[:, k, a * P:(a + 1) * P], FM[:, k, :],
                                         start=k == 0, stop=k == 1)
            i.then_inc(S("fn_mm"), 1)
            pe.wait_ge(S("ml_q_read"), 1)
            ml_keys(2, 0)
            ml_keys(3, 1)
            pe.wait_ge(S("ml_q_read"), 2)
            pe.wait_ge(S("fn_read"), 3)
            i = nc.tensor.matmul(PS[:, 3, :], c2("rot"), QP, start=True, stop=True)
            i.then_inc(S("ml_rot"), 1)
            nc.tensor.matmul(PS[:, 6, 0:T], c2("rot"), CKV[:, 1, 0:T], start=True, stop=True).then_inc(S("ml_rot"), 1)
            for t in range(4):
                b = (2, 4, 5, 0)[t]
                if t == 1:
                    pe.wait_ge(S("ml_k_read"), 2)
                if t == 3:
                    pe.wait_ge(S("ml_k_read"), 4)
                nc.tensor.matmul(PS[:, b, :], CKN[:, t * P:(t + 1) * P], ukv[:, 512:1024], start=True, stop=True)\
                    .then_inc(S("ml_v"), 1)

            def ml_scores(i):
                h, t = i // 2, i % 2
                b = (1, 3)[i % 2]
                if i == 0:
                    pe.wait_ge(S("rope_done"), 2)
                    pe.wait_ge(S("ml_k_read"), 4)
                if i >= 2:
                    pe.wait_ge(S("ml_exp"), i - 1)
                nc.tensor.matmul(PS[:, b, :], QN[:, h, t * P:(t + 1) * P], KN[:, h, :], start=True, stop=False)
                r = half(h % 2)
                nc.tensor.matmul(PS[:, b, :], QR[r, (h // 2) * T + t * P:(h // 2) * T + (t + 1) * P], KPE[r, :],
                                 start=False, stop=True).then_inc(S("ml_s"), 1)

            def ml_transpose(i):
                pe.wait_ge(S("ml_p"), i + 1)
                if i == 0:
                    pe.wait_ge(S("ml_v_read"), 4)
                if i >= 2:
                    pe.wait_ge(S("ml_pt"), i - 1)
                for c in range(4):
                    j = nc.tensor.transpose(PS[:, 4 + i % 2, c * P:(c + 1) * P], PR[:, i % 2, c * P:(c + 1) * P], ident)
                j.then_inc(S("ml_tr"), 1)

            def ml_values(i):
                h, t = i // 2, i % 2
                pe.wait_ge(S("ml_pt"), i + 1)
                for c in range(4):
                    j = nc.tensor.matmul(PS[:, 0 if h < 2 else 2, (h % 2) * T + t * P:(h % 2) * T + (t + 1) * P],
                                         VT[:, c, h * P:(h + 1) * P], PT[:, i % 2, c * P:(c + 1) * P],
                                         start=c == 0, stop=c == 3)
                j.then_inc(S("ml_o"), 1)

            def hg_transpose(d, t):
                if t == 0:
                    pe.wait_ge(S("hg_kw"), d + 1)
                if d == 0 and t == 0:
                    pe.wait_ge(S("rope"), 3)
                if d == 0 and t == 1:
                    pe.wait_ge(S("modv"), 4)
                if d == 1 or t >= 2:
                    pe.wait_ge(S("hg_kwt"), 4 * d + t - 1)
                for h in range(4):
                    i = nc.tensor.transpose(PS[:, 6 + t % 2, h * P:(h + 1) * P],
                                            ZF[:, d, t // 2, h, (t % 2) * P:(t % 2 + 1) * P], ident)
                i.then_inc(S("hg_tr"), 1)

            ml_scores(0)
            ml_scores(1)
            for i in range(9):
                if i < 8:
                    ml_transpose(i)
                if i:
                    ml_values(i - 1)
                if 2 <= i <= 5:
                    hg_transpose(0, i - 2)
                if i < 6:
                    ml_scores(i + 2)

            for d in range(2):
                if d == 1:
                    for t in range(4):
                        hg_transpose(1, t)
                pe.wait_ge(S("hg_kwt"), 4 * d + 4)
                if d == 0:
                    pe.wait_ge(S("ml_o_read"), 2)
                    pe.wait_ge(S("ml_exp"), 8)
                else:
                    pe.wait_ge(S("hg_copied"), 6)
                for s in (1, 0):
                    for n in range(4):
                        t, r = n // 2, half(n % 2)
                        for h in range(4):
                            i = nc.tensor.matmul(PS[:, 2 * (1 - s) + n % 2, t * T + h * 64:t * T + h * 64 + 64],
                                                 KWT[r, 2 * s + t, h, :], HI[r, 2 * s + t, h * 64:h * 64 + 64],
                                                 start=True, stop=True)
                    i.then_inc(S("hg_upd"), 1)
                for l in range(7):
                    if l < 6:
                        pe.wait_ge(S("hg_pair"), 6 * d + l + 1)
                        q, k = (QM0, KM0) if l % 2 == 0 else (QMd(d), KMd(d))
                    elif d == 0:
                        continue
                    else:
                        pe.wait_ge(S("hg_ks"), 2)
                        q, k = QQ, KS
                    bb = (4, 5) if l % 2 == 0 else (0, 1)
                    if l == 0 and d == 0:
                        pe.wait_ge(S("ml_pt"), 8)
                    if l == 1:
                        pe.wait_ge(S("hg_state"), 7 * d + 7)
                    if l >= 2:
                        pe.wait_ge(S("hg_copied"), 6 * d + l - 1)
                    for m in range(8):
                        h, t = m // 2, m % 2
                        i = nc.tensor.matmul(PS[:, bb[m // 4], (m % 4) * P:(m % 4 + 1) * P],
                                             k[:, h * T + t * P:h * T + (t + 1) * P],
                                             q[:, h * T + t * P:h * T + (t + 1) * P], start=True, stop=True)
                    i.then_inc(S("hg_sc"), 1)
            pe.wait_ge(S("hg_copied"), 13)
            pe.wait_ge(S("hg_qf"), 2)
            for h in range(4):
                for t in range(2):
                    out = PS[half(h % 2), 2, (h // 2) * T + t * P:(h // 2) * T + (t + 1) * P]
                    nc.tensor.matmul(out, HI[:, t, h * 64:h * 64 + 64], SC[:, (2 * h + t) * P:(2 * h + t + 1) * P],
                                     start=True, stop=False, skip_group_check=True)
                    for d in range(2):
                        for n in (2 * t, 2 * t + 1):
                            i = nc.tensor.matmul(PS[half(h % 2), 2, (h // 2) * T + n * 64:(h // 2) * T + n * 64 + 64],
                                                 SX[:, d, n, h * 64:h * 64 + 64],
                                                 QF[:, d, h * T + n * 64:h * T + n * 64 + 64],
                                                 start=False, stop=d == 1, skip_group_check=True)
            i.then_inc(S("hg_o"), 1)
            pe.wait_ge(S("hg_osq"), 1)
            nc.tensor.matmul(PS[:, 3, :], blk, SQO, start=True, stop=True).then_inc(S("hg_oss"), 1)
            out_units_pe(pe, U_OUT2, "o2", 4)
            norm_pe(pe, 6)
            ffn_pe(pe, 2, "ffn2")
            norm_pe(pe, 7)

        @block.scalar
        def _(act):
            act.dma_start(par, A["par"]).then_inc(S("par_loaded"), 16)
            act.dma_start(cst, A["cst"]).then_inc(S("cst_loaded"), 16)
            act.dma_start(csb, A["csb"]).then_inc(S("csb_loaded"), 16)
            act.wait_ge(S("memset_done"), 3)
            act.wait_ge(S("par_loaded"), 16)
            norm_act(act, 0, before=LN_EXP, meanwhile=lambda: (hi(act, 0), hi(act, 1)))
            hi(act, 2)
            act.wait_ge(S("glr_mm"), 1)
            nc.scalar.activation(GLR, PS[0:16, 3, 0:T], ACT.Copy).then_inc(S("glr_done"), 1)

            def copy_proj(u):
                act.wait_ge(S("unit_done"), u + 1)
                nc.scalar.activation(PROJ[:, u, :], PS[:, 4, :], ACT.Copy).then_inc(S("proj0_copied"), 1)

            def qk_square(j):
                act.wait_ge(S(f"proj{j % 2}_copied"), (8 + j) // 2 + 1)
                nc.scalar.activation(SQF[:, j * 512:(j + 1) * 512], PROJ[:, 8 + j, :], ACT.Square)\
                    .then_inc(S("qk_sq"), 1)

            def qk_rstd(j):
                r = RSF[:, j * 512:(j + 1) * 512]
                act.wait_ge(S("qk_ss"), j + 1)
                nc.scalar.activation(r, PS[:, QK_BANK[j], :], ACT.Ln, scale=1.0 / 64, bias=prm_eps)\
                    .then_inc(S("qk_rs"), 1)
                act.wait_ge(S("qk_rs"), 2 * j + 1)
                nc.scalar.activation(r, r, ACT.Exp, scale=-0.5).then_inc(S("qk_rs"), 1)

            for u in range(6):
                if u % 2 == 0:
                    copy_proj(u)
                hi(act, u + 3)
            act.wait_ge(S("gate_mm"), 1)
            for a in range(2):
                i = nc.scalar.activation(GE[:, a * T:(a + 1) * T], PS[:, 3, a * T:(a + 1) * T], ACT.Abs,
                                         bias=prm("bgate", a))
            i.then_inc(S("gate_read"), 1)
            act.wait_ge(S("gate_read"), 1)
            nc.scalar.activation(GE, GE, ACT.Exp, scale=-1.0).then_inc(S("gate_act"), 1)
            act.wait_ge(S("gate_act"), 1)
            nc.scalar.activation(GE, GE, ACT.Ln, bias=1.0).then_inc(S("gate_act"), 1)
            act.wait_ge(S("gla_diff"), 1)
            nc.scalar.activation(KEND, KEND, ACT.Exp, scale=1.0 / 16).then_inc(S("gla_exp"), 1)
            nc.scalar.activation(DEC, CUM.rearrange("p (m c) -> p m c", c=CHUNK)[:, :, CHUNK - 1], ACT.Exp,
                                 scale=1.0 / 16).then_inc(S("gla_exp"), 1)
            copy_proj(6)
            hi(act, 9)
            act.wait_ge(S("proj1_copied"), 3)
            table(SILU)
            nc.scalar.activation(RSG, PROJ[:, 4:6, :].rearrange("p a n -> p (a n)"), ACT.Silu).then_inc(S("r_silu"), 1)
            table(LN_EXP)
            hi(act, 10)
            act.wait_ge(S("ktok_mm"), 1)
            nc.scalar.activation(KTOK, PS[:, 2, :], ACT.Copy).then_inc(S("ktok_done"), 1)
            copy_proj(8)
            qk_square(0)
            hi(act, 11)
            hi(act, 12)
            qk_square(1)
            act.wait_ge(S("og_mm"), 1)
            nc.scalar.activation(OG, banks(2, 4), ACT.Copy, scale=CHUNK ** -0.5).then_inc(S("og_done"), 1)
            act.wait_ge(S("og_done"), 1)
            nc.scalar.activation(OR, OG, ACT.Square).then_inc(S("og_sq"), 1)
            qk_rstd(0)
            copy_proj(10)
            qk_square(2)
            hi(act, 13)
            act.wait_ge(S("og_ss"), 1)
            nc.scalar.activation(OR, banks(0, 2), ACT.Ln, scale=1.0 / P, bias=prm_eps).then_inc(S("og_rs"), 1)
            act.wait_ge(S("og_rs"), 1)
            nc.scalar.activation(OR, OR, ACT.Exp, scale=-0.5).then_inc(S("og_rs"), 1)
            qk_rstd(1)
            qk_square(3)
            qk_rstd(2)
            qk_rstd(3)

            def sb_log(g):
                l = SBL[:, g % 2]
                act.wait_ge(S("sb_z"), g + 1)
                if g >= 2:
                    act.wait_ge(S("sb_keep"), g - 1)
                nc.scalar.activation(l, PS[:, 2 * (g % 2):2 * (g % 2) + 2, 0:384], ACT.Abs, scale=0.125)\
                    .then_inc(S("sb_a"), 1)
                act.wait_ge(S("sb_a"), 3 * g + 1)
                nc.scalar.activation(l, l, ACT.Exp, scale=-1.0).then_inc(S("sb_a"), 1)
                act.wait_ge(S("sb_a"), 3 * g + 2)
                nc.scalar.activation(l, l, ACT.Ln, bias=1.0).then_inc(S("sb_a"), 1)

            def sb_weights(g):
                act.wait_ge(S("sb_lz2"), g + 1)
                nc.scalar.activation(SBZ[:, g % 3], SBZ[:, g % 3], ACT.Exp).then_inc(S("sb_exp"), 1)

            def sb_store(g):
                act.wait_ge(S("sb_o"), g + 1)
                nc.scalar.activation(MIX[:, 4 + g, :], PS[:, 6, 0:T], ACT.Copy).then_inc(S("sb_o_read"), 1)

            def mix1_ready(act, j):
                if j < 2:
                    act.wait_ge(S("gla_out"), 1)
                    act.wait_ge(S("unit_done"), N_IN1)
                else:
                    act.wait_ge(S("sb_o_read"), 2 * (j - 1))

            act.wait_ge(S("qkn_done"), 4)
            act.wait_ge(S("gla_out"), 1)
            for g in range(6):
                if g < 4:
                    sb_log(g)
                if g == 0:
                    hi(act, 14)
                if 1 <= g < 5:
                    sb_weights(g - 1)
                if g == 3:
                    mix_split_act(act, 0, mix1_ready, (0, 1))
                if g >= 2:
                    sb_store(g - 2)

            mix_split_act(act, 0, mix1_ready, (2, 3))
            for j in range(1, N_OUT):
                hi(act, U_OUT1 + j + 2)
            folded_act(act, 1, after=SILU)
            nc.scalar.activation(CSL.rearrange("p k c -> p (k c)"), prm("c2", 0, 16), ACT.Silu).then_inc(S("csl_done"), 1)
            ffn_act(act, 0, True)
            folded_act(act, 2, before=LN_EXP, after=SIGMOID)
            def diagonal(n):
                k, j = PE_TILES[n // TAPS], n % TAPS
                if n >= RING:
                    act.wait_ge(S("diag_used"), n - RING + 1)
                nc.scalar.activation(DG[:, n % RING, :], ident, ACT.Copy, scale=prm("wdw", k * TAPS + j))\
                    .then_inc(S("diag_built"), 1)

            for j in range(N_PW1):
                hi(act, U_PW1 + j + 2)
                act.wait_ge(S("pw_done"), j + 1)
                if j >= 2:
                    act.wait_ge(S("cu_done"), j - 1)
                nc.scalar.activation(SIG[:, j % 2, :], PWR[:, j % 2, T:2 * T], ACT.Sigmoid,
                                     bias=prm("bpw1", 8 + j)).then_inc(S("sig_done"), 1)
                for n in range(RING // N_PW1 * j, RING // N_PW1 * (j + 1)):
                    diagonal(n)
            nth = 0
            for n in range(RING, RING + len(PE_TILES) * TAPS):
                if n < len(PE_TILES) * TAPS:
                    diagonal(n)
                if n - RING + 1 == TAPS * (nth + 1):
                    act.wait_ge(S("diag_used"), TAPS * (nth + 1))
                    k = PE_TILES[nth]
                    nc.scalar.activation(HN[:, k, :], PS[:, nth, 0:T], ACT.Identity, bias=prm("bdw", k))\
                        .then_inc(S("cv_pe_done"), 1)
                    nth += 1
            table(LN_EXP)
            act.wait_ge(S("ln_sum"), 1)
            nc.scalar.activation(MU, PS[:, 6, 0:T], ACT.Copy, scale=1.0 / D).then_inc(S("ln_mu"), 1)
            for j in range(2):
                act.wait_ge(S("ln_d"), j + 1)
                nc.scalar.activation(SQ[:, 4 * j:4 * j + 4, :], HN[:, 4 * j:4 * j + 4, :], ACT.Square)\
                    .then_inc(S("ln_sq"), 1)
            act.wait_ge(S("ln_ss"), 1)
            nc.scalar.activation(RS, PS[:, 6, T:2 * T], ACT.Ln, scale=1.0 / D, bias=prm_eps).then_inc(S("ln_a"), 1)
            act.wait_ge(S("ln_a"), 1)
            nc.scalar.activation(RS, RS, ACT.Exp, scale=-0.5).then_inc(S("ln_a"), 1)
            table(SILU)
            for j in range(4):
                for k in (2 * j, 2 * j + 1):
                    act.wait_ge(S("ln_n"), k + 1)
                    i = nc.scalar.activation(SQ[:, k, :], HN[:, k, :], ACT.Silu, bias=prm("lnb", k))
                i.then_inc(S("ln_silu"), 1)
                act.wait_ge(S("ln_silu"), j + 1)
                nc.scalar.activation(a_hi[:, 2 * j:2 * j + 2, 1, :], SQ[:, 2 * j:2 * j + 2, :], ACT.Copy)\
                    .then_inc(S("cv_hi"), 1)
            for j in range(N_OUT):
                hi(act, U_PW2 + j + 2)
            folded_act(act, 3, before=LN_EXP)
            ffn_act(act, 1, True, lambda: norm_act(act, 4, lambda k: MOD[:, k, 1:2], after=SILU))
            act.wait_ge(S("mod_done"), 136)
            act.dma_start(mlw, A["mlw"]).then_inc(S("mlw_loaded"), 16)
            norm_act(act, 5, lambda k: MOD[:, k, 0:1], before=LN_EXP)
            act.wait_ge(S("mod_sum"), 2)
            act.dma_start(cst2, A["cst2"]).then_inc(S("cst2_loaded"), 16)
            def hg_log_step(d, n):
                z, g = fl(ZF[:, d]), fl(GG[d])
                if n:
                    act.wait_ge(S("hg_a"), 3 * d + n)
                if n == 0:
                    i = nc.scalar.activation(g, z, ACT.Abs)
                elif n == 1:
                    i = nc.scalar.activation(g, g, ACT.Exp, scale=-1.0)
                else:
                    i = nc.scalar.activation(g, g, ACT.Ln, bias=1.0)
                i.then_inc(S("hg_a"), 1)

            def hg_complement(d):
                act.wait_ge(S("hg_gz"), d + 1)
                nc.scalar.activation(fl(KK[d]), fl(KK[d]), ACT.Exp).then_inc(S("hg_k"), 1)

            def hg_key_decay(d):
                act.wait_ge(S("hg_w"), d + 1)
                nc.scalar.activation(fl(ZF[:, d]), fl(ZF[:, 0]) if d == 0 else fl(GG[1]), ACT.Exp)\
                    .then_inc(S("hg_we"), 1)

            def hg_chunk_decay(d):
                nc.scalar.activation(AD[:, d, :],
                                     CC[d].rearrange("p s h (n c) -> p (s h n) c", c=CHUNK)[:, :, CHUNK - 1], ACT.Exp)\
                    .then_inc(S("hg_ad"), 1)
                if d == 1:
                    act.wait_ge(S("hg_qx"), 1)
                nc.scalar.activation(QF[:, d, :], fl(CC[0])[:, 0:1024] if d == 0 else QF[:, 1, :], ACT.Exp)\
                    .then_inc(S("hg_qxe"), 1)

            def hg_keys(d, t):
                act.wait_ge(S("hg_tr"), 4 * d + t + 1)
                if d == 1 and t == 0:
                    act.wait_ge(S("hg_upd"), 2)
                nc.scalar.activation(KWT[:, t].rearrange("p h k -> p (h k)"), PS[:, 6 + t % 2, :], ACT.Copy)\
                    .then_inc(S("hg_kwt"), 1)

            def hg_pair_decay(d, l):
                act.wait_ge(S("hg_e"), 6 * d + l + 1)
                nc.scalar.activation(EX[:, l % 2, :], EX[:, l % 2, :], ACT.Exp).then_inc(S("hg_ee"), 1)

            def hg_log(d):
                hg_log_step(d, 0)
                hg_log_step(d, 1)
                hg_log_step(d, 2)

            for j in range(N_IN2):
                u = U_IN2 + j
                if j + 2 < N_IN2:
                    hi(act, u + 2)
                if j == 6:
                    hg_log(0)
                if j == 8:
                    act.wait_ge(S("in2_read"), 7)
                    nc.scalar.activation(SQ2[:, 0:512], XO[:, 0:2, :].rearrange("p k t -> p (k t)"), ACT.Square)
                    nc.scalar.activation(SQ2[:, 512:1024], CKV[:, 0, :], ACT.Square).then_inc(S("ml_sq"), 1)
                    hg_complement(0)
                if j == 10:
                    table(SILU)
                    act.wait_ge(S("in2_read"), 10)
                    nc.scalar.activation(QQ, XO[:, 2:6, :].rearrange("p k t -> p (k t)"), ACT.Silu)\
                        .then_inc(S("hg_q"), 1)
                    nc.scalar.activation(XO[:, 6:8, :], XO[:, 6:8, :], ACT.Silu).then_inc(S("hg_z"), 1)
                    table(LN_EXP)
                act.wait_ge(S("unit_done"), u + 1)
                if j == 0:
                    nc.scalar.activation(CKV, PS[:, 0:2, :], ACT.Copy).then_inc(S("in2_read"), 1)
                elif j < 5:
                    b, dd, hh = 2 * (j % 2), (j - 1) // 2, 2 * ((j - 1) % 2)
                    for e in range(2):
                        i = nc.scalar.activation(ZF[:, dd, :, hh + e, :],
                                                 PS[:, b + e, :].rearrange("p (s t) -> p s t", s=2), ACT.Copy)
                    i.then_inc(S("in2_read"), 1)
                elif j == 5:
                    nc.scalar.activation(HI.rearrange("p a n -> p (a n)"), banks(2, 4), ACT.Copy)\
                        .then_inc(S("in2_read"), 1)
                else:
                    b = 4 + (j - 6) % 2
                    nc.scalar.activation(XO[:, 2 * (j - 6):2 * (j - 6) + 2, :].rearrange("p a n -> p (a n)"),
                                         PS[:, b, :], ACT.Copy).then_inc(S("in2_read"), 1)
            act.wait_ge(S("ml_ss"), 1)
            nc.scalar.activation(RS2[:, 0:T], PS[:, 6, 0:T], ACT.Ln, scale=1.0 / 256, bias=prm_eps)
            nc.scalar.activation(RS2[:, 512:1024], PS[:, 7, :], ACT.Ln, scale=1.0 / 128, bias=prm_eps)\
                .then_inc(S("ml_ln"), 1)
            act.wait_ge(S("ml_ln"), 1)
            nc.scalar.activation(RS2[:, 0:T], RS2[:, 0:T], ACT.Exp, scale=-0.5)
            nc.scalar.activation(RS2[:, 512:1024], RS2[:, 512:1024], ACT.Exp, scale=-0.5).then_inc(S("ml_rs"), 1)
            act.wait_ge(S("fn_mm"), 1)
            nc.scalar.activation(FC, banks(0, 2), ACT.Copy).then_inc(S("fc_done"), 1)
            def ml_keys(h):
                act.wait_ge(S("ml_k"), h + 1)
                nc.scalar.activation(KN[:, h, :], PS[:, (4, 5, 0, 1)[h], :], ACT.Copy).then_inc(S("ml_k_read"), 1)

            ml_keys(0)
            ml_keys(1)
            act.wait_ge(S("fn_mm"), 2)
            nc.scalar.activation(FM.rearrange("p k t -> p (k t)"), PS[:, 2, :], ACT.Copy, scale=1.0 / 128)\
                .then_inc(S("fm_done"), 1)
            act.wait_ge(S("ml_q"), 1)
            nc.scalar.activation(QN.rearrange("p h t -> p (h t)"), banks(0, 2), ACT.Copy).then_inc(S("ml_q_read"), 1)
            act.wait_ge(S("ml_q"), 2)
            nc.scalar.activation(QP, PS[:, 2, :], ACT.Copy).then_inc(S("ml_q_read"), 1)
            act.wait_ge(S("fn_mm"), 3)
            nc.scalar.activation(MIX[:, 6:8, :].rearrange("p k t -> p (k t)"), PS[:, 3, :], ACT.Copy)\
                .then_inc(S("fn_read"), 3)
            ml_keys(2)
            ml_keys(3)
            hg_key_decay(0)
            for t in range(4):
                act.wait_ge(S("ml_v"), t + 1)
                nc.scalar.activation(VT[:, t, :], PS[:, (2, 4, 5, 0)[t], :], ACT.Copy).then_inc(S("ml_v_read"), 1)
            hg_chunk_decay(0)
            scale = 192 ** -0.5

            def ml_exp(i):
                act.wait_ge(S("ml_max"), i + 1)
                nc.scalar.activation(MXS[:, i:i + 1], MXS[:, i:i + 1], ACT.Copy, scale=-scale).then_inc(S("ml_neg"), 1)
                act.wait_ge(S("ml_neg"), i + 1)
                if i >= 2:
                    act.wait_ge(S("ml_tr"), i - 1)
                nc.scalar.activation(PR[:, i % 2, :], PS[:, (1, 3)[i % 2], :], ACT.Exp, scale=scale,
                                     bias=MXS[:, i:i + 1], accum_out=MXS[:, 8 + i:9 + i]).then_inc(S("ml_exp"), 1)

            ml_exp(0)
            ml_exp(1)
            for i in range(8):
                act.wait_ge(S("ml_tr"), i + 1)
                if i >= 2:
                    act.wait_ge(S("ml_o"), i - 1)
                nc.scalar.activation(PT[:, i % 2, :], PS[:, 4 + i % 2, :], ACT.Copy).then_inc(S("ml_pt"), 1)
                if i < 6:
                    ml_exp(i + 2)
                if 3 <= i <= 6:
                    hg_keys(0, i - 3)
                if 2 <= i <= 4:
                    hg_log_step(1, i - 2)
            for j in range(2):
                act.wait_ge(S("ml_o"), 8)
                nc.scalar.activation(OA[:, j * 512:(j + 1) * 512], PS[:, (0, 2)[j], :], ACT.Copy)\
                    .then_inc(S("ml_o_read"), 1)

            for l in range(6):
                hg_pair_decay(0, l)
                if l == 2:
                    hg_complement(1)
                if l == 4:
                    hg_key_decay(1)
                if l == 5:
                    hg_chunk_decay(1)
                if l == 3:
                    hi(act, U_OUT2)
            for t in range(4):
                hg_keys(1, t)
            def mix2_ready(act, j):
                if j == 0:
                    act.wait_ge(S("ml_o_read"), 2)
                    act.wait_ge(S("hg_e"), 6)
                if j == 2:
                    act.wait_ge(S("hg_out"), 1)
            for l in range(6):
                hg_pair_decay(1, l)
                if l == 3:
                    mix_split_act(act, 1, mix2_ready, (0, 1))
            act.wait_ge(S("hg_o"), 1)
            nc.scalar.activation(OH, PS[:, 2, :], ACT.Copy).then_inc(S("hg_r"), 1)
            act.wait_ge(S("hg_r"), 1)
            nc.scalar.activation(SQO, OH, ACT.Square).then_inc(S("hg_osq"), 1)
            act.wait_ge(S("hg_oss"), 1)
            nc.scalar.activation(RSO, PS[:, 3, :], ACT.Ln, scale=1.0 / 64, bias=prm_eps).then_inc(S("hg_r"), 1)
            act.wait_ge(S("hg_r"), 2)
            nc.scalar.activation(RSO, RSO, ACT.Exp, scale=-0.5).then_inc(S("hg_r"), 1)

            mix_split_act(act, 1, mix2_ready, (2, 3))
            for j in range(-1, N_OUT):
                hi(act, U_OUT2 + j + 2)
            norm_act(act, 6, lambda k: MOD[:, 24 + k, 0:1], after=SILU)
            ffn_act(act, 2)
            norm_act(act, 7, split=False, before=LN_EXP)

        @block.vector
        def _(dve):
            dve.memset(zero, 0.0).then_inc(S("memset_done"), 1)
            dve.memset(epsc, EPS).then_inc(S("memset_done"), 1)
            dve.memset(RESET, 1.0).then_inc(S("memset_done"), 1)
            dve.wait_ge(S("memset_done"), 3)
            dve.memset(RESET.rearrange("p (m c) -> p m c", c=CHUNK)[:, :, 0:1], 0.0).then_inc(S("memset_done"), 1)
            dve.wait_ge(S("par_loaded"), 16)
            lo(dve, 0)
            lo(dve, 1)
            norm_dve(dve, 0, lambda k: prm("mixn0", k))
            lo(dve, 2)

            def copy_proj(u):
                dve.wait_ge(S("unit_done"), u + 1)
                dve.tensor_copy(PROJ[:, u, :], PS[:, 5, :]).then_inc(S("proj1_copied"), 1)

            def qk_norm(j):
                dve.wait_ge(S("qk_rs"), 2 * j + 2)
                dve.scalar_tensor_tensor(QKN[:, j * 512:(j + 1) * 512], PROJ[:, 8 + j, :],
                                         prm(("sbk", "sbq")[j // 2]), RSF[:, j * 512:(j + 1) * 512], ALU.mult,
                                         ALU.mult).then_inc(S("qkn_done"), 1)

            for u in range(6):
                if u % 2 == 1:
                    copy_proj(u)
                lo(dve, u + 3)
            dve.wait_ge(S("gate_mm"), 1)
            dve.wait_ge(S("gate_read"), 1)
            for a in range(2):
                dve.tensor_scalar(LA[:, a * T:(a + 1) * T], PS[:, 3, a * T:(a + 1) * T], prm("bgate", a), 0.0,
                                  ALU.add, ALU.min).then_inc(S("gate_read"), 1)
            dve.wait_ge(S("gate_read"), 3)
            dve.wait_ge(S("gate_act"), 2)
            dve.tensor_tensor(LA, LA, GE, ALU.subtract).then_inc(S("gla_dve"), 1)
            dve.wait_ge(S("gla_dve"), 1)
            dve.wait_ge(S("memset_done"), 4)
            dve.tensor_tensor_scan(CUM, RESET, LA, 0.0, ALU.mult, ALU.add).then_inc(S("gla_dve"), 1)
            dve.wait_ge(S("gla_dve"), 2)
            cum = CUM.rearrange("p (m c) -> p m c", c=CHUNK)
            dve.tensor_tensor(KEND.rearrange("p (m c) -> p m c", c=CHUNK),
                              cum[:, :, CHUNK - 1:CHUNK].to_broadcast([P, 8, CHUNK]), cum, ALU.subtract)\
                .then_inc(S("gla_diff"), 1)
            dve.wait_ge(S("gla_exp"), 1)
            dve.wait_ge(S("proj0_copied"), 2)
            dve.tensor_tensor(KEND, KEND, PROJ[:, 2, :], ALU.mult).then_inc(S("kend_done"), 1)
            lo(dve, 9)
            copy_proj(7)
            lo(dve, 10)
            dve.wait_ge(S("upd_mm"), 1)
            dve.wait_ge(S("gla_exp"), 2)
            for n in range(4):
                for a in range(2):
                    U = PS[:, n % 2, ((n // 2) * 2 + a) * P:((n // 2) * 2 + a + 1) * P]
                    if n == 0:
                        dve.tensor_copy(ST[:, 0, a, :], U).then_inc(S("state_done"), 1)
                    else:
                        dve.wait_ge(S("state_done"), 2 * n + a - 1)
                        dve.scalar_tensor_tensor(ST[:, n, a, :], ST[:, n - 1, a, :], DEC[:, a * 4 + n:a * 4 + n + 1], U,
                                                 ALU.mult, ALU.add).then_inc(S("state_done"), 1)
            lo(dve, 11)
            copy_proj(9)
            lo(dve, 12)
            qk_norm(0)
            lo(dve, 13)
            dve.wait_ge(S("og_rs"), 2)
            dve.scalar_tensor_tensor(OG, OG, prm("glan"), OR, ALU.mult, ALU.mult).then_inc(S("og_norm"), 1)
            qk_norm(1)
            copy_proj(11)
            dve.wait_ge(S("og_norm"), 1)
            dve.wait_ge(S("r_silu"), 1)
            og = OG.rearrange("p (e a t) -> p a e t", e=2, a=2)
            mx = MIX[:, 0:4, :].rearrange("p (a e) t -> p a e t", a=2)
            rg = RSG.rearrange("p (a e t) -> p a e t", a=2, e=2)
            for a in range(2):
                i = dve.tensor_tensor(mx[:, a], og[:, a], rg[:, a], ALU.mult)
            i.then_inc(S("gla_out"), 1)
            qk_norm(2)
            qk_norm(3)

            dve.wait_ge(S("csb_loaded"), 16)
            mb = sbmask.unsqueeze(1).to_broadcast([P, 2, 384])

            def sb_keep(g):
                z = PS[:, 2 * (g % 2):2 * (g % 2) + 2, 0:384]
                dve.wait_ge(S("sb_a"), 3 * g + 3)
                if g:
                    dve.wait_ge(S("sb_v"), 3 * g)
                    dve.wait_ge(S("sb_keep"), g)
                dve.tensor_scalar(SBK, z, 0.125, 0.0, ALU.mult, ALU.max).then_inc(S("sb_v"), 1)
                dve.wait_ge(S("sb_v"), 3 * g + 1)
                dve.scalar_tensor_tensor(SBK, SBK, -1.0, SBL[:, g % 2], ALU.mult, ALU.subtract).then_inc(S("sb_v"), 1)
                dve.wait_ge(S("sb_v"), 3 * g + 2)
                if g >= 2:
                    dve.wait_ge(S("sb_between"), g - 1)
                dve.tensor_tensor(SBM[:, g % 2], SBK, mb, ALU.mult).then_inc(S("sb_keep"), 1)
                if g == 3:
                    dve.wait_ge(S("sb_o"), 1)
                dve.scalar_tensor_tensor(SBZ[:, g % 3], z, 0.125, SBK, ALU.mult, ALU.add).then_inc(S("sb_v"), 1)

            def sb_add(g):
                dve.wait_ge(S("sb_v"), 3 * g + 3)
                dve.wait_ge(S("sb_between"), g + 1)
                dve.tensor_tensor(SBZ[:, g % 3], SBZ[:, g % 3], PS[:, 4:6, 0:384], ALU.add).then_inc(S("sb_lz2"), 1)

            def sb_mask(g):
                w = SBZ[:, g % 3].rearrange("p e (b n) -> p e b n", b=3)[:, :, 0:3:2, :]
                m = sbmask.rearrange("p (b n) -> p b n", b=3)[:, 0:3:2, :].unsqueeze(1).to_broadcast([P, 2, 2, P])
                dve.wait_ge(S("sb_exp"), g + 1)
                dve.tensor_tensor(w, w, m, ALU.mult).then_inc(S("sb_w"), 1)

            for g in range(6):
                if g < 4:
                    sb_keep(g)
                if g >= 2:
                    sb_mask(g - 2)
                if 1 <= g < 5:
                    sb_add(g - 1)
                if g == 4:
                    mix_split_dve(dve, 0, (0, 1))
            lo(dve, 14)
            mix_split_dve(dve, 0, (2, 3))

            def residual_units(u0, add, norm=None):
                for j in range(N_OUT):
                    if not (u0 == U_OUT1 and j == 0):
                        if u0 == U_PW2 and j == 0:
                            dve.wait_ge(S("lo_done"), u0 + 2)
                        lo(dve, u0 + j + 2)
                    dve.wait_ge(S("unit_done"), u0 + j + 1)
                    add(j)
                    if norm and j:
                        folded_lo(dve, norm, j - 1)
                if norm:
                    folded_lo(dve, norm, 3)

            def plain(j):
                ks = slice(2 * j, 2 * j + 2)
                dve.tensor_tensor(X[:, ks, :], X[:, ks, :], PS[:, 4 + j % 2, :].rearrange("p (k t) -> p k t", k=2),
                                  ALU.add).then_inc(S("x_updated"), 1)

            residual_units(U_OUT1, plain, 1)
            ffn_dve(dve, 0, folded=True, behind=2)
            dve.memset(CU[:, :, 0:TAPS - 1], 0.0).then_inc(S("cu_zero"), 1)
            dve.wait_ge(S("cu_zero"), 1)

            def scaled(k):
                dve.wait_ge(S("unit_done"), U_PW1 + k + 1)
                if k == 0:
                    dve.wait_ge(S("norm_rs"), 3)
                if k >= 2:
                    dve.wait_ge(S("cu_done"), k - 1)
                dve.tensor_tensor(PWR[:, k % 2, :].rearrange("p (a t) -> p a t", a=2),
                                  PS[:, 4 + k % 2, :].rearrange("p (a t) -> p a t", a=2),
                                  RS.unsqueeze(1).to_broadcast([P, 2, T]), ALU.mult).then_inc(S("pw_done"), 1)

            def gate(k):
                if k + 1 < KT:
                    scaled(k + 1)
                dve.wait_ge(S("sig_done"), k + 1)
                dve.scalar_tensor_tensor(CU[:, k, TAPS - 1:TAPS - 1 + T], PWR[:, k % 2, 0:T], prm("bpw1", k),
                                         SIG[:, k % 2, :], ALU.add, ALU.mult).then_inc(S("cu_done"), 1)

            scaled(0)
            n, gated_ = 0, 0
            for group in ((0, 1), (2, 3, 4)):
                while gated_ <= group[-1]:
                    gate(gated_)
                    gated_ += 1
                dve.wait_ge(S("cu_done"), group[-1] + 1)
                for j in range(TAPS):
                    for k in group:
                        u, w = CU[:, k, j:j + T], prm("wdw", k * TAPS + j)
                        if j == 0:
                            dve.tensor_scalar(HN[:, k, :], u, w, prm("bdw", k), ALU.mult, ALU.add)\
                                .then_inc(S("tap_done"), 1)
                        else:
                            dve.wait_ge(S("tap_done"), n - len(group) + 1)
                            i = dve.scalar_tensor_tensor(HN[:, k, :], u, w, HN[:, k, :], ALU.mult, ALU.add)
                            i.then_inc(S("tap_done"), 1)
                        n += 1
                        if n % TAP_GAP == 0 and gated_ < KT:
                            gate(gated_)
                            gated_ += 1
            dve.wait_ge(S("tap_done"), (KT - len(PE_TILES)) * TAPS)
            dve.wait_ge(S("ln_mu"), 1)
            for j in range(2):
                ks = slice(4 * j, 4 * j + 4)
                dve.tensor_tensor(HN[:, ks, :], HN[:, ks, :], MU.unsqueeze(1).to_broadcast([P, 4, T]), ALU.subtract)\
                    .then_inc(S("ln_d"), 1)
            dve.wait_ge(S("ln_a"), 2)
            for k in range(KT):
                dve.scalar_tensor_tensor(HN[:, k, :], HN[:, k, :], prm("lng", k), RS, ALU.mult, ALU.mult)\
                    .then_inc(S("ln_n"), 1)
            for j in range(4):
                ks = slice(2 * j, 2 * j + 2)
                dve.wait_ge(S("cv_hi"), j + 1)
                dve.tensor_tensor(a_lo[:, ks, 1, :], SQ[:, ks, :], a_hi[:, ks, 1, :].bitcast(F32), ALU.subtract)\
                    .then_inc(S("act_lo"), 1)

            def biased(j):
                for e in range(2):
                    k = 2 * j + e
                    i = dve.scalar_tensor_tensor(X[:, k, :], PS[:, 4 + j % 2, e * T:(e + 1) * T], prm("bpw2", k),
                                                 X[:, k, :], ALU.add, ALU.add)
                i.then_inc(S("x_updated"), 1)

            residual_units(U_PW2, biased, 3)
            modp = PS[:, 7, 0:96].rearrange("p (n c) -> p n c", c=2)
            dve.wait_ge(S("mod_sum"), 1)
            dve.tensor_tensor(MOD[:, 0:16, :], modp[:, 0:16, :], prm("bmod", 0, 16).unsqueeze(2).to_broadcast([P, 16, 2]),
                              ALU.add).then_inc(S("modv"), 1)
            dve.wait_ge(S("modv"), 1)
            for n, c in enumerate((0, 1)):
                dve.scalar_tensor_tensor(GSC[:, n, :], MOD[:, 8:16, c], 1.0, prm("n1g", 0, 8), ALU.add, ALU.mult)\
                    .then_inc(S("modv"), 1)
            dve.wait_ge(S("modv"), 3)
            ffn_dve(dve, 1, folded=True,
                    between=lambda: norm_dve(dve, 4, lambda k: GSC[:, 1, k:k + 1], lambda k: MOD[:, k, 1:2]))
            norm_dve(dve, 5, lambda k: GSC[:, 0, k:k + 1], lambda k: MOD[:, k, 0:1])
            dve.wait_ge(S("mod_sum"), 2)
            dve.tensor_tensor(MOD[:, 16:48, 0], modp[:, 16:48, 0], prm("bmod", 16, 32), ALU.add).then_inc(S("modv"), 1)
            dve.wait_ge(S("modv"), 4)
            dve.scalar_tensor_tensor(GSC[:, 2, :], MOD[:, 32:40, 0], 1.0, prm("n2g", 0, 8), ALU.add, ALU.mult)\
                .then_inc(S("modv"), 1)
            ch = lambda ap: ap.rearrange("p s h (n c) -> p (s h n) c", c=CHUNK)

            def hg_gates(d):
                z, g = ZF[:, d], GG[d]
                dve.wait_ge(S("hg_a"), 3 * d + 3)
                dve.scalar_tensor_tensor(fl(g), fl(z), 0.0, fl(g), ALU.min, ALU.subtract).then_inc(S("hg_v"), 1)

            def hg_log_complement(d):
                dve.wait_ge(S("hg_v"), 2 * d + 1)
                dve.tensor_tensor(fl(KK[d]), fl(GG[d]), fl(ZF[:, d]), ALU.subtract).then_inc(S("hg_gz"), 1)

            for j in range(N_IN2 - 2):
                lo(dve, U_IN2 + j + 2)
                if j == 6:
                    hg_gates(0)
                    hg_log_complement(0)

            def hg_sums(d):
                for s in range(2):
                    for h in range(4):
                        i = dve.tensor_tensor_scan(CC[d][:, s, h, :], RST64, GG[d][:, s, h, :], 0.0, ALU.mult, ALU.add)
                i.then_inc(S("hg_v"), 1)

            def hg_exponents(d):
                dve.wait_ge(S("hg_v"), 2 * d + 2)
                dve.wait_ge(S("hg_gz"), d + 1)
                if d == 0:
                    end = ch(CC[0])[:, :, CHUNK - 1:CHUNK].to_broadcast([P, 32, CHUNK])
                    dve.tensor_tensor(ch(ZF[:, 0]), end, ch(CC[0]), ALU.subtract).then_inc(S("hg_w"), 1)
                else:
                    endx = ch(CC[1])[:, 0:16, CHUNK - 1:CHUNK].to_broadcast([P, 16, CHUNK])
                    dve.tensor_tensor(fl(GG[1]), fl(CC[1]), fl(GG[1]), ALU.subtract).then_inc(S("hg_w"), 1)
                    dve.wait_ge(S("hg_w"), 2)
                    dve.tensor_tensor(QF[:, 1, :].rearrange("p (m c) -> p m c", c=CHUNK), endx, ch(GG[1])[:, 0:16, :],
                                      ALU.subtract).then_inc(S("hg_qx"), 1)

            def hg_gated_keys(d):
                dve.wait_ge(S("hg_k"), d + 1)
                dve.wait_ge(S("hg_we"), d + 1)
                dve.tensor_tensor(fl(ZF[:, d]), fl(ZF[:, d]), fl(KK[d]), ALU.mult).then_inc(S("hg_kw"), 1)

            def hg_key_sum(d):
                k = fl(KK[d])[:, 0:1024]
                if d == 0:
                    dve.tensor_copy(KS, k).then_inc(S("hg_ks"), 1)
                else:
                    dve.tensor_tensor(KS, KS, k, ALU.add).then_inc(S("hg_ks"), 1)

            def hg_gated_queries(d):
                dve.wait_ge(S("hg_qxe"), d + 1)
                dve.wait_ge(S("hg_q"), 1)
                dve.tensor_tensor(QF[:, d, :], QF[:, d, :], QQ, ALU.mult).then_inc(S("hg_qf"), 1)

            dve.wait_ge(S("modv"), 5)
            dve.wait_ge(S("cst2_loaded"), 16)
            dve.wait_ge(S("ml_rs"), 1)
            for k in range(2):
                i = dve.scalar_tensor_tensor(CQN[:, k, :], XO[:, k, :], prm("qng", k), RS2[:, 0:T], ALU.mult, ALU.mult)
            i.then_inc(S("ml_n"), 1)
            dve.scalar_tensor_tensor(CKN, CKV[:, 0, :], prm("kvg"), RS2[:, 512:1024], ALU.mult, ALU.mult)\
                .then_inc(S("ml_n"), 1)
            dve.wait_ge(S("norm_hn"), 24)
            dve.memset(RST64, 1.0).then_inc(S("hg_reset"), 1)
            dve.wait_ge(S("hg_reset"), 1)
            dve.memset(RST64.rearrange("p (m c) -> p m c", c=CHUNK)[:, :, 0:1], 0.0).then_inc(S("hg_reset"), 1)
            dve.wait_ge(S("hg_reset"), 2)
            dve.wait_ge(S("unit_done"), U_OUT2)
            hg_sums(0)
            hg_exponents(0)
            cos2 = c2("cos").unsqueeze(1).to_broadcast([P, 2, T])
            sin2 = c2("sin").unsqueeze(1).to_broadcast([P, 2, T])
            v2 = lambda ap: ap.rearrange("p (a t) -> p a t", a=2)
            dve.wait_ge(S("ml_q_read"), 2)
            dve.wait_ge(S("ml_rot"), 2)
            dve.tensor_tensor(v2(QR), v2(PS[:, 3, :]), sin2, ALU.mult).then_inc(S("rope"), 1)
            dve.tensor_tensor(v2(QP), v2(QP), cos2, ALU.mult).then_inc(S("rope"), 1)
            dve.tensor_tensor(KPE[:, 0:T], PS[:, 6, 0:T], c2("sin"), ALU.mult).then_inc(S("rope"), 1)
            dve.tensor_tensor(KPE[:, T:2 * T], CKV[:, 1, 0:T], c2("cos"), ALU.mult).then_inc(S("rope"), 1)
            dve.wait_ge(S("rope"), 4)
            dve.tensor_tensor(QR, QR, QP, ALU.add).then_inc(S("rope_done"), 1)
            dve.tensor_tensor(KPE[:, 0:T], KPE[:, 0:T], KPE[:, T:2 * T], ALU.add).then_inc(S("rope"), 1)
            dve.wait_ge(S("rope"), 5)
            dve.tensor_copy(KPE[:, T:2 * T], CKV[:, 1, T:2 * T]).then_inc(S("rope_done"), 1)

            def ml_max(i):
                dve.wait_ge(S("ml_s"), i + 1)
                dve.reduce_max(MXS[:, i:i + 1], PS[:, (1, 3)[i % 2], :], AX.X).then_inc(S("ml_max"), 1)

            for i in range(8):
                ml_max(i)
                dve.wait_ge(S("ml_exp"), i + 1)
                dve.reciprocal(MXS[:, 16 + i:17 + i], MXS[:, 8 + i:9 + i]).then_inc(S("ml_rc"), 1)
                dve.wait_ge(S("ml_rc"), i + 1)
                dve.tensor_scalar(PR[:, i % 2, :], PR[:, i % 2, :], MXS[:, 16 + i:17 + i], None, ALU.mult)\
                    .then_inc(S("ml_p"), 1)

                if i == 1:
                    hg_gated_keys(0)
                if i == 6:
                    hg_key_sum(0)
                if i == 7:
                    hg_gates(1)
            hg_gated_queries(0)

            def hg_states(d):
                order = [(1, n) for n in range(4)] + [(0, n) for n in range(4)]
                if d == 1:
                    order = [(s, 3 - n) for s, n in order]
                dve.wait_ge(S("hg_ad"), d + 1)
                v = lambda ap: ap.rearrange("p (h v) -> p h v", h=4)
                prev = None
                ad = AD[:, d, :].rearrange("p (s h n) -> p s h n", s=2, h=4)
                for c, (s, n) in enumerate(order[:7]):
                    upd = PS[:, 2 * (1 - s) + n % 2, (n // 2) * T:(n // 2) * T + T]
                    s2, n2 = order[c + 1]
                    dst = SX[:, d, n2, :] if s2 == 0 else (STT if c % 2 == 0 else STU)
                    dve.wait_ge(S("hg_upd"), 2 * d + (2 - s))
                    if prev is None:
                        dve.tensor_copy(dst, upd).then_inc(S("hg_state"), 1)
                    else:
                        dve.wait_ge(S("hg_state"), 7 * d + c)
                        dve.tensor_tensor(v(dst), v(prev), ad[:, s, :, n:n + 1].to_broadcast([P, 4, 64]), ALU.mult)\
                            .then_inc(S("hg_dec"), 1)
                        dve.wait_ge(S("hg_dec"), 6 * d + c)
                        dve.tensor_tensor(dst, dst, upd, ALU.add).then_inc(S("hg_state"), 1)
                    prev = dst

            def pair_products(d, l):
                m = LEVELS[l]
                w = lambda ap: ap.rearrange("p (a b m) -> p a b m", b=2, m=m)
                q, k = (QM0, KM0) if l % 2 == 0 else (QMd(d), KMd(d))
                qs, ks_ = (1, 0) if d == 0 else (0, 1)
                e = w(EX[:, l % 2, :])
                dve.wait_ge(S("hg_ee"), 6 * d + l + 1)
                if l == 1:
                    dve.wait_ge(S("hg_tr"), 4 * d + 4)
                if l >= 2:
                    dve.wait_ge(S("hg_sc"), 6 * d + l - 1)
                dve.tensor_tensor(w(q)[:, :, qs, :], w(QQ)[:, :, qs, :], e[:, :, qs, :], ALU.mult)
                dve.tensor_tensor(w(k)[:, :, ks_, :], w(fl(KK[d])[:, 0:1024])[:, :, ks_, :], e[:, :, ks_, :], ALU.mult)\
                    .then_inc(S("hg_pair"), 1)

            def pair_copy(d, l):
                bb = 4 if l % 2 == 0 else 0
                dve.wait_ge(S("hg_sc"), 6 * d + l + 1)
                mi = 6 * d + l
                mask = c2("lmask")[:, mi * P:(mi + 1) * P].bitcast(I32).unsqueeze(1).to_broadcast([P, 8, P])
                if mi:
                    dve.wait_ge(S("hg_copied"), mi)
                dve.copy_predicated(SC.rearrange("p (m t) -> p m t", m=8), mask,
                                    banks(bb, bb + 2).rearrange("p (m t) -> p m t", m=8))\
                    .then_inc(S("hg_copied"), 1)

            dve.wait_ge(S("hg_zero"), 3)
            dve.wait_ge(S("ml_o"), 8)
            pair_products(0, 0)
            pair_products(0, 1)
            hg_states(0)
            pair_copy(0, 0)
            pair_products(0, 2)
            hg_log_complement(1)
            pair_copy(0, 1)
            pair_products(0, 3)
            hg_sums(1)
            pair_copy(0, 2)
            pair_products(0, 4)
            hg_exponents(1)
            pair_copy(0, 3)
            pair_products(0, 5)
            pair_copy(0, 4)
            pair_copy(0, 5)
            hg_gated_keys(1)
            lo(dve, U_OUT2)
            hg_key_sum(1)
            hg_gated_queries(1)
            pair_products(1, 0)
            pair_products(1, 1)
            hg_states(1)
            for l in range(7):
                if l == 5:
                    mix_split_dve(dve, 1, (0, 1))
                pair_copy(1, l)
                if l < 4:
                    pair_products(1, l + 2)
            dve.wait_ge(S("hg_r"), 3)
            for a in range(2):
                dve.scalar_tensor_tensor(OH[:, a * T:(a + 1) * T], OH[:, a * T:(a + 1) * T], prm("hgg", a),
                                         RSO[:, a * T:(a + 1) * T], ALU.mult, ALU.mult).then_inc(S("hg_f"), 1)
            dve.wait_ge(S("hg_f"), 2)
            dve.wait_ge(S("hg_z"), 1)
            dve.tensor_tensor(MIX[:, 4:6, :].rearrange("p k t -> p (k t)"), OH,
                              XO[:, 6:8, :].rearrange("p k t -> p (k t)"), ALU.mult).then_inc(S("hg_out"), 1)
            mix_split_dve(dve, 1, (2, 3))
            lo(dve, U_OUT2 + 1)

            def gated(j):
                for e in range(2):
                    k = 2 * j + e
                    i = dve.scalar_tensor_tensor(X[:, k, :], PS[:, 4 + j % 2, e * T:(e + 1) * T], MOD[:, 16 + k, 0:1],
                                                 X[:, k, :], ALU.mult, ALU.add)
                i.then_inc(S("x_updated"), 1)

            residual_units(U_OUT2, gated)
            norm_dve(dve, 6, lambda k: GSC[:, 2, k:k + 1], lambda k: MOD[:, 24 + k, 0:1])
            ffn_dve(dve, 2, lambda k: MOD[:, 40 + k, 0:1])
            norm_dve(dve, 7, lambda k: prm("fing", k), split=False)

        @block.gpsimd
        def _(pool):
            pool.wait_ge(S("act_lo"), 8)
            for n in range(4):
                pool.memset(MODACC[:, n, :], 0.0).then_inc(S("mod_done"), 1)
            for m in range(2):
                pool.dma_start(modraw[:, m, :], A["wmod"][m]).then_inc(S(f"mod_loaded{m}"), 16)
            pool.dma_start(CTX.rearrange("p k t -> p (k t)"), A["ctxT"]).then_inc(S("ctx_loaded"), 16)

            def mod_product(out, k, c, n):
                pool.wait_ge(S("mod_done"), n)
                pool.tensor_tensor(out, modraw[:, k % 2, :], CSL[:, k, c:c + 1].to_broadcast([P, 1024]), ALU.mult)\
                    .then_inc(S("mod_done"), 1)

            def mod_add(acc, x, n):
                pool.wait_ge(S("mod_done"), n)
                pool.tensor_tensor(acc, acc, x, ALU.add).then_inc(S("mod_done"), 1)

            def mod_next(g, k, n):
                pool.wait_ge(S("mod_done"), n)
                pool.dma_start(modraw[:, k % 2, :], A["wmod"][g * KT + k + 2])\
                    .then_inc(S(f"mod_loaded{k % 2}"), 16)

            acc_of = lambda g: MODACC[:, g, :]
            pool.wait_ge(S("csl_done"), 1)
            for g in range(2):
                for k in range(KT):
                    n = g * 32 + (4 + 4 * k)
                    pool.wait_ge(S(f"mod_loaded{k % 2}"), g * 64 + 16 * (k // 2 + 1))
                    mod_product(MODTMP, k, 0, n)
                    mod_add(acc_of(g), MODTMP, n + 1)
                    mod_product(modraw[:, k % 2, :], k, 1, n + 2)
                    mod_add(acc_of(g + 2), modraw[:, k % 2, :], n + 3)
                    mod_next(g, k, n + 4)
            for u in range(U_PW1 + 2, U_PW1 + N_PW1 + 2):
                pool.wait_ge(S("hi_done"), u + 1)
                pool.wait_ge(S("lo_done"), u)
                pool.tensor_tensor(w_lo[:, u % SLOTS, :], raw[:, u % RAW_SLOTS, :], w_hi[:, u % SLOTS, :].bitcast(F32),
                                   ALU.subtract).then_inc(S("lo_done"), 1)
            pool.wait_ge(S("mod_sum"), 1)
            for n in range(4):
                pool.memset(MODACC[:, n, :], 0.0).then_inc(S("mod_done"), 1)

            def mod_group(g, last=False):
                for k in range(KT):
                    n = g * 16 + (72 + 2 * k)
                    pool.wait_ge(S(f"mod_loaded{k % 2}"), g * 64 + (128 + 16 * (k // 2 + 1)))
                    mod_product(modraw[:, k % 2, :], k, 0, n)
                    mod_add(acc_of(g), modraw[:, k % 2, :], n + 1)
                    if not (last and k >= KT - 2):
                        mod_next(g + 2, k, n + 2)

            for g in range(4):
                mod_group(g, g == 3)

            def pair_exponents(d, l):
                m = LEVELS[l]
                w = lambda ap: ap.rearrange("p (a b m) -> p a b m", b=2, m=m)
                x = w(fl(CC[0] if d == 0 else GG[1])[:, 0:1024])
                ref = (x[:, :, 0, m - 1:m] if d == 0 else x[:, :, 1, 0:1]).to_broadcast([P, 512 // m, m])
                e = w(EX[:, l % 2, :])
                if l == 0:
                    pool.wait_ge(*((S("hg_v"), 2) if d == 0 else (S("hg_w"), 2)))
                if d or l >= 2:
                    pool.wait_ge(S("hg_pair"), 6 * d + l - 1)
                pool.tensor_tensor(e[:, :, 1, :], x[:, :, 1, :], ref, ALU.subtract)
                pool.tensor_tensor(e[:, :, 0, :], ref, x[:, :, 0, :], ALU.subtract).then_inc(S("hg_e"), 1)

            pool.wait_ge(S("ml_v"), 4)
            pair_exponents(0, 0)
            pair_exponents(0, 1)
            pool.wait_ge(S("ml_o"), 8)
            for buf in (QM0, KM0, SC):
                pool.memset(buf, 0.0).then_inc(S("hg_zero"), 1)
            for l in range(2, 6):
                pair_exponents(0, l)
            for l in range(6):
                pair_exponents(1, l)


def _tiles(a):
    k, n = a.shape
    return a.reshape(k // P, P, n // P, P).transpose(2, 0, 1, 3)


def _feature_units(blocks):
    b = np.stack(blocks)
    return b.reshape(-1, BLK, P, P).transpose(0, 2, 1, 3).reshape(-1, P, UNIT)


def _token_units(w):
    return w.reshape(KT, P, -1, 256).transpose(2, 1, 0, 3).reshape(-1, P, UNIT)


def _ffn_units(wg, wu, wd):
    g, u = _tiles(wg), _tiles(wu)
    d = wd.reshape(FT, P, KT, P).transpose(0, 2, 1, 3)
    gu = [_feature_units([g[f], u[f]])[0] for f in range(FT)]
    dn = [np.concatenate([d[2 * j], d[2 * j + 1]]).transpose(1, 0, 2).reshape(P, UNIT) for j in range(FT // 2)]
    out = [gu[0], gu[1]]
    for j in range(1, FT // 2):
        out += [gu[2 * j], gu[2 * j + 1], dn[j - 1]]
    return np.stack(out + [dn[-1]])


def _cols(a):
    return a.reshape(-1, P).T


def _constants():
    ones = np.ones((P, P), np.float32)
    blk = np.kron(np.eye(2, dtype=np.float32), np.ones((64, 64), np.float32))
    cst = np.concatenate([ones, blk, np.eye(P, dtype=np.float32)], 1)
    i = np.arange(P)
    after = (i[:, None] > i[None, :]).astype(np.float32)
    before = (i[:, None] < i[None, :]).astype(np.float32)
    csb = np.concatenate([after, before, ones, before], 1)
    masks = []
    for d in range(2):
        for m in LEVELS:
            pair, side = i // (2 * m), (i // m) % 2
            q, k = (1, 0) if d == 0 else (0, 1)
            masks.append((pair[:, None] == pair[None, :]) & (side[:, None] == k) & (side[None, :] == q))
    masks.append(np.eye(P, dtype=bool))
    lmask = np.concatenate([m.astype(np.float32) for m in masks], 1)
    f = np.arange(64)
    w = 2 * np.pi * np.outer(f, f) / 64
    e2 = np.eye(2)
    fd = np.concatenate([np.kron(e2, np.cos(w)), np.kron(e2, -np.sin(w))], 1).astype(np.float32)
    t = np.arange(T)
    w = 2 * np.pi * (np.outer(t, t) % T) / T
    ft = np.stack([np.cos(w), np.sin(w)]).reshape(2, 2, P, T).transpose(2, 0, 1, 3).reshape(P, -1).astype(np.float32)
    row, col = (np.arange(T) // 64).astype(np.float32), (np.arange(T) % 64).astype(np.float32)
    inv = (10000.0 ** (-np.arange(0, 32, 2, dtype=np.float32) / 32)).astype(np.float32)
    ar, ac = row[:, None] * inv, col[:, None] * inv
    ang = np.concatenate([ar, ar, ac, ac], 1).T
    cos, sin = (np.concatenate([g(ang)] * 2, 0).astype(np.float32) for g in (np.cos, np.sin))
    rot = np.zeros((64, 64), np.float32)
    for o in range(16):
        rot[16 + o, o] = -1.0
        rot[o, 16 + o] = 1.0
        rot[48 + o, 32 + o] = -1.0
        rot[32 + o, 48 + o] = 1.0
    rot = np.kron(np.eye(2, dtype=np.float32), rot)
    return cst, csb, np.concatenate([lmask, fd, ft, cos, sin, rot], 1)


def _lay_out(v):
    f = {k: np.asarray(a) for k, a in v.items()}
    w_in = f["hy_w_in"][0]
    c = np.cumsum([0, 256, 256, 512, 512, 16, 512, 512, 512])
    gq, gk, gv, gr, glr, sq, sk, sv = (w_in[:, a:b] for a, b in zip(c[:-1], c[1:]))
    fm = lambda *ws: _feature_units([t for w in ws for t in _tiles(w)])
    units = [_token_units(gv), fm(gk, gq, gr), _token_units(sv), fm(sk, sq), fm(f["hy_w_out"][0]),
             _ffn_units(f["ffn_w_gate"][0], f["ffn_w_up"][0], f["ffn_w_down"][0])]
    pw = _tiles(f["cv_w_pw1"][0])
    units += [_feature_units([t for j in range(8) for t in (pw[j], pw[8 + j])]), fm(f["cv_w_pw2"][0]),
              _ffn_units(f["ffn_w_gate"][1], f["ffn_w_up"][1], f["ffn_w_down"][1])]
    w2 = f["w_in_2"][0]
    c = np.cumsum([0, 256, 128, 64, 512, 512, 512, 256, 256, 256])
    cq, ckv, kr, hq, hff, hfb, hi, hg, fn = (w2[:, a:b] for a, b in zip(c[:-1], c[1:]))
    units += [fm(np.concatenate([ckv, kr, kr], 1), hff, hfb), _token_units(hi), fm(cq, hq, hg, fn),
              fm(f["w_out_2"][0])]
    gu = f["w_gate_up_2"][0]
    units += [_ffn_units(gu[:, :FT * P], gu[:, FT * P:], f["w_down_2"][0])]
    wstream = np.concatenate(units)
    cst, csb, cs2 = _constants()
    wf = f["w_fourier_2"][0].reshape(2, P, 256).transpose(1, 0, 2).reshape(P, 512)
    uq = f["w_uq_2"][0].reshape(256, 4, 192)
    uq = np.concatenate([uq[:, :, :128].reshape(256, 512), uq[:, :, 128:].reshape(256, 256)], 1)
    uq = uq.reshape(2, P, 768).transpose(1, 0, 2).reshape(P, 1536)
    ukv = f["w_ukv_2"][0].reshape(P, 4, 256)
    ukv = np.concatenate([ukv[:, :, :128].reshape(P, 512), ukv[:, :, 128:].reshape(P, 512)], 1)
    g2 = np.zeros((P, 256), np.float32)
    g2[:16] = f["hy_w_gate2"][0]
    cc = np.stack([_cols(f["c_2"][0]), _cols(f["c_ctx_2"])], 2).reshape(P, 16)
    par = np.concatenate([
        _cols(f["mix_norm"][0]), _cols(f["mix_norm"][1]), _cols(f["ffn_norm"][0]), _cols(f["ffn_norm"][1]),
        _cols(f["hy_gla_norm"][0]), _cols(np.tile(f["hy_sb_q_norm"][0], 2)), _cols(np.tile(f["hy_sb_k_norm"][0], 2)),
        _cols(f["hy_b_gate"][0]), _cols(f["cv_b_pw1"][0]), _cols(f["cv_b_dw"][0]), _cols(f["cv_ln_g"][0]),
        _cols(f["cv_ln_b"][0]), _cols(f["cv_b_pw2"][0]),
        f["cv_w_dw"][0].reshape(TAPS, KT, P).transpose(2, 1, 0).reshape(P, -1), cc, _cols(f["b_mod_2"][0]),
        _cols(f["norm1_g_2"][0]), _cols(f["norm2_g_2"][0]), _cols(f["q_norm_g_2"][0]), _cols(f["kv_norm_g_2"][0]),
        _cols(f["hg_norm_g_2"][0]), _cols(f["final_norm_g_2"]),
        glr.reshape(KT, P, 16).transpose(1, 0, 2).reshape(P, -1), g2], 1)
    act = lambda a: a[0].T.reshape(KT, P, T).transpose(1, 0, 2).reshape(P, KT * T)
    arrays = {
        "wstream": wstream, "wmod": f["w_mod_2"][0].reshape(KT, P, 6, 1024).transpose(2, 0, 1, 3).reshape(MODB, P, 1024),
        "xT": act(f["x"]), "ctxT": act(f["ctx_2"]), "par": par, "cst": cst, "csb": csb,
        "cst2": np.concatenate([cs2, wf], 1), "mlw": np.concatenate([uq, ukv], 1),
    }
    return {k: np.ascontiguousarray(a, dtype=np.float32) for k, a in arrays.items()}


def kernel(**inputs):
    import concourse.bacc as bacc
    from concourse import mybir
    from concourse.bass_utils import run_bass_kernel_spmd

    nc = bacc.Bacc("TRN2", target_bir_lowering=False, num_devices=1)
    arrays = _lay_out(inputs)
    A = {k: nc.dram_tensor(k, a.shape, mybir.dt.float32, kind="ExternalInput").ap() for k, a in arrays.items()}
    A["out"] = nc.dram_tensor("out", (P, KT * T), mybir.dt.float32, kind="ExternalOutput").ap()
    program(nc, A)
    r = run_bass_kernel_spmd(nc, [arrays], core_ids=[0])
    y = r.results[0]["out"]
    return np.ascontiguousarray(y.reshape(P, KT, T).transpose(1, 0, 2).reshape(D, T).T.reshape(1, T, D))
```
